# Optimizing a Trainium2 kernel written in Bass

```python
import jax, jax.numpy as jnp
from jax import lax
import numpy as np

D_MODEL = 1024
BATCH = 1
SEQ = 128
DEPTH = 2
DEC_BATCH = 1
DEC_SEQ = 512
PAST_LEN = 128

GRID_W = 64
ROPE_THETA = 10000.0
Q_BLOCK = 128
EPS = 1e-6

D_MIX = D_MODEL
GROUP_W = D_MIX // 4

RW_HEADS = 4
RW_HEAD_DIM = GROUP_W // RW_HEADS
RW_DECAY_RANK = 64
RW_ICLR_RANK = 32
RW_GATE_RANK = 128
RW_DECAY_SCALE = 0.6065306597

MLA_HEADS = 4
MLA_NOPE_DIM = 64
MLA_ROPE_DIM = 32
MLA_V_DIM = GROUP_W // MLA_HEADS
MLA_QK_DIM = MLA_NOPE_DIM + MLA_ROPE_DIM
MLA_Q_RANK = 192
MLA_KV_RANK = 128

GQA_HEADS = 4
GQA_KV_HEADS = 2
GQA_HEAD_DIM = GROUP_W // GQA_HEADS
GQA_GROUP = GQA_HEADS // GQA_KV_HEADS

CONV_W = 3

IN_SPLITS = (
    GROUP_W, GROUP_W, GROUP_W,
    RW_DECAY_RANK, RW_DECAY_RANK,
    RW_ICLR_RANK, RW_ICLR_RANK,
    RW_GATE_RANK,
    MLA_Q_RANK, MLA_KV_RANK, MLA_ROPE_DIM,
    GQA_HEADS * GQA_HEAD_DIM, GQA_KV_HEADS * GQA_HEAD_DIM, GQA_KV_HEADS * GQA_HEAD_DIM,
    GROUP_W, GROUP_W, GROUP_W,
)
D_IN = 2720

PEER_HEADS = 8
PEER_N_KEYS = 128
PEER_N_EXPERTS = PEER_N_KEYS * PEER_N_KEYS
PEER_QDIM = 256
PEER_HALF = PEER_QDIM // 2
PEER_TOPK = 16
PEER_BLOCK = 128

kernel_name = 'hybrid_diffusion_trunk_step'

def rms_norm(x, g):
    xf = x.astype(jnp.float32)
    y = xf * lax.rsqrt(jnp.mean(xf * xf, axis=-1, keepdims=True) + EPS)
    return (y * g.astype(jnp.float32)).astype(x.dtype)

def heads(x, n):
    return x.reshape(x.shape[:-1] + (n, x.shape[-1] // n))

def split_cols(x, sizes):
    offs = np.cumsum(np.array(sizes))[:-1]
    return jnp.split(x, [int(o) for o in offs], axis=-1)

def grid_rope(n_tok, rot_dim):
    rows = n_tok // GRID_W
    row = jnp.repeat(jnp.arange(rows, dtype=jnp.float32), GRID_W)
    col = jnp.tile(jnp.arange(GRID_W, dtype=jnp.float32), rows)
    n_freq = rot_dim // 4
    freqs = ROPE_THETA ** (-jnp.arange(n_freq, dtype=jnp.float32) / n_freq)
    ang = jnp.concatenate([row[:, None] * freqs, col[:, None] * freqs], axis=-1)
    return jnp.cos(ang), jnp.sin(ang)

def apply_rope(x, cs):
    cos, sin = cs[0][None, :, None, :], cs[1][None, :, None, :]
    half = x.shape[-1] // 2
    x1 = x[..., :half].astype(jnp.float32)
    x2 = x[..., half:].astype(jnp.float32)
    return jnp.concatenate([x1 * cos - x2 * sin, x1 * sin + x2 * cos], axis=-1).astype(x.dtype)

def attention(q, k, v, scale):
    b, tq, hk, g, d = q.shape
    nb = tq // Q_BLOCK
    q_blocks = jnp.moveaxis(q.reshape(b, nb, Q_BLOCK, hk, g, d), 1, 0)

    def one_block(qb):
        s = jnp.einsum('bqhgd,bkhd->bhgqk', qb, k).astype(jnp.float32) * scale
        pr = jax.nn.softmax(s, axis=-1).astype(v.dtype)
        return jnp.einsum('bhgqk,bkhe->bqhge', pr, v)

    o = lax.map(one_block, q_blocks)
    return jnp.moveaxis(o, 0, 1).reshape(b, tq, hk, g, v.shape[-1])

def wkv7_scan(r, w, k, v, kk, a, s0, reverse):
    def step(s, inp):
        r_t, w_t, k_t, v_t, kk_t, a_t = inp
        s_kk = jnp.einsum('bhvk,bhk->bhv', s, kk_t)
        s = (s * w_t[:, :, None, :] - s_kk[..., None] * (kk_t * a_t)[:, :, None, :]
             + v_t[..., :, None] * k_t[..., None, :])
        return s, jnp.einsum('bhvk,bhk->bhv', s, r_t)

    xs = tuple(jnp.moveaxis(t, 1, 0) for t in (r, w, k, v, kk, a))
    s_fin, ys = lax.scan(step, s0, xs, reverse=reverse)
    return jnp.moveaxis(ys, 0, 1), s_fin

def rwkv7_mixer(r, k, v, wd, ad, gd, p, s_ctx):
    b, t, _ = r.shape
    kkf = heads(k * p['rw_kk'], RW_HEADS).astype(jnp.float32)
    kk = (kkf * lax.rsqrt(jnp.sum(kkf * kkf, axis=-1, keepdims=True) + EPS)).astype(k.dtype)
    rh, kh, vh = heads(r, RW_HEADS), heads(k, RW_HEADS), heads(v, RW_HEADS)
    ys, finals = [], []
    for d in range(2):
        w = jnp.exp(-RW_DECAY_SCALE * jax.nn.sigmoid(p['rw_w0'][d] + jnp.tanh(wd[d]) @ p['rw_wu'][d]))
        a = jax.nn.sigmoid(p['rw_a0'][d] + ad[d] @ p['rw_au'][d])
        k_d = k * (1 + (a - 1) * p['rw_ka'])
        if s_ctx is None:
            s_init = jnp.zeros((b, RW_HEADS, RW_HEAD_DIM, RW_HEAD_DIM), r.dtype)
        else:
            s_init = s_ctx[:, d].astype(r.dtype)
        y, s_fin = wkv7_scan(rh, heads(w, RW_HEADS), heads(k_d, RW_HEADS), vh, kk,
                             heads(a, RW_HEADS), s_init, reverse=(d == 1))
        ys.append(y)
        finals.append(s_fin)
    y = rms_norm(ys[0] + ys[1], p['rw_gn'].reshape(RW_HEADS, RW_HEAD_DIM))
    bonus = jnp.sum(rh * kh * p['rw_rk'], axis=-1, keepdims=True) * vh
    g = jax.nn.sigmoid(gd) @ p['rw_gu']
    out = (y + bonus).reshape(b, t, GROUP_W) * g
    return out, jnp.stack(finals, axis=1)

def mla_expand(ckv, k_rope, p):
    kv = heads(ckv @ p['mla_wukv'], MLA_HEADS)
    k_nope, v = kv[..., :MLA_NOPE_DIM], kv[..., MLA_NOPE_DIM:]
    k_r = jnp.broadcast_to(k_rope[:, :, None, :], k_nope.shape[:-1] + (MLA_ROPE_DIM,))
    k = rms_norm(jnp.concatenate([k_nope, k_r], axis=-1), p['mla_kn_g'])
    return k, v

def rope_tail(x, cs, d):
    return jnp.concatenate([x[..., :-d], apply_rope(x[..., -d:], cs)], axis=-1)

def mla_mixer(q_c, ckv_raw, k_rope, p, rope, ctx):
    q = heads(rms_norm(q_c, p['mla_qa_g']) @ p['mla_wuq'], MLA_HEADS)
    q = rms_norm(q, p['mla_qn_g'])
    ckv = rms_norm(ckv_raw, p['mla_kva_g'])
    k, v = mla_expand(ckv, k_rope, p)
    if ctx is not None:
        q = rope_tail(q, rope, MLA_ROPE_DIM)
        k = rope_tail(k, rope, MLA_ROPE_DIM)
        k_ctx, v_ctx = mla_expand(ctx[0], ctx[1], p)
        k = jnp.concatenate([k_ctx, k], axis=1)
        v = jnp.concatenate([v_ctx, v], axis=1)
    o = attention(q[:, :, :, None, :], k, v, MLA_QK_DIM ** -0.5)
    return o.reshape(q.shape[:2] + (GROUP_W,)), ckv

def gqa_mixer(q_g, k_g, v_g, p, rope, ctx):
    q = rms_norm(heads(q_g, GQA_HEADS), p['gqa_qn_g'])
    k = rms_norm(heads(k_g, GQA_KV_HEADS), p['gqa_kn_g'])
    v = heads(v_g, GQA_KV_HEADS)
    k_keep, v_keep = k, v
    if ctx is not None:
        q = apply_rope(q, rope)
        k = jnp.concatenate([ctx[0], apply_rope(k, rope)], axis=1)
        v = jnp.concatenate([ctx[1], v], axis=1)
    b, t = q.shape[:2]
    o = attention(q.reshape(b, t, GQA_KV_HEADS, GQA_GROUP, GQA_HEAD_DIM), k, v, GQA_HEAD_DIM ** -0.5)
    return o.reshape(b, t, GROUP_W), k_keep, v_keep

def short_conv_mixer(x_in, b_g, c_g, p):
    u = c_g * x_in
    up = jnp.pad(u, ((0, 0), (1, 1), (0, 0)))
    w = p['conv_w']
    y = up[:, :-2] * w[0] + up[:, 1:-1] * w[1] + up[:, 2:] * w[2] + p['conv_b']
    return b_g * y

def peer_ffn(h, p):
    b, t, d = h.shape
    xb = h.reshape(-1, PEER_BLOCK, d)
    U, V = p['peer_u'], p['peer_v']

    def block(x):
        q = (x @ p['peer_wq']).reshape(PEER_BLOCK, PEER_HEADS, 2, PEER_HALF)
        s1 = jnp.einsum('nhd,hkd->nhk', q[:, :, 0], p['peer_k1']).astype(jnp.float32)
        s2 = jnp.einsum('nhd,hkd->nhk', q[:, :, 1], p['peer_k2']).astype(jnp.float32)
        v1, i1 = lax.top_k(s1, PEER_TOPK)
        v2, i2 = lax.top_k(s2, PEER_TOPK)
        cand = (v1[..., :, None] + v2[..., None, :]).reshape(PEER_BLOCK, PEER_HEADS, PEER_TOPK * PEER_TOPK)
        cand_idx = (i1[..., :, None] * PEER_N_KEYS + i2[..., None, :]).reshape(PEER_BLOCK, PEER_HEADS, PEER_TOPK * PEER_TOPK)
        best, pos = lax.top_k(cand, PEER_TOPK)
        idx = jnp.take_along_axis(cand_idx, pos, axis=-1)
        g = jax.nn.softmax(best, axis=-1).astype(x.dtype)
        act = jax.nn.gelu(jnp.einsum('nhkd,nd->nhk', U[idx], x))
        return jnp.einsum('nhk,nhkd->nd', g * act, V[idx])

    return lax.map(block, xb).reshape(b, t, d)

def trunk_layer(x, mod, p, rope_mla, rope_gqa, ctx):
    shift1, scale1, gate1, shift2, scale2, gate2 = jnp.split(mod, 6, axis=-1)
    h = rms_norm(x, p['norm1_g']) * (1 + scale1) + shift1
    (r, k, v, wd_f, wd_b, ad_f, ad_b, gd, q_c, ckv_raw, k_rope,
     q_g, k_g, v_g, x_in, b_g, c_g) = split_cols(h @ p['w_in'], IN_SPLITS)
    ctx_state = None if ctx is None else ctx[0]
    ctx_mla = None if ctx is None else (ctx[1], ctx[2])
    ctx_gqa = None if ctx is None else (ctx[3], ctx[4])
    o_a, s_a = rwkv7_mixer(r, k, v, (wd_f, wd_b), (ad_f, ad_b), gd, p, ctx_state)
    o_b, ckv = mla_mixer(q_c, ckv_raw, k_rope, p, rope_mla, ctx_mla)
    o_c, k_c, v_c = gqa_mixer(q_g, k_g, v_g, p, rope_gqa, ctx_gqa)
    o_d = short_conv_mixer(x_in, b_g, c_g, p)
    x = x + gate1 * (jnp.concatenate([o_a, o_b, o_c, o_d], axis=-1) @ p['w_out'])
    h2 = rms_norm(x, p['norm2_g']) * (1 + scale2) + shift2
    x = x + gate2 * peer_ffn(h2, p)
    return x, (s_a, ckv, k_rope, k_c, v_c)

def setup_inputs(seed: int = 0) -> dict:
    key = jax.random.key(seed)
    ks = iter(jax.random.split(key, 48))

    def nrm(shape, scale):
        return jax.random.normal(next(ks), shape, jnp.float32) * scale

    def gain(shape, base=1.0):
        return base + nrm(shape, 0.05)

    return {
        'x_prompt': nrm((BATCH, SEQ, D_MODEL), 1.0),
        'x_sample': nrm((DEC_BATCH, DEC_SEQ, D_MODEL), 1.0),
        'state_rwkv': nrm((DEC_BATCH, DEPTH, 2, RW_HEADS, RW_HEAD_DIM, RW_HEAD_DIM), 0.5),
        'cache_mla_ckv': nrm((DEC_BATCH, DEPTH, PAST_LEN, MLA_KV_RANK), 1.0),
        'cache_mla_krope': nrm((DEC_BATCH, DEPTH, PAST_LEN, MLA_ROPE_DIM), 1.0),
        'cache_gqa_k': nrm((DEC_BATCH, DEPTH, PAST_LEN, GQA_KV_HEADS, GQA_HEAD_DIM), 1.0),
        'cache_gqa_v': nrm((DEC_BATCH, DEPTH, PAST_LEN, GQA_KV_HEADS, GQA_HEAD_DIM), 1.0),
        'c': nrm((DEC_BATCH, D_MODEL), 1.0),
        'c_ctx': nrm((D_MODEL,), 1.0),
        'norm1_g': gain((DEPTH, D_MODEL)),
        'norm2_g': gain((DEPTH, D_MODEL)),
        'w_mod': nrm((DEPTH, D_MODEL, 6 * D_MODEL), 0.5 * D_MODEL ** -0.5),
        'b_mod': nrm((DEPTH, 6 * D_MODEL), 0.02),
        'w_in': nrm((DEPTH, D_MODEL, D_IN), D_MODEL ** -0.5),
        'w_out': nrm((DEPTH, D_MIX, D_MODEL), D_MIX ** -0.5),
        'rw_w0': nrm((DEPTH, 2, GROUP_W), 0.5),
        'rw_wu': nrm((DEPTH, 2, RW_DECAY_RANK, GROUP_W), RW_DECAY_RANK ** -0.5),
        'rw_a0': nrm((DEPTH, 2, GROUP_W), 0.5),
        'rw_au': nrm((DEPTH, 2, RW_ICLR_RANK, GROUP_W), 0.5 * RW_ICLR_RANK ** -0.5),
        'rw_gu': nrm((DEPTH, RW_GATE_RANK, GROUP_W), RW_GATE_RANK ** -0.5),
        'rw_kk': gain((DEPTH, GROUP_W), 0.85),
        'rw_ka': gain((DEPTH, GROUP_W)),
        'rw_rk': nrm((DEPTH, RW_HEADS, RW_HEAD_DIM), 0.1),
        'rw_gn': gain((DEPTH, GROUP_W)),
        'mla_qa_g': gain((DEPTH, MLA_Q_RANK)),
        'mla_wuq': nrm((DEPTH, MLA_Q_RANK, MLA_HEADS * MLA_QK_DIM), MLA_Q_RANK ** -0.5),
        'mla_kva_g': gain((DEPTH, MLA_KV_RANK)),
        'mla_wukv': nrm((DEPTH, MLA_KV_RANK, MLA_HEADS * (MLA_NOPE_DIM + MLA_V_DIM)), MLA_KV_RANK ** -0.5),
        'mla_qn_g': gain((DEPTH, MLA_QK_DIM)),
        'mla_kn_g': gain((DEPTH, MLA_QK_DIM)),
        'gqa_qn_g': gain((DEPTH, GQA_HEAD_DIM)),
        'gqa_kn_g': gain((DEPTH, GQA_HEAD_DIM)),
        'conv_w': nrm((DEPTH, CONV_W, GROUP_W), 0.5),
        'conv_b': nrm((DEPTH, GROUP_W), 0.02),
        'peer_wq': nrm((DEPTH, D_MODEL, PEER_HEADS * PEER_QDIM), D_MODEL ** -0.5),
        'peer_k1': nrm((DEPTH, PEER_HEADS, PEER_N_KEYS, PEER_HALF), PEER_HALF ** -0.5),
        'peer_k2': nrm((DEPTH, PEER_HEADS, PEER_N_KEYS, PEER_HALF), PEER_HALF ** -0.5),
        'peer_u': nrm((DEPTH, PEER_N_EXPERTS, D_MODEL), D_MODEL ** -0.5),
        'peer_v': nrm((DEPTH, PEER_N_EXPERTS, D_MODEL), 0.5),
    }

def reference(x_prompt, x_sample, state_rwkv, cache_mla_ckv, cache_mla_krope, cache_gqa_k, cache_gqa_v,
              c, c_ctx, norm1_g, norm2_g, w_mod, b_mod, w_in, w_out,
              rw_w0, rw_wu, rw_a0, rw_au, rw_gu, rw_kk, rw_ka, rw_rk, rw_gn,
              mla_qa_g, mla_wuq, mla_kva_g, mla_wukv, mla_qn_g, mla_kn_g,
              gqa_qn_g, gqa_kn_g, conv_w, conv_b,
              peer_wq, peer_k1, peer_k2, peer_u, peer_v):
    n_lat = x_sample.shape[1]
    rope_mla = grid_rope(n_lat, MLA_ROPE_DIM)
    rope_gqa = grid_rope(n_lat, GQA_HEAD_DIM)
    y_prompt, y_sample = x_prompt, x_sample
    st_a, st_ckv, st_kr, st_k, st_v = [], [], [], [], []
    for l in range(DEPTH):
        p = {
            'norm1_g': norm1_g[l], 'norm2_g': norm2_g[l], 'w_in': w_in[l], 'w_out': w_out[l],
            'rw_w0': rw_w0[l], 'rw_wu': rw_wu[l], 'rw_a0': rw_a0[l], 'rw_au': rw_au[l],
            'rw_gu': rw_gu[l], 'rw_kk': rw_kk[l], 'rw_ka': rw_ka[l], 'rw_rk': rw_rk[l], 'rw_gn': rw_gn[l],
            'mla_qa_g': mla_qa_g[l], 'mla_wuq': mla_wuq[l], 'mla_kva_g': mla_kva_g[l],
            'mla_wukv': mla_wukv[l], 'mla_qn_g': mla_qn_g[l], 'mla_kn_g': mla_kn_g[l],
            'gqa_qn_g': gqa_qn_g[l], 'gqa_kn_g': gqa_kn_g[l], 'conv_w': conv_w[l], 'conv_b': conv_b[l],
            'peer_wq': peer_wq[l], 'peer_k1': peer_k1[l], 'peer_k2': peer_k2[l],
            'peer_u': peer_u[l], 'peer_v': peer_v[l],
        }
        mod_ctx = jax.nn.silu(c_ctx) @ w_mod[l] + b_mod[l]
        y_prompt, (s_a, ckv, kr, k_c, v_c) = trunk_layer(y_prompt, mod_ctx, p, None, None, None)
        st_a.append(s_a)
        st_ckv.append(ckv)
        st_kr.append(kr)
        st_k.append(k_c)
        st_v.append(v_c)
        mod_lat = (jax.nn.silu(c) @ w_mod[l] + b_mod[l])[:, None, :]
        ctx = (state_rwkv[:, l], cache_mla_ckv[:, l], cache_mla_krope[:, l], cache_gqa_k[:, l], cache_gqa_v[:, l])
        y_sample, _ = trunk_layer(y_sample, mod_lat, p, rope_mla, rope_gqa, ctx)
    new_state_rwkv = jnp.stack(st_a, axis=1)
    new_cache_mla_ckv = jnp.stack(st_ckv, axis=1)
    new_cache_mla_krope = jnp.stack(st_kr, axis=1)
    new_cache_gqa_k = jnp.stack(st_k, axis=1)
    new_cache_gqa_v = jnp.stack(st_v, axis=1)
    return (y_prompt, y_sample, new_state_rwkv, new_cache_mla_ckv, new_cache_mla_krope, new_cache_gqa_k, new_cache_gqa_v)


_drawn_inputs = setup_inputs


def setup_inputs(seed=0):
    import zlib

    import numpy as np

    out = dict(_drawn_inputs(seed))
    spreads = {}
    factors = {'state_rwkv': 8.0,
     'cache_mla_ckv': 5.5,
     'cache_mla_krope': 7.781,
     'cache_gqa_k': 6.315,
     'cache_gqa_v': 5.504,
     'rw_kk': 6.095,
     'rw_gn': 5.376,
     'mla_qa_g': 8.0,
     'mla_qn_g': 8.0,
     'mla_kn_g': 8.0,
     'gqa_qn_g': 8.0,
     'conv_b': 6.347}
    for name, (base, spread) in spreads.items():
        noise = np.random.default_rng([zlib.crc32(name.encode()), seed]).standard_normal(out[name].shape)
        drawn = base * np.exp(spread * noise) if base else spread * noise
        out[name] = __import__('jax').numpy.asarray(drawn.astype(out[name].dtype))
    for name, factor in factors.items():
        out[name] = (out[name] * factor).astype(out[name].dtype)
    return out
```

```python
from contextlib import ExitStack, contextmanager

import numpy as np

import concourse.bass as bass
from concourse import mybir

F32 = mybir.dt.float32
U32 = mybir.dt.uint32
ALU = mybir.AluOpType
ACT = mybir.ActivationFunctionType
AX = mybir.AxisListType

P = 128
DEPTH, D, SEQ, DEC, PAST = 2, 1024, 128, 512, 128
TILES = (SEQ + DEC) // P
TOK = TILES * P
KC = D // P
EPS = 1e-6
GW = 256
HD = 64
D_IN = 2720
DECAY = 0.6065306597
Q_RANK, KV_RANK, ROPE, NOPE = 192, 128, 32, 64
QK = NOPE + ROPE
HEADS, NKEY, TOPK, NEXP = 8, 128, 16, 128 * 128
SLOTS = HEADS * TOPK

ZR, ZK, ZV, ZWD, ZAD, ZGD = 0, 256, 512, 768, 896, 960
ZQC, ZCKV, ZKR, ZQG, ZKG, ZVG = 1088, 1280, 1408, 1440, 1696, 1824
ZX, ZB, ZC = 1952, 2208, 2464

ROW_PARTS = [("rw_kk", 256), ("rw_ka", 256), ("wa0", 1024), ("rw_rk", 256), ("rw_gn", 256),
             ("qa_g", 192), ("kva_g", 128), ("qk_g", 768), ("gqa_g", 384),
             ("conv_w", 768), ("conv_b", 256), ("expert_base", 1)]
ROW, _at = {}, 0
for _name, _n in ROW_PARTS:
    ROW[_name] = (_at, _n)
    _at += _n
NROW = _at

CONST_PARTS = [("ident", 128), ("tri0", 256), ("tri1", 256), ("level0", 7 * 128), ("level1", 7 * 128),
               ("cum0", 128), ("cum1", 128), ("half0", 2), ("half1", 2), ("blocks", 128),
               ("from_prev", 128), ("from_prev_tile", 128), ("from_next", 128), ("from_next_tile", 128),
               ("pick", 256), ("sixteen", 16), ("rope", 4 * 96)]
CONST, _at = {}, 0
for _name, _n in CONST_PARTS:
    CONST[_name] = (_at, _n)
    _at += _n
NCONST = _at


def constants():
    c = np.zeros((P, NCONST), np.float32)

    def put(name, a):
        s, n = CONST[name]
        c[:a.shape[0], s:s + n] = a

    s, t = np.arange(P)[:, None], np.arange(P)[None, :]
    put("ident", (s == t))
    before = [s < t, s > t]
    for d in range(2):
        put(f"tri{d}", np.concatenate([before[d], before[d] | (s == t)], 1))
        levels = []
        for j in range(7):
            w = 2 ** j
            first, second = (s, t) if d == 0 else (t, s)
            levels.append((s // (2 * w) == t // (2 * w)) & (first // w % 2 == 0) & (second // w % 2 == 1))
        put(f"level{d}", np.concatenate(levels, 1))
        early = (s < 64) if d == 0 else (s >= 64)
        put(f"cum{d}", (before[d] | (s == t)).astype(np.float32) - early)
        put(f"half{d}", np.concatenate([early, ~early], 1))
    put("blocks", (s // HD == t // HD))
    put("from_prev", (s == t - 1))
    put("from_prev_tile", (s == P - 1) & (t == 0))
    put("from_next", (s == t + 1))
    put("from_next_tile", (s == 0) & (t == P - 1))
    pick = np.zeros((2, 2, P), np.float32)
    pick[0, 0] = pick[1, 1] = 1
    put("pick", pick.reshape(2, 256))
    put("sixteen", np.tile(np.arange(16), (P, 1)))
    pos = np.arange(DEC)
    row, col = (pos // 64).astype(np.float32), (pos % 64).astype(np.float32)
    parts = []
    for rot in (HD, ROPE):
        nf = rot // 4
        f = (np.float32(10000.0) ** (-np.arange(nf, dtype=np.float32) / np.float32(nf))).astype(np.float32)
        ang = np.concatenate([row[:, None] * f, col[:, None] * f], 1)
        parts += [np.cos(ang), np.sin(ang)]
    put("rope", np.concatenate(parts, 1).reshape(4, P, 96).transpose(1, 0, 2).reshape(P, 384))
    return c


class Marks:

    def __init__(self, sem, *names):
        self.sem, self.names, self.made = sem, names, 0

    def __call__(self, name, step=0):
        return self.sem, step * len(self.names) + self.names.index(name) + 1

    def one(self, name, step=0):
        self.made += 1
        assert self(name, step)[1] == self.made, (name, step, self.made)
        return 1


class Order:

    def __init__(self, eng, sem):
        self.eng, self.sem, self.n = eng, sem, 0

    def __call__(self, ins):
        ins.then_inc(self.sem, 1)
        self.n += 1
        self.eng.wait_ge(self.sem, self.n)


@contextmanager
def stage(nc):
    with ExitStack() as ctx:
        made = []

        def sem(name):
            made.append(ctx.enter_context(nc.semaphore(name)))
            return made[-1]

        yield sem
        nums = [s.num for s in made]
        assert max(nums) - min(nums) + 1 == len(nums)
        nc.all_engine_barrier(sems_to_clear=range(min(nums), max(nums) + 1))


class Memory:

    def __init__(self):
        self.inp, self.out = {}, {}


def at_layer(ap, l):
    x = ap[bass.ds(l, 1)]
    names = "abcd"[:len(ap.shape) - 1]
    left = " ".join(names)
    right = f"(l {names[0]}) " + " ".join(names[1:])
    return x.rearrange(f"l {left} -> {right}")


def row(m, name, a=0, n=None):
    s, full = ROW[name]
    return m.rows[:, s + a:s + a + (full if n is None else n)]


def const(m, name, a=0, n=None, parts=P):
    s, full = CONST[name]
    return m.const[0:parts, s + a:s + a + (full if n is None else n)]


def bc(ap, axis, n):
    x = ap.unsqueeze(axis)
    return x.broadcast_to(tuple(n if i == axis else k for i, k in enumerate(x.shape)))


def stage_start(nc, m):
    with stage(nc) as sem:
        loaded, tanh_ready, ordered = sem("start_loaded"), sem("cond_tanh_ready"), sem("start_order")
        with nc.Block() as block:
            @block.sync
            def _(eng):
                eng.dma_start(m.cond[:, :, :], m.inp["cond"]).then_inc(loaded, 16)
                eng.dma_start(m.const[:, :], m.inp["const"]).then_inc(loaded, 16)
                eng.dma_start(m.x[:, 0, :], m.inp["x_prompt"][0]).then_inc(loaded, 16)
                eng.dma_start(m.x[:, 1:TILES, :],
                              m.inp["x_sample"][0].rearrange("(t p) d -> p t d", p=P)).then_inc(loaded, 16)
                eng.wait_ge(loaded, 64)

            @block.scalar
            def _(eng):
                eng.wait_ge(loaded, 64)
                eng.activation(m.cond_tanh[:, :, :], m.cond[:, :, :], ACT.Tanh, scale=0.5).then_inc(tanh_ready, 1)

            @block.vector
            def _(eng):
                o = Order(eng, ordered)
                eng.wait_ge(loaded, 64)
                o(eng.memset(m.neg_half[:, :], -0.5))
                eng.wait_ge(tanh_ready, 1)
                o(eng.tensor_scalar(m.cond_tanh[:, :, :], m.cond_tanh[:, :, :], 0.5, 0.5, ALU.mult, ALU.add))
                o(eng.tensor_tensor(m.cond[:, :, :], m.cond[:, :, :], m.cond_tanh[:, :, :], ALU.mult))


def stage_modulation(nc, m, l):
    NB = 6 * D // 512
    with stage(nc) as sem:
        loaded = sem("params_loaded")
        w_loaded = [sem(f"w_mod_loaded{b}") for b in range(2)]
        pe = Marks(sem("mod_chunk_made"), "chunk")
        pe_cols = sem("mod_columns_made")
        pe_gate = Marks(sem("gate_rows_made"), "gate")
        row_ready = Marks(sem("mod_row_ready"), "chunk")
        gate_kept = Marks(sem("gate_rows_kept"), "gate")
        ordered = sem("mod_order")
        modrow, bias = m.modrow, m.modbias
        with nc.Block() as block:
            @block.sync
            def _(eng):
                eng.dma_start(m.rows[:, :], m.inp["rows"][bass.ds(l, 1)].rearrange("l n -> (l n)").partition_broadcast(P)).then_inc(loaded, 16)
                eng.dma_start(bias, m.inp["b_mod"][bass.ds(l, 1)].rearrange("l n -> (l n)").partition_broadcast(2)).then_inc(loaded, 16)
                eng.dma_start(m.norm_g[:, :, :], at_layer(m.inp["norm_g"], l)).then_inc(loaded, 16)
                src = at_layer(m.inp["w_mod"], l).rearrange("(c p) n -> p c n", p=P)
                for i in range(NB):
                    if i >= 2:
                        eng.wait_ge(*pe("chunk", i - 2))
                    eng.dma_start(m.w[i % 2], src[:, :, i * 512:(i + 1) * 512]).then_inc(w_loaded[i % 2], 16)
                eng.wait_ge(loaded, 48)

            @block.tensor
            def _(eng):
                for i in range(NB):
                    eng.wait_ge(w_loaded[i % 2], 16 * (i // 2 + 1))
                    if i >= 2:
                        eng.wait_ge(*row_ready("chunk", i - 2))
                    for c in range(KC):
                        mm = eng.matmul(m.ps[0:2, i % 2, :], m.cond[:, c, :], m.w[i % 2][:, c, :],
                                        start=(c == 0), stop=(c == KC - 1))
                    mm.then_inc(pe.sem, pe.one("chunk", i))
                eng.wait_ge(*row_ready("chunk", NB - 1))
                ident2 = const(m, "ident", 0, 2, parts=2)
                for v, part in enumerate((0, 1, 3, 4)):
                    for c in range(KC):
                        k = v * KC + c
                        mm = eng.transpose(m.ps[:, 2, 2 * k:2 * k + 2],
                                           modrow[:, part * D + c * P:part * D + (c + 1) * P], ident2)
                mm.then_inc(pe_cols, 1)
                for k in range(8):
                    g, s, half = k // 4, k // 2 % 2, k % 2
                    if k >= 4:
                        eng.wait_ge(*gate_kept("gate", k - 4))
                    eng.matmul(m.ps[:, 4 + k % 4, :], const(m, "pick", s * P, P, parts=2),
                               modrow[:, (2 + 3 * g) * D + half * 512:(2 + 3 * g) * D + half * 512 + 512],
                               start=True, stop=True).then_inc(pe_gate.sem, pe_gate.one("gate", k))

            @block.vector
            def _(eng):
                o = Order(eng, ordered)
                eng.wait_ge(loaded, 48)
                for i in range(NB):
                    eng.wait_ge(*pe("chunk", i))
                    eng.tensor_tensor(modrow[:, i * 512:(i + 1) * 512], m.ps[0:2, i % 2, :],
                                      bias[:, i * 512:(i + 1) * 512], ALU.add).then_inc(row_ready.sem, row_ready.one("chunk", i))
                eng.wait_ge(pe_cols, 1)
                o(eng.tensor_copy(m.mod_col[:, :, :, :].rearrange("p v s c -> p v c s"),
                                  m.ps[:, 2, 0:8 * KC].rearrange("p (v c s) -> p v c s", v=4, s=2)))
                for n in range(2):
                    for s in range(2):
                        o(eng.scalar_tensor_tensor(m.mod_col[:, 2 * n + 1, s, :], m.mod_col[:, 2 * n + 1, s, :], 1.0,
                                                   m.norm_g[:, n, :], ALU.add, ALU.mult))
                for k in range(8):
                    g, s, half = k // 4, k // 2 % 2, k % 2
                    eng.wait_ge(*pe_gate("gate", k))
                    eng.tensor_copy(m.gate[:, g, s, half * 512:(half + 1) * 512],
                                    m.ps[:, 4 + k % 4, :]).then_inc(gate_kept.sem, gate_kept.one("gate", k))


def stage_norm_project(nc, m, l, which):
    w_dram = m.inp["w_in"] if which == 0 else m.inp["peer_wq"]
    width = D_IN if which == 0 else HEADS * 2 * P
    NB = -(-width // 512)
    XS = m.o
    with stage(nc) as sem:
        w_loaded = [sem(f"w_loaded{b}") for b in range(2)]
        squares = Marks(sem("squares_summed"), "tile")
        mean_ready, rstd_ready = sem("mean_square_ready"), sem("rstd_ready")
        scaled = Marks(sem("tile_scaled"), "tile")
        turned = Marks(sem("chunk_turned"), "chunk")
        h_lat, h_ctx = Marks(sem("h_latent_ready"), "chunk"), Marks(sem("h_context_ready"), "chunk")
        made = Marks(sem("product_made"), "block")
        kept = [Marks(sem("product_kept_by_vector"), "block"), Marks(sem("product_kept_by_scalar"), "block")]
        ordered, keys_loaded = sem("norm_order"), sem("keys_loaded")

        blocks = []
        for n in range(NB):
            cols = min(512, width - n * 512)
            if which == 0:
                blocks += [(n, t, cols) for t in range(TILES)]
            else:
                blocks += [(n, 2 * j + part, (P, DEC)[part]) for j in range(4) for part in range(2)]

        last_of = [max(i for i, b in enumerate(blocks) if b[0] == n) for n in range(NB)]

        def output(i):
            n, k, cols = blocks[i]
            if which == 0:
                return m.z[:, k, n * 512:n * 512 + cols]
            j, part = 4 * n + k // 2, k % 2
            return m.qT[:, j, part * P:part * P + cols]

        with nc.Block() as block:
            @block.sync
            def _(eng):
                src = at_layer(w_dram, l).rearrange("(c p) n -> p c n", p=P)
                for n in range(NB):
                    cols = min(512, width - n * 512)
                    if n >= 2:
                        eng.wait_ge(*made("block", last_of[n - 2]))
                    eng.dma_start(m.w[n % 2][:, :, 0:cols], src[:, :, n * 512:n * 512 + cols]).then_inc(w_loaded[n % 2], 16)

            @block.scalar
            def _(eng):
                for t in range(TILES):
                    eng.activation(XS[:, t, :], m.x[:, t, :], ACT.Square, scale=float(D) ** -0.5,
                                   accum_out=m.small[:, t:t + 1]).then_inc(squares.sem, squares.one("tile", t))
                for c in range(KC):
                    eng.wait_ge(*turned("chunk", c))
                    eng.activation(m.hT[:, c, 0:P], m.ps[:, 2 * (c % 2) + 1, 0:P], ACT.Identity,
                                   scale=m.mod_col[:, 2 * which + 1, 0, c:c + 1],
                                   bias=m.mod_col[:, 2 * which, 0, c:c + 1]).then_inc(h_ctx.sem, h_ctx.one("chunk", c))
                for i in range(1, len(blocks), 2):
                    eng.wait_ge(*made("block", i))
                    eng.activation(output(i), m.ps[:, 4 + i % 4, 0:blocks[i][2]], ACT.Copy).then_inc(
                        kept[1].sem, kept[1].one("block", i // 2))

            @block.gpsimd
            def _(eng):
                eng.wait_ge(mean_ready, 1)
                eng.tensor_tensor(m.small[:, 16:16 + TILES], m.small[:, 8:8 + TILES], m.neg_half[:, 0:TILES],
                                  ALU.pow).then_inc(rstd_ready, 1)

            @block.vector
            def _(eng):
                eng.wait_ge(*squares("tile", TILES - 1))
                eng.tensor_scalar(m.small[:, 8:8 + TILES], m.small[:, 0:TILES], EPS, None, ALU.add).then_inc(mean_ready, 1)
                eng.wait_ge(rstd_ready, 1)
                for t in range(TILES):
                    eng.tensor_scalar(XS[:, t, :], m.x[:, t, :], m.small[:, 16 + t:17 + t], None,
                                      ALU.mult).then_inc(scaled.sem, scaled.one("tile", t))
                for c in range(KC):
                    eng.wait_ge(*turned("chunk", c))
                    eng.tensor_scalar(m.hT[:, c, P:TOK], m.ps[:, 2 * (c % 2), :],
                                      m.mod_col[:, 2 * which + 1, 1, c:c + 1], m.mod_col[:, 2 * which, 1, c:c + 1],
                                      ALU.mult, ALU.add).then_inc(h_lat.sem, h_lat.one("chunk", c))
                for i in range(0, len(blocks), 2):
                    eng.wait_ge(*made("block", i))
                    eng.tensor_copy(output(i), m.ps[:, 4 + i % 4, 0:blocks[i][2]]).then_inc(
                        kept[0].sem, kept[0].one("block", i // 2))

            @block.tensor
            def _(eng):
                eng.wait_ge(*scaled("tile", TILES - 1))
                for c in range(KC):
                    if c >= 2:
                        eng.wait_ge(*h_lat("chunk", c - 2))
                        eng.wait_ge(*h_ctx("chunk", c - 2))
                    eng.transpose(m.ps[:, 2 * (c % 2) + 1, 0:P], XS[:, 0, c * P:(c + 1) * P], const(m, "ident"))
                    for t in range(1, TILES):
                        mm = eng.transpose(m.ps[:, 2 * (c % 2), (t - 1) * P:t * P], XS[:, t, c * P:(c + 1) * P],
                                           const(m, "ident"))
                    mm.then_inc(turned.sem, turned.one("chunk", c))
                eng.wait_ge(*h_lat("chunk", KC - 1))
                eng.wait_ge(*h_ctx("chunk", KC - 1))
                for i, (n, k, cols) in enumerate(blocks):
                    if i == 0 or blocks[i - 1][0] != n:
                        eng.wait_ge(w_loaded[n % 2], 16 * (n // 2 + 1))
                    if i >= 4:
                        eng.wait_ge(*kept[i % 2]("block", (i - 4) // 2))
                    for c in range(KC):
                        if which == 0:
                            mm = eng.matmul(m.ps[:, 4 + i % 4, 0:cols], m.hT[:, c, k * P:(k + 1) * P],
                                            m.w[n % 2][:, c, 0:cols], start=(c == 0), stop=(c == KC - 1))
                        else:
                            j, part = k // 2, k % 2
                            mm = eng.matmul(m.ps[:, 4 + i % 4, 0:cols], m.w[n % 2][:, c, j * P:(j + 1) * P],
                                            m.hT[:, c, part * P:part * P + cols], start=(c == 0), stop=(c == KC - 1))
                    mm.then_inc(made.sem, made.one("block", i))


def stage_rwkv(nc, m, l):
    STEPS = TILES
    LANES = range(2)
    PE_POINTS = (["ranks_turned", "logits", "cumulated", "rows_turned", "products", "c0"]
                 + [f"{x}{j}" for j in range(1, 7) for x in ("cx", "xy")] + ["rhs", "u", "end"])
    V_POINTS = (["logits_biased", "gates", "exclusive", "factors", "keys_turned", "masked", "c0t", "xy0"]
                + ["state_scaled"] + [f"xy{j}" for j in range(1, 7)] + ["y_kept", "state_kept"])
    A_POINTS = (["rank_tanh", "rank_copied", "tanh", "decays_read", "decays", "queries_turned"]
                + [f"cx{j}" for j in range(1, 7)] + ["rhs", "u"])
    G_POINTS = ["norm"] + [f"level{j}" for j in range(1, 7)]

    def tile_of(n, d):
        return n if n == 0 or d == 0 else TILES - n

    with stage(nc) as sem:
        loaded, zeroed = sem("rwkv_weights_loaded"), sem("state_zeroed")
        state_loaded = sem("state_loaded")
        state_stored = sem("state_stored")
        pe = [Marks(sem(f"pe{d}"), *PE_POINTS) for d in LANES]
        vec = [Marks(sem(f"vector{d}"), *V_POINTS) for d in LANES]
        act = [Marks(sem(f"scalar{d}"), *A_POINTS) for d in LANES]
        pool = [Marks(sem(f"pool{d}"), *G_POINTS) for d in LANES]
        squares = [Marks(sem(f"squares{d}"), "sum") for d in LANES]
        ordered, act_ordered = sem("rwkv_order"), sem("rwkv_scalar_order")
        ident = const(m, "ident")

        def bank(d, k):
            return m.ps[:, 4 * d + k, :]

        def heads4(ap):
            return ap.rearrange("p (h x) -> p h x", h=4)

        with nc.Block() as block:
            @block.sync
            def _(eng):
                eng.dma_start(m.wu[:, :, :], at_layer(m.inp["rw_wu"], l).rearrange("e r n -> r e n")).then_inc(loaded, 16)
                eng.dma_start(m.au[:, :, :], at_layer(m.inp["rw_au"], l).rearrange("e r n -> r e n")).then_inc(loaded, 16)
                eng.dma_start(m.gu[:, :], at_layer(m.inp["rw_gu"], l)).then_inc(loaded, 16)
                for d in LANES:
                    eng.wait_ge(*vec[d]("state_kept", 0))
                    for par in range(2):
                        eng.dma_start(m.out["state"][bass.ds(l, 1), d, par].rearrange("l k q v -> (l k) q v"),
                                      m.state[d][par * HD:(par + 1) * HD, :, par * HD:(par + 1) * HD]).then_inc(state_stored, 16)
                eng.wait_ge(state_stored, 64)
                for d in LANES:
                    for par in range(2):
                        eng.dma_start(m.state[d][par * HD:(par + 1) * HD, :, par * HD:(par + 1) * HD],
                                      m.inp["state"][bass.ds(l, 1), d, par].rearrange("l k q v -> (l k) q v")).then_inc(state_loaded, 16)
                eng.wait_ge(state_loaded, 64)
                eng.wait_ge(loaded, 48)

            @block.tensor
            def _(eng):
                eng.wait_ge(loaded, 48)
                for n in range(STEPS):
                    tl = [tile_of(n, d) for d in LANES]
                    for d in LANES:
                        if n > 0:
                            eng.wait_ge(*vec[d]("state_kept", n - 1))
                        z = m.z[:, tl[d], :]
                        eng.transpose(bank(d, 0)[0:64, 0:P], z[:, ZWD + 64 * d:ZWD + 64 * d + 64], ident)
                        eng.transpose(bank(d, 0)[0:32, P:2 * P], z[:, ZAD + 32 * d:ZAD + 32 * d + 32],
                                      ident).then_inc(pe[d].sem, pe[d].one("ranks_turned", n))
                    for d in LANES:
                        eng.wait_ge(*act[d]("rank_copied", n))
                        eng.matmul(bank(d, 1)[:, 0:GW], m.wdT[d][:, :], m.wu[:, d, :], start=True, stop=True)
                        eng.matmul(bank(d, 1)[:, GW:2 * GW], m.adT[d][:, :], m.au[:, d, :], start=True,
                                   stop=True).then_inc(pe[d].sem, pe[d].one("logits", n))
                    for d in LANES:
                        eng.wait_ge(*vec[d]("gates", n))
                        eng.matmul(bank(d, 0)[:, 0:GW], const(m, f"cum{d}"), m.sg[d][:, 0:GW], start=True, stop=True)
                        for q in range(2):
                            mm = eng.matmul(bank(d, 0)[:, GW + 2 * q:GW + 2 * q + 2], m.sg[d][:, q * P:(q + 1) * P],
                                            const(m, f"half{d}"), start=True, stop=True)
                        mm.then_inc(pe[d].sem, pe[d].one("cumulated", n))
                    for d in LANES:
                        eng.wait_ge(*vec[d]("factors", n))
                        for q in range(2):
                            for k, a in enumerate((m.kq[d], m.rq[d])):
                                eng.transpose(bank(d, 2)[:, (2 * q + k) * P:(2 * q + k + 1) * P], a[:, q * P:(q + 1) * P], ident)
                            for k, a in enumerate((m.bd[d], m.kd[d])):
                                mm = eng.transpose(bank(d, 3)[:, (2 * q + k) * P:(2 * q + k + 1) * P], a[:, q * P:(q + 1) * P], ident)
                        mm.then_inc(pe[d].sem, pe[d].one("rows_turned", n))
                    for d in LANES:
                        eng.wait_ge(*act[d]("queries_turned", n))
                        eng.wait_ge(*vec[d]("keys_turned", n))
                        for h in range(4):
                            q, base = h // 2, HD * (h % 2)
                            rhs = m.qT_rw[d][base:base + HD, q * 2 * P:(q + 1) * 2 * P]
                            for k in range(2):
                                mm = eng.matmul(bank(d, 2 * k + h % 2)[:, q * 2 * P:(q + 1) * 2 * P],
                                                m.kT_rw[d][base:base + HD, (2 * q + k) * P:(2 * q + k + 1) * P], rhs,
                                                start=True, stop=True)
                        mm.then_inc(pe[d].sem, pe[d].one("products", n))
                    for d in LANES:
                        eng.wait_ge(*vec[d]("c0t", n))
                        for h in range(4):
                            mm = eng.matmul(bank(d, 0)[:, h * P:(h + 1) * P], m.ct[d][0][:, h * P:(h + 1) * P], ident,
                                            start=True, stop=True)
                        mm.then_inc(pe[d].sem, pe[d].one("c0", n))
                    for j in range(1, 7):
                        for d in LANES:
                            eng.wait_ge(*vec[d](f"xy{j - 1}", n))
                            eng.wait_ge(*pool[d](f"level{j}", n))
                            for h in range(4):
                                s = slice(h * P, (h + 1) * P)
                                mm = eng.matmul(bank(d, 1)[:, s], m.ct[d][j % 2][:, s], m.inv[d][:, s], start=True, stop=True)
                            mm.then_inc(pe[d].sem, pe[d].one(f"cx{j}", n))
                        for d in LANES:
                            eng.wait_ge(*act[d](f"cx{j}", n))
                            for h in range(4):
                                s = slice(h * P, (h + 1) * P)
                                if j < 6:
                                    eng.matmul(bank(d, 2)[:, s], m.invT[d][:, s], m.cx[d][:, s], start=True, stop=True)
                                mm = eng.matmul(bank(d, 3)[:, s], m.cx[d][:, s], m.invT[d][:, s], start=True, stop=True)
                            mm.then_inc(pe[d].sem, pe[d].one(f"xy{j}", n))
                    for d in LANES:
                        v = m.z[:, tl[d], ZV:ZV + GW]
                        eng.wait_ge(*vec[d]("state_scaled", n))
                        for h in range(4):
                            q = h // 2
                            if h % 2 == 0:
                                eng.matmul(bank(d, 0)[:, q * P:(q + 1) * P], m.qT_rw[d][:, 2 * q * P:(2 * q + 1) * P],
                                           m.state_in[d][:, q, :], start=True, stop=False, skip_group_check=True)
                            mm = eng.matmul(bank(d, 0)[:, h * HD:(h + 1) * HD], m.mg[d][:, 2 * h * P:(2 * h + 1) * P],
                                            v[:, h * HD:(h + 1) * HD], start=False, stop=True, skip_group_check=True)
                        mm.then_inc(pe[d].sem, pe[d].one("rhs", n))
                    for d in LANES:
                        eng.wait_ge(*act[d]("rhs", n))
                        eng.wait_ge(*vec[d]("xy6", n))
                        for h in range(4):
                            mm = eng.matmul(bank(d, 1)[:, h * HD:(h + 1) * HD], m.invT[d][:, h * P:(h + 1) * P],
                                            m.rhs[d][:, h * HD:(h + 1) * HD], start=True, stop=True)
                        mm.then_inc(pe[d].sem, pe[d].one("u", n))
                    for d in LANES:
                        v = m.z[:, tl[d], ZV:ZV + GW]
                        eng.wait_ge(*act[d]("u", n))
                        for h in range(4):
                            q, hs = h // 2, slice(h * HD, (h + 1) * HD)
                            if h % 2 == 0:
                                eng.matmul(bank(d, 2)[:, q * P:(q + 1) * P], m.qT_rw[d][:, (2 * q + 1) * P:(2 * q + 2) * P],
                                           m.state_in[d][:, q, :], start=True, stop=False, skip_group_check=True)
                            eng.matmul(bank(d, 2)[:, hs], m.mg[d][:, (2 * h + 1) * P:(2 * h + 2) * P], v[:, hs],
                                       start=False, stop=False, skip_group_check=True)
                            eng.matmul(bank(d, 2)[:, hs], m.lh[d][:, (2 * h + 1) * P:(2 * h + 2) * P], m.u[d][:, hs],
                                       start=False, stop=True, skip_group_check=True)
                        for q in range(2):
                            qs = slice(q * P, (q + 1) * P)
                            eng.matmul(bank(d, 3)[:, qs], ident, m.state_in[d][:, q, :], start=True, stop=False, skip_group_check=True)
                            eng.matmul(bank(d, 3)[:, qs], m.kd[d][:, qs], v[:, qs], start=False, stop=False, skip_group_check=True)
                            mm = eng.matmul(bank(d, 3)[:, qs], m.bd[d][:, qs], m.u[d][:, qs], start=False, stop=True, skip_group_check=True)
                        mm.then_inc(pe[d].sem, pe[d].one("end", n))

            @block.scalar
            def _(eng):
                o = Order(eng, act_ordered)
                for n in range(STEPS):
                    for d in LANES:
                        eng.wait_ge(*pe[d]("ranks_turned", n))
                        eng.activation(m.wdT[d][:, :], bank(d, 0)[0:64, 0:P], ACT.Tanh).then_inc(act[d].sem, act[d].one("rank_tanh", n))
                        eng.activation(m.adT[d][:, :], bank(d, 0)[0:32, P:2 * P], ACT.Copy).then_inc(act[d].sem, act[d].one("rank_copied", n))
                    for d in LANES:
                        eng.wait_ge(*vec[d]("logits_biased", n))
                        eng.activation(m.sg[d][:, :], m.sg[d][:, :], ACT.Tanh, scale=0.5).then_inc(act[d].sem, act[d].one("tanh", n))
                    for d in LANES:
                        eng.wait_ge(*pe[d]("cumulated", n))
                        if n > 0:
                            eng.wait_ge(*pe[d]("cx6", n - 1))
                        o(eng.activation(m.dec[d][:, 0, :], bank(d, 0)[:, 0:GW], ACT.Exp, scale=-DECAY))
                        o(eng.activation(m.ends[d][:, :], bank(d, 0)[:, GW:GW + 4], ACT.Exp, scale=-DECAY))
                        eng.activation(m.dec[d][:, 1, :], bank(d, 0)[:, 0:GW], ACT.Exp, scale=DECAY).then_inc(act[d].sem, act[d].one("decays_read", n))
                        eng.wait_ge(*vec[d]("exclusive", n))
                        eng.activation(m.dec[d][:, 2, :], m.dec[d][:, 3, :], ACT.Exp, scale=-DECAY).then_inc(act[d].sem, act[d].one("decays", n))
                    for d in LANES:
                        eng.wait_ge(*pe[d]("rows_turned", n))
                        eng.activation(m.qT_rw[d][:, :], bank(d, 2), ACT.Copy).then_inc(act[d].sem, act[d].one("queries_turned", n))
                    for j in range(1, 7):
                        for d in LANES:
                            eng.wait_ge(*pe[d](f"cx{j}", n))
                            eng.activation(m.cx[d][:, :], bank(d, 1), ACT.Copy).then_inc(act[d].sem, act[d].one(f"cx{j}", n))
                    for d in LANES:
                        eng.wait_ge(*pe[d]("rhs", n))
                        eng.activation(m.rhs[d][:, :], bank(d, 0)[:, 0:GW], ACT.Copy).then_inc(act[d].sem, act[d].one("rhs", n))
                    for d in LANES:
                        eng.wait_ge(*pe[d]("u", n))
                        eng.activation(m.u[d][:, :], bank(d, 1)[:, 0:GW], ACT.Copy).then_inc(act[d].sem, act[d].one("u", n))

            @block.gpsimd
            def _(eng):
                for n in range(STEPS):
                    for d in LANES:
                        eng.wait_ge(*squares[d]("sum", n))
                        eng.tensor_tensor(m.kn[d][:, 4:8], m.kn[d][:, 0:4], m.neg_half[:, 0:4], ALU.pow).then_inc(
                            pool[d].sem, pool[d].one("norm", n))
                    for j in range(1, 7):
                        for d in LANES:
                            eng.wait_ge(*vec[d]("masked", n))
                            if j == 2:
                                eng.wait_ge(*vec[d]("xy0", n))
                            if j > 2:
                                eng.wait_ge(*pe[d](f"cx{j - 2}", n))
                            eng.tensor_tensor(heads4(m.ct[d][j % 2][:, :]),
                                              m.lh[d][:, :].rearrange("p (h k x) -> p h k x", h=4, k=2)[:, :, 0, :],
                                              bc(const(m, f"level{d}", j * P, P), 1, 4), ALU.mult).then_inc(
                                pool[d].sem, pool[d].one(f"level{j}", n))

            @block.vector
            def _(eng):
                o = Order(eng, ordered)
                for d in LANES:
                    o(eng.memset(m.state[d][:, :, :], 0.0))
                for n in range(STEPS):
                    tl = [tile_of(n, d) for d in LANES]
                    for d in LANES:
                        kraw, kk, tmp = m.z[:, tl[d], ZK:ZK + GW], m.kk[d][:, :], m.tmp[d][:, :]
                        o(eng.tensor_tensor(kk, kraw, row(m, "rw_kk"), ALU.mult))
                        o(eng.tensor_tensor(tmp, kk, kk, ALU.mult))
                        o(eng.tensor_reduce(m.kn[d][:, 0:4], heads4(tmp), AX.X, ALU.add))
                        eng.tensor_scalar(m.kn[d][:, 0:4], m.kn[d][:, 0:4], EPS, None, ALU.add).then_inc(squares[d].sem, squares[d].one("sum", n))
                    for d in LANES:
                        eng.wait_ge(*pe[d]("logits", n))
                        eng.tensor_tensor(m.sg[d][:, :], bank(d, 1), row(m, "wa0", 512 * d, 512), ALU.add).then_inc(
                            vec[d].sem, vec[d].one("logits_biased", n))
                    for d in LANES:
                        eng.wait_ge(*act[d]("tanh", n))
                        eng.tensor_scalar(m.sg[d][:, :], m.sg[d][:, :], 0.5, 0.5, ALU.mult, ALU.add).then_inc(vec[d].sem, vec[d].one("gates", n))
                    for d in LANES:
                        eng.wait_ge(*vec[d]("gates", n))
                        eng.wait_ge(*pool[d]("norm", n))
                        o(eng.tensor_tensor(heads4(m.kk[d][:, :]), heads4(m.kk[d][:, :]), bc(m.kn[d][:, 4:8], 2, HD), ALU.mult))
                        eng.wait_ge(*act[d]("decays_read", n))
                        eng.tensor_tensor(m.dec[d][:, 3, :], bank(d, 0)[:, 0:GW], m.sg[d][:, 0:GW], ALU.subtract).then_inc(
                            vec[d].sem, vec[d].one("exclusive", n))
                    for d in LANES:
                        z = m.z[:, tl[d], :]
                        a, kraw = m.sg[d][:, GW:2 * GW], z[:, ZK:ZK + GW]
                        tmp, kk = m.tmp[d][:, :], m.kk[d][:, :]
                        o(eng.tensor_tensor(m.rq[d][:, :], z[:, ZR:ZR + GW], m.dec[d][:, 0, :], ALU.mult))
                        o(eng.scalar_tensor_tensor(tmp, a, 1.0, row(m, "rw_ka"), ALU.subtract, ALU.mult))
                        o(eng.scalar_tensor_tensor(tmp, tmp, 1.0, kraw, ALU.add, ALU.mult))
                        o(eng.tensor_tensor(m.kd[d][:, :], tmp, m.dec[d][:, 1, :], ALU.mult))
                        o(eng.tensor_tensor(tmp, kk, a, ALU.mult))
                        o(eng.scalar_tensor_tensor(m.bd[d][:, :], tmp, -1.0, m.dec[d][:, 1, :], ALU.mult, ALU.mult))
                        eng.wait_ge(*act[d]("decays", n))
                        eng.tensor_tensor(m.kq[d][:, :], kk, m.dec[d][:, 2, :], ALU.mult).then_inc(vec[d].sem, vec[d].one("factors", n))
                    for d in LANES:
                        eng.wait_ge(*pe[d]("rows_turned", n))
                        eng.tensor_copy(m.kT_rw[d][:, :], bank(d, 3)).then_inc(vec[d].sem, vec[d].one("keys_turned", n))
                    for d in LANES:
                        eng.wait_ge(*pe[d]("products", n))
                        for k, (bank_k, to) in enumerate(((0, m.lh[d]), (1, m.lh[d]), (2, m.mg[d]), (3, m.mg[d]))):
                            par = k % 2
                            ins = eng.tensor_tensor(to.rearrange("p (q par x) -> p q par x", q=2, par=2)[:, :, par, :],
                                                    bank(d, bank_k).rearrange("p (h x) -> p h x", h=2),
                                                    bc(const(m, f"tri{d}"), 1, 2), ALU.mult)
                            if k < 3:
                                o(ins)
                        ins.then_inc(vec[d].sem, vec[d].one("masked", n))
                        eng.wait_ge(*vec[d]("masked", n))
                        if n > 0:
                            eng.wait_ge(*pe[d]("end", n - 1))
                        eng.tensor_tensor(heads4(m.ct[d][0][:, :]),
                                          m.lh[d][:, :].rearrange("p (h k x) -> p h k x", h=4, k=2)[:, :, 0, :],
                                          bc(const(m, f"level{d}", 0, P), 1, 4), ALU.mult).then_inc(vec[d].sem, vec[d].one("c0t", n))
                        eng.wait_ge(*vec[d]("c0t", n))
                        o(eng.tensor_tensor(heads4(m.invT[d][:, :]), heads4(m.ct[d][0][:, :]), bc(ident, 1, 4), ALU.add))
                    for d in LANES:
                        eng.wait_ge(*pe[d]("c0", n))
                        eng.tensor_tensor(heads4(m.inv[d][:, :]), heads4(bank(d, 0)), bc(ident, 1, 4), ALU.add).then_inc(
                            vec[d].sem, vec[d].one("xy0", n))
                    for d in LANES:
                        if n == 1 and d == 0:
                            eng.wait_ge(state_loaded, 64)
                        for q in range(2):
                            ins = eng.tensor_scalar(m.state_in[d][:, q, :], m.state[d][:, q, :], m.ends[d][:, 2 * q:2 * q + 1],
                                                    None, ALU.mult)
                        ins.then_inc(vec[d].sem, vec[d].one("state_scaled", n))
                    for j in range(1, 7):
                        for d in LANES:
                            eng.wait_ge(*pe[d](f"xy{j}", n))
                            if j < 6:
                                o(eng.tensor_tensor(m.inv[d][:, :], bank(d, 2), m.inv[d][:, :], ALU.add))
                            eng.tensor_tensor(m.invT[d][:, :], bank(d, 3), m.invT[d][:, :], ALU.add).then_inc(
                                vec[d].sem, vec[d].one(f"xy{j}", n))
                    for d in LANES:
                        eng.wait_ge(*pe[d]("end", n))
                        eng.tensor_copy(m.o[:, tl[d], d * GW:(d + 1) * GW], bank(d, 2)[:, 0:GW]).then_inc(vec[d].sem, vec[d].one("y_kept", n))
                        for q in range(2):
                            ins = eng.scalar_tensor_tensor(m.state[d][:, q, :], bank(d, 3)[:, q * P:(q + 1) * P],
                                                           m.ends[d][:, 2 * q + 1:2 * q + 2], const(m, "blocks"), ALU.mult, ALU.mult)
                            if q == 0:
                                o(ins)
                        ins.then_inc(vec[d].sem, vec[d].one("state_kept", n))
                        eng.wait_ge(*vec[d]("state_kept", n))


def stage_rwkv_output(nc, m):
    with stage(nc) as sem:
        pe = Marks(sem("gate_pe"), "turned", "gated")
        act = Marks(sem("gate_scalar"), "tanh")
        vec = Marks(sem("gate_vector"), "squares", "sigmoid", "done")
        pool = Marks(sem("gate_pool"), "norm")
        ordered = sem("gate_order")

        def heads4(ap):
            return ap.rearrange("p (h x) -> p h x", h=4)

        with nc.Block() as block:
            @block.tensor
            def _(eng):
                for t in range(TILES):
                    if t > 0:
                        eng.wait_ge(*vec("done", t - 1))
                    eng.transpose(m.ps[:, 0, 0:P], m.z[:, t, ZGD:ZGD + P], const(m, "ident")).then_inc(pe.sem, pe.one("turned", t))
                    eng.wait_ge(*vec("sigmoid", t))
                    eng.matmul(m.ps[:, 1, 0:GW], m.gdT[:, :], m.gu[:, :], start=True, stop=True).then_inc(pe.sem, pe.one("gated", t))

            @block.scalar
            def _(eng):
                for t in range(TILES):
                    eng.wait_ge(*pe("turned", t))
                    if t > 0:
                        eng.wait_ge(*pe("gated", t - 1))
                    eng.activation(m.gdT[:, :], m.ps[:, 0, 0:P], ACT.Tanh, scale=0.5).then_inc(act.sem, act.one("tanh", t))

            @block.gpsimd
            def _(eng):
                for t in range(TILES):
                    eng.wait_ge(*vec("squares", t))
                    eng.tensor_tensor(m.kn[0][:, 4:8], m.kn[0][:, 0:4], m.neg_half[:, 0:4], ALU.pow).then_inc(pool.sem, pool.one("norm", t))

            @block.vector
            def _(eng):
                o = Order(eng, ordered)
                for t in range(TILES):
                    z = m.z[:, t, :]
                    y, tmp, bonus = m.kk[0][:, :], m.tmp[0][:, :], m.kk[1][:, :]
                    o(eng.tensor_tensor(y, m.o[:, t, 0:GW], m.o[:, t, GW:2 * GW], ALU.add))
                    o(eng.tensor_tensor(tmp, y, y, ALU.mult))
                    o(eng.tensor_reduce(m.kn[0][:, 0:4], heads4(tmp), AX.X, ALU.add))
                    eng.tensor_scalar(m.kn[0][:, 0:4], m.kn[0][:, 0:4], 1.0 / HD, EPS, ALU.mult, ALU.add).then_inc(vec.sem, vec.one("squares", t))
                    o(eng.tensor_tensor(tmp, z[:, ZR:ZR + GW], z[:, ZK:ZK + GW], ALU.mult))
                    o(eng.tensor_tensor(tmp, tmp, row(m, "rw_rk"), ALU.mult))
                    o(eng.tensor_reduce(m.kn[1][:, 0:4], heads4(tmp), AX.X, ALU.add))
                    o(eng.tensor_tensor(heads4(bonus), heads4(z[:, ZV:ZV + GW]), bc(m.kn[1][:, 0:4], 2, HD), ALU.mult))
                    eng.wait_ge(*act("tanh", t))
                    eng.tensor_scalar(m.gdT[:, :], m.gdT[:, :], 0.5, 0.5, ALU.mult, ALU.add).then_inc(vec.sem, vec.one("sigmoid", t))
                    eng.wait_ge(*pool("norm", t))
                    o(eng.tensor_tensor(heads4(y), heads4(y), bc(m.kn[0][:, 4:8], 2, HD), ALU.mult))
                    o(eng.tensor_tensor(y, y, row(m, "rw_gn"), ALU.mult))
                    o(eng.tensor_tensor(y, y, bonus, ALU.add))
                    eng.wait_ge(*pe("gated", t))
                    eng.tensor_tensor(m.o[:, t, 0:GW], y, m.ps[:, 1, 0:GW], ALU.mult).then_inc(vec.sem, vec.one("done", t))
                    eng.wait_ge(*vec("done", t))


def rope(o, eng, x, half, cos, sin, tmp):
    heads = x.shape[1]
    x1, x2 = x[:, :, 0:half], x[:, :, half:2 * half]
    c, s = bc(cos, 1, heads), bc(sin, 1, heads)
    t1, t2 = (t.rearrange("p (h x) -> p h x", h=heads) for t in tmp)
    o(eng.tensor_tensor(t1, x2, s, ALU.mult))
    o(eng.tensor_tensor(t2, x1, s, ALU.mult))
    o(eng.tensor_tensor(x1, x1, c, ALU.mult))
    o(eng.tensor_tensor(x2, x2, c, ALU.mult))
    o(eng.tensor_tensor(x1, x1, t1, ALU.subtract))
    o(eng.tensor_tensor(x2, x2, t2, ALU.add))


def stage_attention_inputs(nc, m, l):
    STEPS = TILES + 1
    with stage(nc) as sem:
        loaded, stored = sem("attn_loaded"), sem("caches_stored")
        squares = Marks(sem("first_squares"), "sum")
        act = Marks(sem("attn_scalar"), "latents_turned", "values", "squares", "queries_kept")
        vec = Marks(sem("first_mean"), "mean", "rows")
        vec2 = Marks(sem("attn_vector"), "gqa_q", "gqa_k", "expanded", "mean", "rows", "keys_kept")
        pool, pool2 = Marks(sem("first_norm"), "norm"), Marks(sem("second_norm"), "norm")
        pe = Marks(sem("attn_pe"), "turned", "expanded", "heads_turned")
        ordered, act_ordered = sem("attn_order"), sem("attn_scalar_order")
        ident = const(m, "ident")

        def slot(i):
            return {0: 0, TILES: 1}.get(i, i + 1)

        with nc.Block() as block:
            @block.sync
            def _(eng):
                wuq = at_layer(m.inp["mla_wuq"], l)
                eng.dma_start(m.wuq0, wuq[0:P, :]).then_inc(loaded, 16)
                eng.dma_start(m.wuq1, wuq[P:Q_RANK, :]).then_inc(loaded, 16)
                eng.dma_start(m.wukv, at_layer(m.inp["mla_wukv"], l)).then_inc(loaded, 16)
                eng.dma_start(m.cache_ckv, at_layer(m.inp["cache_mla_ckv"][0], l)).then_inc(loaded, 16)
                eng.dma_start(m.cache_krope, at_layer(m.inp["cache_mla_krope"][0], l)).then_inc(loaded, 16)
                eng.dma_start(m.cache_k, at_layer(m.inp["cache_gqa_k"][0], l).rearrange("t h x -> t (h x)")).then_inc(loaded, 16)
                eng.dma_start(m.cache_v, at_layer(m.inp["cache_gqa_v"][0], l).rearrange("t h x -> t (h x)")).then_inc(loaded, 16)
                eng.dma_start(at_layer(m.out["krope"][0], l), m.z[:, 0, ZKR:ZKR + ROPE]).then_inc(stored, 16)
                eng.dma_start(at_layer(m.out["gqa_v"][0], l).rearrange("t h x -> t (h x)"), m.z[:, 0, ZVG:ZVG + 2 * HD]).then_inc(stored, 16)
                eng.wait_ge(*vec("rows", 0))
                eng.dma_start(at_layer(m.out["ckv"][0], l), m.cn).then_inc(stored, 16)
                eng.dma_start(at_layer(m.out["gqa_k"][0], l).rearrange("t h x -> t (h x)"), m.gqk[:, 4 * HD:6 * HD]).then_inc(stored, 16)
                eng.wait_ge(stored, 64)
                eng.wait_ge(loaded, 112)

            @block.scalar
            def _(eng):
                o = Order(eng, act_ordered)

                def first(t):
                    if t > 0:
                        eng.wait_ge(*vec("rows", t - 1))
                        eng.wait_ge(*vec2("mean", t - 1))
                    z = m.z[:, t, :]
                    o(eng.activation(m.sq[:, 0:Q_RANK], z[:, ZQC:ZQC + Q_RANK], ACT.Square, scale=Q_RANK ** -0.5, accum_out=m.small[:, 0:1]))
                    o(eng.activation(m.sq[:, 0:KV_RANK], z[:, ZCKV:ZCKV + KV_RANK], ACT.Square, scale=KV_RANK ** -0.5, accum_out=m.small[:, 1:2]))
                    eng.activation(m.sq[:, 0:6 * HD], z[:, ZQG:ZQG + 6 * HD], ACT.Square, scale=HD ** -0.5).then_inc(squares.sem, squares.one("sum", t))

                for i in range(STEPS):
                    if i < TILES:
                        first(i)
                    eng.wait_ge(*pe("turned", i))
                    lo = 0 if i < TILES else 256
                    eng.activation(m.latT[:, lo:384], m.ps[:, 0, lo:384], ACT.Copy).then_inc(act.sem, act.one("latents_turned", i))
                    eng.wait_ge(*vec2("expanded", i))
                    eng.activation(m.vm[:, slot(i), :].rearrange("p (h x) -> p h x", h=4),
                                   m.ps[:, 4, :].rearrange("p (h x) -> p h x", h=4)[:, :, NOPE:P], ACT.Copy).then_inc(act.sem, act.one("values", i))
                    lo = 0 if i < TILES else 4
                    if i < TILES:
                        eng.wait_ge(*vec("mean", i))
                    eng.activation(m.sq[:, lo * QK:8 * QK], m.qk[:, lo * QK:8 * QK], ACT.Square, scale=QK ** -0.5).then_inc(act.sem, act.one("squares", i))
                    eng.wait_ge(*pe("heads_turned", i))
                    if i < TILES:
                        eng.activation(m.qTm[:, :, i * P:(i + 1) * P], m.ps[0:QK, 5, :].rearrange("p (h x) -> p h x", h=4),
                                       ACT.Copy).then_inc(act.sem, act.one("queries_kept", i))

            @block.gpsimd
            def _(eng):
                for i in range(STEPS):
                    if i < TILES:
                        eng.wait_ge(*vec("mean", i))
                        eng.tensor_tensor(m.small[:, 8:16], m.small[:, 0:8], m.neg_half[:, 0:8], ALU.pow).then_inc(pool.sem, pool.one("norm", i))
                    eng.wait_ge(*vec2("mean", i))
                    lo = 0 if i < TILES else 4
                    eng.tensor_tensor(m.small[:, 24 + lo:32], m.small[:, 16 + lo:24], m.neg_half[:, lo:8], ALU.pow).then_inc(pool2.sem, pool2.one("norm", i))

            @block.tensor
            def _(eng):
                eng.wait_ge(loaded, 112)
                for i in range(STEPS):
                    token = i < TILES
                    if token:
                        eng.wait_ge(*vec("rows", i))
                        eng.transpose(m.ps[:, 0, 0:P], m.qn[:, 0:P], ident)
                        eng.transpose(m.ps[0:64, 0, P:2 * P], m.qn[:, P:Q_RANK], ident)
                        for h in range(4):
                            eng.transpose(m.ps[0:HD, 1, h * P:(h + 1) * P], m.gqk[:, h * HD:(h + 1) * HD], ident)
                    for h in range(2):
                        src = m.gqk[:, (4 + h) * HD:(5 + h) * HD] if token else m.cache_k[:, h * HD:(h + 1) * HD]
                        if i > 0 and h == 0:
                            eng.wait_ge(*vec2("gqa_k", i - 1))
                        eng.transpose(m.ps[0:HD, 2, h * P:(h + 1) * P], src, ident)
                    eng.transpose(m.ps[:, 0, 2 * P:3 * P], m.cn if token else m.cache_ckv, ident).then_inc(pe.sem, pe.one("turned", i))
                    eng.wait_ge(*act("latents_turned", i))
                    if token:
                        eng.matmul(m.ps[:, 3, 0:4 * QK], m.latT[:, 0:P], m.wuq0, start=True, stop=False)
                        eng.matmul(m.ps[:, 3, 0:4 * QK], m.latT[0:64, P:2 * P], m.wuq1, start=False, stop=True)
                    if i > 0:
                        eng.wait_ge(*act("values", i - 1))
                    eng.matmul(m.ps[:, 4, :], m.latT[:, 2 * P:3 * P], m.wukv, start=True, stop=True).then_inc(pe.sem, pe.one("expanded", i))
                    eng.wait_ge(*vec2("rows", i))
                    if token:
                        for h in range(4):
                            eng.transpose(m.ps[0:QK, 5, h * P:(h + 1) * P], m.qk[:, h * QK:(h + 1) * QK], ident)
                    for h in range(4):
                        mm = eng.transpose(m.ps[0:QK, 6, h * P:(h + 1) * P], m.qk[:, (4 + h) * QK:(5 + h) * QK], ident)
                    mm.then_inc(pe.sem, pe.one("heads_turned", i))

            @block.vector
            def _(eng):
                o = Order(eng, ordered)
                for i in range(STEPS):
                    token = i < TILES
                    if token:
                        z, tab = m.z[:, i, :], 96 * (i - 1)
                        eng.wait_ge(*squares("sum", i))
                        o(eng.tensor_reduce(m.small[:, 2:8], m.sq[:, 0:6 * HD].rearrange("p (h x) -> p h x", h=6), AX.X, ALU.add))
                        eng.tensor_scalar(m.small[:, 0:8], m.small[:, 0:8], EPS, None, ALU.add).then_inc(vec.sem, vec.one("mean", i))
                        eng.wait_ge(*pool("norm", i))
                        if i == 1:
                            eng.wait_ge(stored, 64)
                        g6 = m.gqk.rearrange("p (h x) -> p h x", h=6)
                        o(eng.tensor_tensor(g6, z[:, ZQG:ZQG + 6 * HD].rearrange("p (h x) -> p h x", h=6),
                                            bc(m.small[:, 10:16], 2, HD), ALU.mult))
                        o(eng.tensor_tensor(m.gqk, m.gqk, row(m, "gqa_g"), ALU.mult))
                        if i > 0:
                            rope(o, eng, g6, 32, const(m, "rope", tab, 32), const(m, "rope", tab + 32, 32), (m.rt1, m.rt2))
                        o(eng.scalar_tensor_tensor(m.qn[:, :], z[:, ZQC:ZQC + Q_RANK], m.small[:, 8:9], row(m, "qa_g"), ALU.mult, ALU.mult))
                        eng.scalar_tensor_tensor(m.cn, z[:, ZCKV:ZCKV + KV_RANK], m.small[:, 9:10], row(m, "kva_g"),
                                                 ALU.mult, ALU.mult).then_inc(vec.sem, vec.one("rows", i))
                    eng.wait_ge(*pe("turned", i))
                    if token:
                        eng.tensor_copy(m.qTg[:, :, i * P:(i + 1) * P], m.ps[0:HD, 1, :].rearrange("p (h x) -> p h x", h=4)).then_inc(
                            vec2.sem, vec2.one("gqa_q", i))
                    else:
                        eng.tensor_copy(m.small[:, 0:1], m.neg_half[:, 0:1]).then_inc(vec2.sem, vec2.one("gqa_q", i))
                    eng.tensor_copy(m.kTg[:, :, slot(i) * P:(slot(i) + 1) * P],
                                    m.ps[0:HD, 2, 0:2 * P].rearrange("p (h x) -> p h x", h=2)).then_inc(vec2.sem, vec2.one("gqa_k", i))
                    eng.wait_ge(*pe("expanded", i))
                    if token:
                        o(eng.tensor_copy(m.qk[:, 0:4 * QK], m.ps[:, 3, 0:4 * QK]))
                    k4 = m.qk[:, 4 * QK:8 * QK].rearrange("p (h x) -> p h x", h=4)
                    o(eng.tensor_copy(k4[:, :, 0:NOPE], m.ps[:, 4, :].rearrange("p (h x) -> p h x", h=4)[:, :, 0:NOPE]))
                    kr = m.z[:, i, ZKR:ZKR + ROPE] if token else m.cache_krope
                    eng.tensor_copy(k4[:, :, NOPE:QK], bc(kr, 1, 4)).then_inc(vec2.sem, vec2.one("expanded", i))
                    eng.wait_ge(*act("squares", i))
                    lo = 0 if token else 4
                    n = 8 - lo
                    o(eng.tensor_reduce(m.small[:, 16 + lo:24], m.sq[:, lo * QK:8 * QK].rearrange("p (h x) -> p h x", h=n), AX.X, ALU.add))
                    eng.tensor_scalar(m.small[:, 16 + lo:24], m.small[:, 16 + lo:24], EPS, None, ALU.add).then_inc(vec2.sem, vec2.one("mean", i))
                    eng.wait_ge(*pool2("norm", i))
                    x = m.qk[:, lo * QK:8 * QK].rearrange("p (h x) -> p h x", h=n)
                    o(eng.tensor_tensor(x, x, bc(m.small[:, 24 + lo:32], 2, QK), ALU.mult))
                    ins = eng.tensor_tensor(m.qk[:, lo * QK:8 * QK], m.qk[:, lo * QK:8 * QK], row(m, "qk_g", lo * QK, n * QK), ALU.mult)
                    if token and i > 0:
                        o(ins)
                        rope(o, eng, x[:, :, NOPE:QK], 16, const(m, "rope", tab + 64, 16), const(m, "rope", tab + 80, 16),
                             (m.rt1[:, 0:128], m.rt2[:, 0:128]))
                        ins = eng.tensor_copy(m.small[:, 0:1], m.neg_half[:, 0:1])
                    ins.then_inc(vec2.sem, vec2.one("rows", i))
                    eng.wait_ge(*pe("heads_turned", i))
                    eng.tensor_copy(m.kTm[:, :, slot(i) * P:(slot(i) + 1) * P],
                                    m.ps[0:QK, 6, :].rearrange("p (h x) -> p h x", h=4)).then_inc(vec2.sem, vec2.one("keys_kept", i))
                    eng.wait_ge(*vec2("keys_kept", i))


def stage_attention(nc, m):
    UNITS = [(t, kind, h) for t in range(TILES) for kind in range(2) for h in range(4)]
    N = len(UNITS)

    def keys(t):
        return (0, 1) if t == 0 else (1, TILES)

    def key_v(kind, h, s):
        if kind == 0:
            return m.vm[:, s, h * HD:(h + 1) * HD]
        if s == 1:
            return m.cache_v[:, h // 2 * HD:(h // 2 + 1) * HD]
        return m.z[:, s if s == 0 else s - 1, ZVG + h // 2 * HD:ZVG + (h // 2 + 1) * HD]

    SCALE = (QK ** -0.5, HD ** -0.5)
    with stage(nc) as sem:
        pe = [Marks(sem(f"{n}_pe"), "unit") for n in ("scores", "turned", "attended")]
        most = Marks(sem("max_ready"), "raw", "unit")
        expd = Marks(sem("exp_ready"), "unit")
        kept_a, kept_v = Marks(sem("turned_kept_scalar"), "unit"), Marks(sem("turned_kept_vector"), "unit")
        done = Marks(sem("attention_done"), "inverse", "unit")
        with nc.Block() as block:
            @block.tensor
            def _(eng):
                def scores(u):
                    t, kind, h = UNITS[u]
                    s0, n = keys(t)
                    q = (m.qTm if kind == 0 else m.qTg)[:, h, t * P:(t + 1) * P]
                    k = m.kTm[:, h, :] if kind == 0 else m.kTg[:, h // 2, :]
                    if u >= 2:
                        eng.wait_ge(*expd("unit", u - 2))
                    mm = eng.matmul(m.ps[:, 2 * (u % 2), 0:min(n, 4) * P], q, k[:, s0 * P:(s0 + min(n, 4)) * P], start=True, stop=True)
                    if n > 4:
                        mm = eng.matmul(m.ps[:, 2 * (u % 2) + 1, 0:P], q, k[:, (s0 + 4) * P:(s0 + 5) * P], start=True, stop=True)
                    mm.then_inc(pe[0].sem, pe[0].one("unit", u))

                scores(0)
                for u in range(N):
                    t, kind, h = UNITS[u]
                    s0, n = keys(t)
                    if u + 1 < N:
                        scores(u + 1)
                    eng.wait_ge(*expd("unit", u))
                    if u >= 1:
                        eng.wait_ge(*kept_v("unit", u - 1))
                        eng.wait_ge(*kept_a("unit", u - 1))
                    for j in range(n):
                        mm = eng.transpose(m.ps[:, 4 + j // 4, j % 4 * P:(j % 4 + 1) * P], m.prob[u % 2][:, j * P:(j + 1) * P], const(m, "ident"))
                    mm.then_inc(pe[1].sem, pe[1].one("unit", u))
                    eng.wait_ge(*kept_v("unit", u))
                    eng.wait_ge(*kept_a("unit", u))
                    if u >= 2:
                        eng.wait_ge(*done("unit", u - 2))
                    for j in range(n):
                        mm = eng.matmul(m.ps[:, 6 + u % 2, 0:HD], m.probT[u % 2][:, j * P:(j + 1) * P], key_v(kind, h, s0 + j),
                                        start=(j == 0), stop=(j == n - 1))
                    mm.then_inc(pe[2].sem, pe[2].one("unit", u))

            @block.scalar
            def _(eng):
                for u in range(N):
                    t, kind, h = UNITS[u]
                    n = keys(t)[1]
                    eng.wait_ge(*most("unit", u))
                    if u >= 2:
                        eng.wait_ge(*pe[1]("unit", u - 2))
                        eng.wait_ge(*done("unit", u - 2))
                    scores = m.ps[:, 2 * (u % 2):2 * (u % 2) + 2, :].rearrange("p b n -> p (b n)")[:, 0:n * P]
                    eng.activation(m.prob[u % 2][:, 0:n * P], scores, ACT.Exp, scale=SCALE[kind],
                                   bias=m.small[:, 2 + u % 2:3 + u % 2], accum_out=m.small[:, 4 + u % 2:5 + u % 2]).then_inc(expd.sem, expd.one("unit", u))
                    eng.wait_ge(*pe[1]("unit", u))
                    if u >= 2:
                        eng.wait_ge(*pe[2]("unit", u - 2))
                    if n > 4:
                        eng.activation(m.probT[u % 2][:, 4 * P:5 * P], m.ps[:, 5, 0:P], ACT.Copy).then_inc(kept_a.sem, kept_a.one("unit", u))
                    else:
                        eng.activation(m.small[:, 12:13], m.neg_half[:, 0:1], ACT.Copy).then_inc(kept_a.sem, kept_a.one("unit", u))
                        eng.wait_ge(*kept_a("unit", u))

            @block.vector
            def _(eng):
                def maximum(u):
                    t, kind, h = UNITS[u]
                    n = keys(t)[1]
                    eng.wait_ge(*pe[0]("unit", u))
                    if u >= 2:
                        eng.wait_ge(*expd("unit", u - 2))
                    scores = m.ps[:, 2 * (u % 2):2 * (u % 2) + 2, :].rearrange("p b n -> p (b n)")[:, 0:n * P]
                    eng.tensor_reduce(m.small[:, u % 2:u % 2 + 1], scores, AX.X, ALU.max).then_inc(most.sem, most.one("raw", u))
                    eng.wait_ge(*most("raw", u))
                    eng.tensor_scalar(m.small[:, 2 + u % 2:3 + u % 2], m.small[:, u % 2:u % 2 + 1], -SCALE[kind], None,
                                      ALU.mult).then_inc(most.sem, most.one("unit", u))

                maximum(0)
                for u in range(N):
                    t, kind, h = UNITS[u]
                    n = keys(t)[1]
                    if u + 1 < N:
                        maximum(u + 1)
                    eng.wait_ge(*pe[1]("unit", u))
                    if u >= 2:
                        eng.wait_ge(*pe[2]("unit", u - 2))
                    eng.tensor_copy(m.probT[u % 2][:, 0:min(n, 4) * P], m.ps[:, 4, 0:min(n, 4) * P]).then_inc(kept_v.sem, kept_v.one("unit", u))
                    eng.reciprocal(m.small[:, 6 + u % 2:7 + u % 2], m.small[:, 4 + u % 2:5 + u % 2]).then_inc(done.sem, done.one("inverse", u))
                    eng.wait_ge(*done("inverse", u))
                    eng.wait_ge(*pe[2]("unit", u))
                    at = (1 + kind) * GW + h * HD
                    eng.tensor_scalar(m.o[:, t, at:at + HD], m.ps[:, 6 + u % 2, 0:HD], m.small[:, 6 + u % 2:7 + u % 2], None,
                                      ALU.mult).then_inc(done.sem, done.one("unit", u))


def stage_conv(nc, m):
    with stage(nc) as sem:
        u_ready, shifted, done, ordered = Marks(sem("conv_u"), "tile"), Marks(sem("conv_shifted"), "tile"), Marks(sem("conv_done"), "tile"), sem("conv_order")
        with nc.Block() as block:
            @block.gpsimd
            def _(eng):
                for t in range(TILES):
                    eng.tensor_tensor(m.z[:, t, 0:GW], m.z[:, t, ZC:ZC + GW], m.z[:, t, ZX:ZX + GW], ALU.mult).then_inc(u_ready.sem, u_ready.one("tile", t))

            @block.tensor
            def _(eng):
                eng.wait_ge(*u_ready("tile", TILES - 1))
                for t in range(TILES):
                    if t >= 2:
                        eng.wait_ge(*done("tile", t - 2))
                    first, last = t <= 1, t in (0, TILES - 1)
                    b = 2 * (t % 2)
                    mm = eng.matmul(m.ps[:, b, 0:GW], const(m, "from_prev"), m.z[:, t, 0:GW], start=True, stop=first)
                    if not first:
                        mm = eng.matmul(m.ps[:, b, 0:GW], const(m, "from_prev_tile"), m.z[:, t - 1, 0:GW], start=False, stop=True)
                    mm = eng.matmul(m.ps[:, b + 1, 0:GW], const(m, "from_next"), m.z[:, t, 0:GW], start=True, stop=last)
                    if not last:
                        mm = eng.matmul(m.ps[:, b + 1, 0:GW], const(m, "from_next_tile"), m.z[:, t + 1, 0:GW], start=False, stop=True)
                    mm.then_inc(shifted.sem, shifted.one("tile", t))

            @block.vector
            def _(eng):
                o = Order(eng, ordered)
                for t in range(TILES):
                    b = 2 * (t % 2)
                    y, tmp = m.o[:, t, 3 * GW:4 * GW], m.z[:, t, GW:2 * GW]
                    eng.wait_ge(*shifted("tile", t))
                    o(eng.tensor_tensor(y, m.ps[:, b, 0:GW], row(m, "conv_w", 0, GW), ALU.mult))
                    o(eng.tensor_tensor(tmp, m.z[:, t, 0:GW], row(m, "conv_w", GW, GW), ALU.mult))
                    o(eng.tensor_tensor(y, y, tmp, ALU.add))
                    o(eng.tensor_tensor(tmp, m.ps[:, b + 1, 0:GW], row(m, "conv_w", 2 * GW, GW), ALU.mult))
                    o(eng.tensor_tensor(y, y, tmp, ALU.add))
                    o(eng.tensor_tensor(y, y, row(m, "conv_b"), ALU.add))
                    eng.tensor_tensor(y, y, m.z[:, t, ZB:ZB + GW], ALU.mult).then_inc(done.sem, done.one("tile", t))


def stage_output(nc, m, l):
    with stage(nc) as sem:
        w_loaded = [sem(f"w_out_loaded{b}") for b in range(2)]
        turned = Marks(sem("o_turned"), "chunk")
        kept_v, kept_a = Marks(sem("o_kept_vector"), "chunk"), Marks(sem("o_kept_scalar"), "chunk")
        made, gated, added = Marks(sem("out_made"), "block"), Marks(sem("out_gated"), "block"), Marks(sem("out_added"), "block")
        blocks = [(n, t) for n in range(2) for t in range(TILES)]
        with nc.Block() as block:
            @block.sync
            def _(eng):
                src = at_layer(m.inp["w_out"], l).rearrange("(c p) n -> p c n", p=P)
                for n in range(2):
                    eng.dma_start(m.w[n], src[:, :, n * 512:(n + 1) * 512]).then_inc(w_loaded[n], 16)

            @block.tensor
            def _(eng):
                for c in range(KC):
                    if c >= 2:
                        eng.wait_ge(*kept_v("chunk", c - 2))
                        eng.wait_ge(*kept_a("chunk", c - 2))
                    eng.transpose(m.ps[:, 2 * (c % 2) + 1, 0:P], m.o[:, 0, c * P:(c + 1) * P], const(m, "ident"))
                    for t in range(1, TILES):
                        mm = eng.transpose(m.ps[:, 2 * (c % 2), (t - 1) * P:t * P], m.o[:, t, c * P:(c + 1) * P], const(m, "ident"))
                    mm.then_inc(turned.sem, turned.one("chunk", c))
                eng.wait_ge(*kept_v("chunk", KC - 1))
                eng.wait_ge(*kept_a("chunk", KC - 1))
                for i, (n, t) in enumerate(blocks):
                    if t == 0:
                        eng.wait_ge(w_loaded[n], 16)
                    if i >= 4:
                        eng.wait_ge(*gated("block", i - 4))
                    for c in range(KC):
                        mm = eng.matmul(m.ps[:, 4 + i % 4, :], m.hT[:, c, t * P:(t + 1) * P], m.w[n][:, c, :],
                                        start=(c == 0), stop=(c == KC - 1))
                    mm.then_inc(made.sem, made.one("block", i))

            @block.scalar
            def _(eng):
                for c in range(KC):
                    eng.wait_ge(*turned("chunk", c))
                    eng.activation(m.hT[:, c, 0:P], m.ps[:, 2 * (c % 2) + 1, 0:P], ACT.Copy).then_inc(kept_a.sem, kept_a.one("chunk", c))

            @block.gpsimd
            def _(eng):
                for i, (n, t) in enumerate(blocks):
                    x = m.x[:, t, n * 512:(n + 1) * 512]
                    eng.wait_ge(*gated("block", i))
                    eng.tensor_tensor(x, x, m.z[:, i % 4, 0:512], ALU.add).then_inc(added.sem, added.one("block", i))

            @block.vector
            def _(eng):
                for c in range(KC):
                    eng.wait_ge(*turned("chunk", c))
                    eng.tensor_copy(m.hT[:, c, P:TOK], m.ps[:, 2 * (c % 2), :]).then_inc(kept_v.sem, kept_v.one("chunk", c))
                for i, (n, t) in enumerate(blocks):
                    eng.wait_ge(*made("block", i))
                    if i >= 4:
                        eng.wait_ge(*added("block", i - 4))
                    eng.tensor_tensor(m.z[:, i % 4, 0:512], m.ps[:, 4 + i % 4, :], m.gate[:, 0, min(t, 1), n * 512:(n + 1) * 512],
                                      ALU.mult).then_inc(gated.sem, gated.one("block", i))


def top16(o, eng, values, index, src, scratch):
    o(eng.max(values[:, 0:8], src))
    o(eng.max_index(index[:, 0:8], values[:, 0:8], src))
    o(eng.match_replace(scratch, values[:, 0:8], src, -3e38))
    o(eng.max(values[:, 8:16], scratch))
    o(eng.max_index(index[:, 8:16], values[:, 8:16], scratch))


def stage_route(nc, m, l):
    J = 2 * HEADS
    with stage(nc) as sem:
        loaded = sem("keys_loaded")
        scored, routed = Marks(sem("scores_made"), "tile"), Marks(sem("scores_read"), "tile")
        shifted, expd, ordered = Marks(sem("best_shifted"), "tile"), Marks(sem("best_exp"), "tile"), sem("route_order")
        with nc.Block() as block:
            @block.sync
            def _(eng):
                eng.dma_start(m.keys, at_layer(m.inp["keys"], l)).then_inc(loaded, 16)

            @block.tensor
            def _(eng):
                eng.wait_ge(loaded, 16)
                for t in range(TILES):
                    if t >= 2:
                        eng.wait_ge(*routed("tile", t - 2))
                    for j in range(J):
                        mm = eng.matmul(m.ps[:, 4 * (t % 2) + j // 4, j % 4 * P:(j % 4 + 1) * P], m.qT[:, j, t * P:(t + 1) * P],
                                        m.keys[:, j, :], start=True, stop=True)
                    mm.then_inc(scored.sem, scored.one("tile", t))

            @block.scalar
            def _(eng):
                for t in range(TILES):
                    eng.wait_ge(*shifted("tile", t))
                    eng.activation(m.best, m.best, ACT.Exp).then_inc(expd.sem, expd.one("tile", t))

            @block.vector
            def _(eng):
                o = Order(eng, ordered)
                for t in range(TILES):
                    eng.wait_ge(*scored("tile", t))
                    for j in range(J):
                        src = m.ps[:, 4 * (t % 2) + j // 4, j % 4 * P:(j % 4 + 1) * P]
                        top16(o, eng, m.key_v[:, j, :], m.key_i[:, j, :], src, m.scratch[:, 0:P])
                    eng.tensor_copy(m.key_f[:, :, :], m.key_i[:, :, :]).then_inc(routed.sem, routed.one("tile", t))
                    eng.wait_ge(*routed("tile", t))
                    for h in range(HEADS):
                        o(eng.tensor_tensor(m.cand[:, 0:256].rearrange("p (a b) -> p a b", a=16), bc(m.key_v[:, 2 * h, :], 2, 16),
                                            bc(m.key_v[:, 2 * h + 1, :], 1, 16), ALU.add))
                        top16(o, eng, m.best[:, h, :], m.pos[:, h, :], m.cand[:, 0:256], m.scratch[:, 0:256])
                    for half in range(2):
                        if half == 0:
                            o(eng.tensor_scalar(m.digit_i[:, :, :], m.pos[:, :, :], 4, None, ALU.logical_shift_right))
                        else:
                            o(eng.tensor_scalar(m.digit_i[:, :, :], m.pos[:, :, :], 15, None, ALU.bitwise_and))
                        o(eng.tensor_copy(m.digit_f[:, :, :], m.digit_i[:, :, :]))
                        for h in range(HEADS):
                            onehot = m.cand[:, h * 256:(h + 1) * 256].rearrange("p (k j) -> p k j", k=16)
                            o(eng.tensor_tensor(onehot, bc(m.digit_f[:, h, :], 2, 16), bc(const(m, "sixteen"), 1, 16), ALU.is_equal))
                            o(eng.tensor_tensor(onehot, onehot, bc(m.key_f[:, 2 * h + half, :], 1, 16), ALU.mult))
                        o(eng.tensor_reduce(m.number[:, half, :], m.cand.rearrange("p (k j) -> p k j", j=16), AX.X, ALU.add))
                    o(eng.scalar_tensor_tensor(m.number[:, 0, :], m.number[:, 0, :], float(NKEY), m.number[:, 1, :], ALU.mult, ALU.add))
                    o(eng.tensor_scalar(m.expert[:, t, :], m.number[:, 0, :], row(m, "expert_base"), None, ALU.add))
                    o(eng.tensor_copy(m.number[:, 1, 0:HEADS], m.best[:, :, 0:1].rearrange("p h k -> p (h k)")))
                    eng.tensor_tensor(m.best[:, :, :], m.best[:, :, :], bc(m.number[:, 1, 0:HEADS], 2, 16), ALU.subtract).then_inc(
                        shifted.sem, shifted.one("tile", t))
                    eng.wait_ge(*expd("tile", t))
                    o(eng.tensor_reduce(m.number[:, 0, 0:HEADS], m.best[:, :, :], AX.X, ALU.add))
                    o(eng.reciprocal(m.number[:, 1, 0:HEADS], m.number[:, 0, 0:HEADS]))
                    o(eng.tensor_tensor(m.share[:, t, :].rearrange("p (h k) -> p h k", h=HEADS), m.best[:, :, :],
                                        bc(m.number[:, 1, 0:HEADS], 2, 16), ALU.mult))


def stage_experts(nc, m, l):
    HALF = 8
    base = l * (TILES * 2 * HEADS)
    with stage(nc) as sem:
        staged, requested = sem("indices_staged"), sem("half_bodies_requested")
        used = [sem("ring_half0_used"), sem("ring_half1_used")]
        turned, h_kept = sem("h_turned"), sem("h_tile_kept")
        copied, acts_used = sem("acts_copied"), sem("gelu_order")
        cube_ready, tanh_ready = sem("cube_ready"), sem("tanh_ready")
        weights_ready, h_free = sem("weights_copied"), sem("tile_done")
        sums_kept = sem("sum_kept")
        with nc.Block() as block:
            @block.gpsimd
            def _(eng):
                with eng.Fori(0, TILES) as t:
                    for phase, table in enumerate((m.inp["peer_u"], m.inp["peer_v"])):
                        with eng.Fori(0, HEADS) as g:
                            body = t * (2 * HEADS) + g + phase * HEADS
                            for half in range(2):
                                eng.wait_ge(used[half], body * HALF)
                                eng.tensor_copy(m.stage_i[:, half * HALF:(half + 1) * HALF],
                                                m.expert_flat[:, bass.ds(t * SLOTS + g * TOPK + half * HALF, HALF)]).then_inc(staged, 1)
                                eng.wait_ge(staged, body * 2 + half + 1)
                                eng.sem_inc(requested, 1)
                                for s in range(half * HALF, (half + 1) * HALF):
                                    eng.indirect_dma_start(m.ring[s], None, at_layer_rows(table),
                                                           bass.IndirectOffsetOnAxis(ap=m.stage_i[:, s:s + 1], axis=0)).then_inc(m.row_loaded[s], 16)

            @block.scalar
            def _(eng):
                with eng.Fori(0, TILES) as t:
                    eng.wait_ge(turned, t)
                    eng.activation(m.h_tile, m.hT[:, :, bass.ds(t * P, P)], ACT.Copy).then_inc(h_kept, 1)
                    eng.wait_ge(cube_ready, t + 1)
                    eng.activation(m.cube, m.cube, ACT.Tanh, scale=0.7978845608028654).then_inc(tanh_ready, 1)
                    eng.wait_ge(h_free, t * 2 + 1)
                    eng.activation(m.sum0, m.ps[:, 2:4, :].rearrange("p b n -> p (b n)"), ACT.Copy).then_inc(sums_kept, 1)

            @block.tensor
            def _(eng):
                with eng.Fori(0, TILES) as t:
                    eng.wait_ge(h_kept, t + 1)
                    eng.wait_ge(cube_ready, t)
                    for c in range(KC):
                        mm = eng.transpose(m.ps[:, c // 4, c % 4 * P:(c % 4 + 1) * P], m.h_tile[:, c, :], const(m, "ident"))
                    mm.then_inc(turned, 1)

            @block.vector
            def _(eng):
                h_rows = m.ps[:, 0:2, :].rearrange("p b n -> p (b n)")
                acc = [m.ps[:, 2 + 2 * k:4 + 2 * k, :].rearrange("p b n -> p (b n)") for k in range(2)]
                ORD = 7
                with eng.Fori(0, TILES) as t:
                    with eng.Fori(0, HEADS) as g:
                        body = t * (2 * HEADS) + g
                        eng.wait_ge(turned, t + 1)
                        eng.wait_ge(copied, t * (2 * HEADS) + g)
                        for s in range(TOPK):
                            eng.wait_ge(m.row_loaded[s], (base + body) * 16 + 16)
                            eng.tensor_tensor_reduce(m.ring[s], m.ring[s], h_rows, 1.0, 0.0, ALU.mult, ALU.add,
                                                     m.act16[:, s:s + 1]).then_inc(used[s // HALF], 1)
                        eng.wait_ge(used[0], body * HALF + HALF)
                        eng.wait_ge(used[1], body * HALF + HALF)
                        eng.tensor_copy(m.acts[:, bass.ds(g * TOPK, TOPK)], m.act16[:, :]).then_inc(copied, 1)
                    eng.wait_ge(copied, t * (2 * HEADS) + HEADS)
                    k = t * ORD
                    eng.tensor_tensor(m.cube, m.acts, m.acts, ALU.mult).then_inc(acts_used, 1)
                    eng.wait_ge(acts_used, k + 1)
                    eng.tensor_scalar(m.cube, m.cube, 0.044715, 1.0, ALU.mult, ALU.add).then_inc(acts_used, 1)
                    eng.wait_ge(acts_used, k + 2)
                    eng.tensor_tensor(m.cube, m.cube, m.acts, ALU.mult).then_inc(cube_ready, 1)
                    eng.wait_ge(tanh_ready, t + 1)
                    eng.scalar_tensor_tensor(m.cube, m.cube, 1.0, m.acts, ALU.add, ALU.mult).then_inc(acts_used, 1)
                    eng.wait_ge(acts_used, k + 3)
                    eng.tensor_copy(m.share_t, m.share_flat[:, bass.ds(t * SLOTS, SLOTS)]).then_inc(acts_used, 1)
                    eng.wait_ge(acts_used, k + 4)
                    eng.scalar_tensor_tensor(m.acts, m.cube, 0.5, m.share_t, ALU.mult, ALU.mult).then_inc(acts_used, 1)
                    eng.wait_ge(acts_used, k + 5)
                    eng.memset(acc[0], 0.0).then_inc(acts_used, 1)
                    eng.memset(acc[1], 0.0).then_inc(acts_used, 1)
                    with eng.Fori(0, HEADS) as g:
                        body = t * (2 * HEADS) + g + HEADS
                        eng.wait_ge(acts_used, k + 7)
                        eng.wait_ge(used[0], body * HALF)
                        eng.wait_ge(used[1], body * HALF)
                        eng.tensor_copy(m.act16[:, :], m.acts[:, bass.ds(g * TOPK, TOPK)]).then_inc(copied, 1)
                        eng.wait_ge(copied, body + 1)
                        for s in range(TOPK):
                            eng.wait_ge(m.row_loaded[s], (base + body) * 16 + 16)
                            if s in (HALF, HALF + 1):
                                eng.wait_ge(used[0], body * HALF + s - 1)
                            elif s >= 2:
                                eng.wait_ge(used[s // HALF], body * HALF + s % HALF - 1)
                            eng.scalar_tensor_tensor(acc[s % 2], m.ring[s], m.act16[:, s:s + 1], acc[s % 2], ALU.mult,
                                                     ALU.add).then_inc(used[s // HALF], 1)
                    end = t * (2 * HEADS) + 2 * HEADS
                    eng.wait_ge(used[1], end * HALF)
                    eng.tensor_copy(m.stage_f, m.neg_half[:, 0:1]).then_inc(h_free, 1)
                    eng.wait_ge(sums_kept, t + 1)
                    eng.tensor_tensor(m.o_flat[:, bass.ds(t * D, D)], acc[1], m.sum0, ALU.add).then_inc(h_free, 1)
                    eng.wait_ge(h_free, t * 2 + 2)


def at_layer_rows(table):
    return table.rearrange("l e d -> (l e) d")


def stage_residual(nc, m):
    with stage(nc) as sem:
        ordered = sem("residual_order")
        with nc.Block() as block:
            @block.vector
            def _(eng):
                o = Order(eng, ordered)
                for t in range(TILES):
                    o(eng.tensor_tensor(m.o[:, t, :], m.o[:, t, :], m.gate[:, 1, min(t, 1), :], ALU.mult))
                    o(eng.tensor_tensor(m.x[:, t, :], m.x[:, t, :], m.o[:, t, :], ALU.add))


def stage_finish(nc, m):
    with stage(nc) as sem:
        stored = sem("tokens_stored")
        with nc.Block() as block:
            @block.sync
            def _(eng):
                eng.dma_start(m.out["y_prompt"][0], m.x[:, 0, :]).then_inc(stored, 16)
                eng.dma_start(m.out["y_sample"][0].rearrange("(t p) d -> p t d", p=P), m.x[:, 1:TILES, :]).then_inc(stored, 16)
                eng.wait_ge(stored, 32)


def place(nc, ctx, m):
    def sb(name, shape, dt=F32):
        return ctx.enter_context(nc.sbuf_tensor(name, shape, dt))

    m.x = sb("x", [P, TILES, D])
    m.o = sb("o", [P, TILES, D])
    m.hT = sb("hT", [P, KC, TOK])
    m.z = sb("z", [P, TILES, D_IN])
    m.rows = sb("rows", [P, NROW])
    m.const = sb("const", [P, NCONST])
    m.gate = sb("gate", [P, 2, 2, D])
    m.mod_col = sb("mod_col", [P, 4, 2, KC])
    m.norm_g = sb("norm_g", [P, 2, KC])
    m.cond = sb("cond", [P, KC, 2])
    m.small = sb("small", [P, 32])
    m.neg_half = sb("neg_half", [P, 16])
    wall = sb("w", [P, 2 * KC * 512])
    m.ps = ctx.enter_context(nc.psum_tensor("ps", [P, 8, 512], F32))
    m.w = [wall[:, b * KC * 512:(b + 1) * KC * 512].rearrange("p (c n) -> p c n", c=KC) for b in range(2)]
    m.cond_tanh = wall[:, 0:2 * KC].rearrange("p (c s) -> p c s", c=KC)
    zall = m.z[:, :, :].rearrange("p t n -> p (t n)")
    m.modrow, m.modbias = zall[0:2, 0:6 * D], zall[0:2, 6 * D:12 * D]

    m.state = [sb(f"state{d}", [P, 2, P]) for d in range(2)]
    m.state_in = [sb(f"state_in{d}", [P, 2, P]) for d in range(2)]
    m.gu = sb("gu", [P, GW])
    hall = m.hT[:, :, :].rearrange("p c n -> p (c n)")
    lane = []
    for d, (region, at) in enumerate(((wall, 0), (hall, 0))):
        lane.append(region[:, at:at + 5120])
    over = [wall[:, 5120:5120 + 1536], wall[:, 6656:6656 + 1536]]
    names = ("dec", "ct", "inv", "sg", "rows4", "kT", "qT", "lh", "mg", "invT")
    m.dec, m.ct, m.sg, m.inv, m.kq, m.rq, m.rhs, m.u = [], [], [], [], [], [], [], []
    m.kd, m.bd, m.kT_rw, m.cx, m.qT_rw, m.lh, m.mg, m.invT = [], [], [], [], [], [], [], []
    m.kk, m.tmp, m.kn, m.ends, m.wdT, m.adT = [], [], [], [], [], []
    for d in range(2):
        a, b = lane[d], over[d]
        m.dec.append(a[:, 0:1024].rearrange("p (k n) -> p k n", k=4))
        m.ct.append([a[:, 0:512], a[:, 512:1024]])
        m.sg.append(a[:, 1024:1536])
        m.inv.append(a[:, 1024:1536])
        m.kq.append(a[:, 1536:1792])
        m.rq.append(a[:, 1792:2048])
        m.rhs.append(a[:, 1536:1792])
        m.u.append(a[:, 1792:2048])
        m.kT_rw.append(a[:, 2048:2560])
        m.cx.append(a[:, 2048:2560])
        m.qT_rw.append(a[:, 2560:3072])
        m.lh.append(a[:, 3072:4096])
        m.mg.append(a[:, 4096:5120])
        m.invT.append(b[:, 0:512])
        m.kd.append(b[:, 512:768])
        m.bd.append(b[:, 768:1024])
        m.kk.append(b[:, 1024:1280])
        m.tmp.append(b[:, 1280:1536])
        m.kn.append(sb(f"kn{d}", [P, 8]))
        m.ends.append(sb(f"ends{d}", [P, 4]))
        m.wdT.append(m.o[0:64, d, 512:640])
        m.adT.append(m.o[0:32, d, 640:768])
    m.wu = m.o[0:64, 2, 512:1024].rearrange("r (e n) -> r e n", e=2)
    m.au = m.o[0:32, 3, 512:1024].rearrange("r (e n) -> r e n", e=2)
    m.gdT = m.o[:, 4, 512:640]

    m.qTm = wall[0:QK, 0:2560].rearrange("p (h n) -> p h n", h=4)
    m.kTm = wall[0:QK, 2560:5632].rearrange("p (h n) -> p h n", h=4)
    m.vm = wall[:, 5632:7168].rearrange("p (s n) -> p s n", s=6)
    m.qk = wall[:, 7168:7936]
    m.latT = sb("latT", [P, 384])
    m.qTg = hall[0:HD, 0:2560].rearrange("p (h n) -> p h n", h=4)
    m.kTg = hall[0:HD, 2560:4096].rearrange("p (h n) -> p h n", h=2)
    m.sq = hall[:, 4096:4864]
    m.cache_v = hall[:, 4864:4992]
    m.cn = hall[:, 4992:5120]
    m.wuq0, m.wuq1 = m.o[:, 0, 256:640], m.o[0:64, 0, 640:1024]
    m.wukv, m.qn = m.o[:, 1, 256:768], m.o[:, 1, 768:960]
    m.gqk, m.rt1, m.rt2 = m.o[:, 2, 256:640], m.o[:, 3, 256:448], m.o[:, 3, 448:640]
    m.cache_ckv, m.cache_krope, m.cache_k = m.o[:, 4, 256:384], m.o[:, 4, 384:416], m.o[:, 4, 416:544]
    m.prob = [m.z[:, k, 0:640] for k in range(2)]
    m.probT = [m.z[:, 2 + k, 0:640] for k in range(2)]

    m.qT = zall[:, 0:2 * HEADS * TOK].rearrange("p (j n) -> p j n", j=2 * HEADS)
    m.keys = wall[:, 0:2048].rearrange("p (j n) -> p j n", j=2 * HEADS)
    m.key_v = wall[:, 2048:2304].rearrange("p (j n) -> p j n", j=2 * HEADS)
    m.key_f = wall[:, 2304:2560].rearrange("p (j n) -> p j n", j=2 * HEADS)
    m.scratch = wall[:, 2560:2816]
    m.best = wall[:, 2816:2944].rearrange("p (h n) -> p h n", h=HEADS)
    m.digit_f = wall[:, 2944:3072].rearrange("p (h n) -> p h n", h=HEADS)
    m.number = wall[:, 3072:3328].rearrange("p (h n) -> p h n", h=2)
    m.cand = m.o[:, 0:2, :].rearrange("p t n -> p (t n)")
    ints = sb("ints", [P, 512], U32)
    m.key_i = ints[:, 0:256].rearrange("p (j n) -> p j n", j=2 * HEADS)
    m.pos = ints[:, 256:384].rearrange("p (h n) -> p h n", h=HEADS)
    m.digit_i = ints[:, 384:512].rearrange("p (h n) -> p h n", h=HEADS)
    expert = sb("expert", [P, TILES, SLOTS], U32)
    m.expert, m.expert_flat = expert, expert[:, :, :].rearrange("p t n -> p (t n)")
    m.share = wall[:, 7552:8192].rearrange("p (t n) -> p t n", t=TILES)
    m.share_flat = wall[:, 7552:8192]
    m.ring = [zall[:, s * D:(s + 1) * D] for s in range(13)] + [wall[:, s * D:(s + 1) * D] for s in range(3)]
    m.h_tile = wall[:, 3072:4096].rearrange("p (c n) -> p c n", c=KC)
    m.sum0 = wall[:, 4096:5120]
    m.acts, m.cube, m.share_t = wall[:, 5120:5248], wall[:, 5248:5376], wall[:, 5376:5504]
    m.act16, m.stage_f = wall[:, 5504:5520], wall[:, 5520:5521]
    m.stage_i = ints[:, 0:16]
    m.o_flat = m.o[:, :, :].rearrange("p t n -> p (t n)")
    m.row_loaded = [ctx.enter_context(nc.semaphore(f"row_loaded{s}")) for s in range(TOPK)]


def build(nc, m):
    with ExitStack() as ctx:
        place(nc, ctx, m)
        stage_start(nc, m)
        with nc.Fori(0, DEPTH) as l:
            stage_modulation(nc, m, l)
            stage_norm_project(nc, m, l, 0)
            stage_rwkv(nc, m, l)
            stage_rwkv_output(nc, m)
            stage_attention_inputs(nc, m, l)
            stage_attention(nc, m)
            stage_conv(nc, m)
            stage_output(nc, m, l)
            stage_norm_project(nc, m, l, 1)
            stage_route(nc, m, l)
            stage_experts(nc, m, l)
            stage_residual(nc, m)
        stage_finish(nc, m)


IN = ["x_prompt", "x_sample", "cache_mla_ckv", "cache_mla_krope", "cache_gqa_k", "cache_gqa_v",
      "b_mod", "w_mod", "w_in", "w_out", "rw_wu", "rw_au", "rw_gu", "mla_wuq", "mla_wukv", "peer_wq",
      "peer_u", "peer_v"]


def layout(inputs):
    a = {k: np.ascontiguousarray(np.asarray(inputs[k])) for k in IN}
    g = {k: np.asarray(v) for k, v in inputs.items()}
    cond = np.stack([g["c_ctx"], g["c"][0]], 1)
    a["cond"] = np.ascontiguousarray(cond.reshape(KC, P, 2).transpose(1, 0, 2))
    a["const"] = constants()
    a["norm_g"] = np.ascontiguousarray(np.stack([g["norm1_g"], g["norm2_g"]], 1).reshape(DEPTH, 2, KC, P).transpose(0, 3, 1, 2))
    wa0 = np.concatenate([g["rw_w0"], g["rw_a0"]], 2).reshape(DEPTH, 1024)
    parts = {"rw_kk": g["rw_kk"], "rw_ka": g["rw_ka"], "wa0": wa0, "rw_rk": g["rw_rk"].reshape(DEPTH, GW),
             "rw_gn": g["rw_gn"], "qa_g": g["mla_qa_g"], "kva_g": g["mla_kva_g"],
             "qk_g": np.concatenate([g["mla_qn_g"]] * 4 + [g["mla_kn_g"]] * 4, 1),
             "gqa_g": np.concatenate([g["gqa_qn_g"]] * 4 + [g["gqa_kn_g"]] * 2, 1),
             "conv_w": g["conv_w"].reshape(DEPTH, 768), "conv_b": g["conv_b"],
             "expert_base": NEXP * np.arange(DEPTH, dtype=np.float32)[:, None]}
    a["rows"] = np.concatenate([parts[k] for k, _ in ROW_PARTS], 1)
    s = g["state_rwkv"][0].reshape(DEPTH, 2, 2, 2, HD, HD)
    a["state"] = np.ascontiguousarray(s.transpose(0, 1, 3, 5, 2, 4))
    keys = np.stack([g["peer_k1"], g["peer_k2"]], 2).reshape(DEPTH, 2 * HEADS, NKEY, P)
    a["keys"] = np.ascontiguousarray(keys.transpose(0, 3, 1, 2))
    return a


OUT = [("y_prompt", (1, SEQ, D)), ("y_sample", (1, DEC, D)), ("state", (DEPTH, 2, 2, HD, 2, HD)),
       ("ckv", (1, DEPTH, SEQ, KV_RANK)), ("krope", (1, DEPTH, SEQ, ROPE)),
       ("gqa_k", (1, DEPTH, SEQ, 2, HD)), ("gqa_v", (1, DEPTH, SEQ, 2, HD))]


def declare(nc, arrays):
    m = Memory()
    for name, a in arrays.items():
        m.inp[name] = nc.dram_tensor("in_" + name, a.shape, F32, kind="ExternalInput").ap()
    for name, shape in OUT:
        m.out[name] = nc.dram_tensor("out_" + name, shape, F32, kind="ExternalOutput").ap()
    return m


def kernel(**inputs):
    import concourse.bacc as bacc
    from concourse.bass_utils import run_bass_kernel_spmd

    arrays = layout(inputs)
    nc = bacc.Bacc("TRN2", target_bir_lowering=False, num_devices=1)
    m = declare(nc, arrays)
    build(nc, m)
    r = run_bass_kernel_spmd(nc, [{"in_" + k: v for k, v in arrays.items()}], core_ids=[0]).results[0]
    state = r["out_state"].transpose(0, 1, 4, 2, 5, 3).reshape(1, DEPTH, 2, 4, HD, HD)
    return tuple(state if n == "state" else r["out_" + n] for n, _ in OUT)
```

```python
from contextlib import ExitStack, contextmanager

import numpy as np

import concourse.bass as bass
from concourse import mybir

F32 = mybir.dt.float32
U32 = mybir.dt.uint32
ALU = mybir.AluOpType
ACT = mybir.ActivationFunctionType
AX = mybir.AxisListType

P = 128
DEPTH, D, SEQ, DEC, PAST = 2, 1024, 128, 512, 128
TILES = (SEQ + DEC) // P
TOK = TILES * P
KC = D // P
EPS = 1e-6
GW = 256
HD = 64
D_IN = 2720
DECAY = 0.6065306597
Q_RANK, KV_RANK, ROPE, NOPE = 192, 128, 32, 64
QK = NOPE + ROPE
HEADS, NKEY, TOPK, NEXP = 8, 128, 16, 128 * 128
SLOTS = HEADS * TOPK

ZR, ZK, ZV, ZWD, ZAD, ZGD = 0, 256, 512, 768, 896, 960
ZQC, ZCKV, ZKR, ZQG, ZKG, ZVG = 1088, 1280, 1408, 1440, 1696, 1824
ZX, ZB, ZC = 1952, 2208, 2464

ROW_PARTS = [("rw_kk", 256), ("rw_ka", 256), ("wa0", 1024), ("rw_rk", 256), ("rw_gn", 256),
             ("qa_g", 192), ("kva_g", 128), ("qk_g", 768), ("gqa_g", 384),
             ("conv_w", 768), ("conv_b", 256), ("expert_base", 1)]
ROW, _at = {}, 0
for _name, _n in ROW_PARTS:
    ROW[_name] = (_at, _n)
    _at += _n
NROW = _at

CONST_PARTS = [("ident", 128), ("tri0", 256), ("tri1", 256), ("level0", 7 * 128), ("level1", 7 * 128),
               ("cum0", 128), ("cum1", 128), ("half0", 2), ("half1", 2), ("blocks", 128),
               ("from_prev", 128), ("from_prev_tile", 128), ("from_next", 128), ("from_next_tile", 128),
               ("pick", 256), ("sixteen", 16), ("rope", 4 * 96)]
CONST, _at = {}, 0
for _name, _n in CONST_PARTS:
    CONST[_name] = (_at, _n)
    _at += _n
NCONST = _at


def constants():
    c = np.zeros((P, NCONST), np.float32)

    def put(name, a):
        s, n = CONST[name]
        c[:a.shape[0], s:s + n] = a

    s, t = np.arange(P)[:, None], np.arange(P)[None, :]
    put("ident", (s == t))
    before = [s < t, s > t]
    for d in range(2):
        put(f"tri{d}", np.concatenate([before[d], before[d] | (s == t)], 1))
        levels = []
        for j in range(7):
            w = 2 ** j
            first, second = (s, t) if d == 0 else (t, s)
            levels.append((s // (2 * w) == t // (2 * w)) & (first // w % 2 == 0) & (second // w % 2 == 1))
        put(f"level{d}", np.concatenate(levels, 1))
        early = (s < 64) if d == 0 else (s >= 64)
        put(f"cum{d}", (before[d] | (s == t)).astype(np.float32) - early)
        put(f"half{d}", np.concatenate([early, ~early], 1))
    put("blocks", (s // HD == t // HD))
    put("from_prev", (s == t - 1))
    put("from_prev_tile", (s == P - 1) & (t == 0))
    put("from_next", (s == t + 1))
    put("from_next_tile", (s == 0) & (t == P - 1))
    pick = np.zeros((2, 2, P), np.float32)
    pick[0, 0] = pick[1, 1] = 1
    put("pick", pick.reshape(2, 256))
    put("sixteen", np.tile(np.arange(16), (P, 1)))
    pos = np.arange(DEC)
    row, col = (pos // 64).astype(np.float32), (pos % 64).astype(np.float32)
    parts = []
    for rot in (HD, ROPE):
        nf = rot // 4
        f = (np.float32(10000.0) ** (-np.arange(nf, dtype=np.float32) / np.float32(nf))).astype(np.float32)
        ang = np.concatenate([row[:, None] * f, col[:, None] * f], 1)
        parts += [np.cos(ang), np.sin(ang)]
    put("rope", np.concatenate(parts, 1).reshape(4, P, 96).transpose(1, 0, 2).reshape(P, 384))
    return c


class Marks:

    def __init__(self, sem, *names):
        self.sem, self.names, self.made = sem, names, 0

    def __call__(self, name, step=0):
        return self.sem, step * len(self.names) + self.names.index(name) + 1

    def one(self, name, step=0):
        self.made += 1
        assert self(name, step)[1] == self.made, (name, step, self.made)
        return 1


class Order:

    def __init__(self, eng, sem, base=0):
        self.eng, self.sem, self.base, self.n = eng, sem, base, 0

    def __call__(self, ins):
        self.mark(ins)
        self.after(0)

    def mark(self, ins):
        ins.then_inc(self.sem, 1)
        self.n += 1

    def after(self, lag):
        if self.n - lag > 0 or not isinstance(self.base, int) or self.base > 0:
            self.eng.wait_ge(self.sem, self.base + self.n - lag)


@contextmanager
def stage(nc):
    with ExitStack() as ctx:
        made = []

        def sem(name):
            made.append(ctx.enter_context(nc.semaphore(name)))
            return made[-1]

        yield sem
        nums = [s.num for s in made]
        assert max(nums) - min(nums) + 1 == len(nums)
        nc.all_engine_barrier(sems_to_clear=range(min(nums), max(nums) + 1))


class Memory:

    def __init__(self):
        self.inp, self.out = {}, {}


def at_layer(ap, l):
    x = ap[bass.ds(l, 1)]
    names = "abcd"[:len(ap.shape) - 1]
    left = " ".join(names)
    right = f"(l {names[0]}) " + " ".join(names[1:])
    return x.rearrange(f"l {left} -> {right}")


def row(m, name, a=0, n=None):
    s, full = ROW[name]
    return m.rows[:, s + a:s + a + (full if n is None else n)]


def const(m, name, a=0, n=None, parts=P):
    s, full = CONST[name]
    return m.const[0:parts, s + a:s + a + (full if n is None else n)]


def bc(ap, axis, n):
    x = ap.unsqueeze(axis)
    return x.broadcast_to(tuple(n if i == axis else k for i, k in enumerate(x.shape)))


def stage_start(nc, m):
    with stage(nc) as sem:
        loaded, tanh_ready, ordered = sem("start_loaded"), sem("cond_tanh_ready"), sem("start_order")
        with nc.Block() as block:
            @block.sync
            def _(eng):
                eng.dma_start(m.cond[:, :, :], m.inp["cond"]).then_inc(loaded, 16)
                eng.dma_start(m.const[:, :], m.inp["const"]).then_inc(loaded, 16)
                eng.dma_start(m.x[:, 0, :], m.inp["x_prompt"][0]).then_inc(loaded, 16)
                eng.dma_start(m.x[:, 1:TILES, :],
                              m.inp["x_sample"][0].rearrange("(t p) d -> p t d", p=P)).then_inc(loaded, 16)
                eng.wait_ge(loaded, 64)

            @block.scalar
            def _(eng):
                eng.wait_ge(loaded, 64)
                eng.activation(m.cond_tanh[:, :, :], m.cond[:, :, :], ACT.Tanh, scale=0.5).then_inc(tanh_ready, 1)

            @block.vector
            def _(eng):
                o = Order(eng, ordered)
                eng.wait_ge(loaded, 64)
                o(eng.memset(m.neg_half[:, :], -0.5))
                eng.wait_ge(tanh_ready, 1)
                o(eng.tensor_scalar(m.cond_tanh[:, :, :], m.cond_tanh[:, :, :], 0.5, 0.5, ALU.mult, ALU.add))
                o(eng.tensor_tensor(m.cond[:, :, :], m.cond[:, :, :], m.cond_tanh[:, :, :], ALU.mult))


def stage_modulation(nc, m, l):
    NB = 6 * D // 512
    with stage(nc) as sem:
        loaded = sem("params_loaded")
        w_loaded = [sem(f"w_mod_loaded{b}") for b in range(2)]
        pe = Marks(sem("mod_chunk_made"), "chunk")
        pe_cols = sem("mod_columns_made")
        pe_gate = Marks(sem("gate_rows_made"), "gate")
        row_ready = Marks(sem("mod_row_ready"), "chunk")
        gate_kept = Marks(sem("gate_rows_kept"), "gate")
        ordered = sem("mod_order")
        modrow, bias = m.modrow, m.modbias
        with nc.Block() as block:
            @block.sync
            def _(eng):
                eng.dma_start(m.rows[:, :], m.inp["rows"][bass.ds(l, 1)].rearrange("l n -> (l n)").partition_broadcast(P)).then_inc(loaded, 16)
                eng.dma_start(bias, m.inp["b_mod"][bass.ds(l, 1)].rearrange("l n -> (l n)").partition_broadcast(2)).then_inc(loaded, 16)
                eng.dma_start(m.norm_g[:, :, :], at_layer(m.inp["norm_g"], l)).then_inc(loaded, 16)
                src = at_layer(m.inp["w_mod"], l).rearrange("(c p) n -> p c n", p=P)
                for i in range(NB):
                    if i >= 2:
                        eng.wait_ge(*pe("chunk", i - 2))
                    eng.dma_start(m.w[i % 2], src[:, :, i * 512:(i + 1) * 512]).then_inc(w_loaded[i % 2], 16)
                eng.wait_ge(loaded, 48)

            @block.tensor
            def _(eng):
                for i in range(NB):
                    eng.wait_ge(w_loaded[i % 2], 16 * (i // 2 + 1))
                    if i >= 2:
                        eng.wait_ge(*row_ready("chunk", i - 2))
                    for c in range(KC):
                        mm = eng.matmul(m.ps[0:2, i % 2, :], m.cond[:, c, :], m.w[i % 2][:, c, :],
                                        start=(c == 0), stop=(c == KC - 1))
                    mm.then_inc(pe.sem, pe.one("chunk", i))
                eng.wait_ge(*row_ready("chunk", NB - 1))
                ident2 = const(m, "ident", 0, 2, parts=2)
                for v, part in enumerate((0, 1, 3, 4)):
                    for c in range(KC):
                        k = v * KC + c
                        mm = eng.transpose(m.ps[:, 2, 2 * k:2 * k + 2],
                                           modrow[:, part * D + c * P:part * D + (c + 1) * P], ident2)
                mm.then_inc(pe_cols, 1)
                for k in range(8):
                    g, s, half = k // 4, k // 2 % 2, k % 2
                    if k >= 4:
                        eng.wait_ge(*gate_kept("gate", k - 4))
                    eng.matmul(m.ps[:, 4 + k % 4, :], const(m, "pick", s * P, P, parts=2),
                               modrow[:, (2 + 3 * g) * D + half * 512:(2 + 3 * g) * D + half * 512 + 512],
                               start=True, stop=True).then_inc(pe_gate.sem, pe_gate.one("gate", k))

            @block.vector
            def _(eng):
                o = Order(eng, ordered)
                eng.wait_ge(loaded, 48)
                for i in range(NB):
                    eng.wait_ge(*pe("chunk", i))
                    eng.tensor_tensor(modrow[:, i * 512:(i + 1) * 512], m.ps[0:2, i % 2, :],
                                      bias[:, i * 512:(i + 1) * 512], ALU.add).then_inc(row_ready.sem, row_ready.one("chunk", i))
                eng.wait_ge(pe_cols, 1)
                o(eng.tensor_copy(m.mod_col[:, :, :, :].rearrange("p v s c -> p v c s"),
                                  m.ps[:, 2, 0:8 * KC].rearrange("p (v c s) -> p v c s", v=4, s=2)))
                for n in range(2):
                    for s in range(2):
                        o(eng.scalar_tensor_tensor(m.mod_col[:, 2 * n + 1, s, :], m.mod_col[:, 2 * n + 1, s, :], 1.0,
                                                   m.norm_g[:, n, :], ALU.add, ALU.mult))
                for k in range(8):
                    g, s, half = k // 4, k // 2 % 2, k % 2
                    eng.wait_ge(*pe_gate("gate", k))
                    eng.tensor_copy(m.gate[:, g, s, half * 512:(half + 1) * 512],
                                    m.ps[:, 4 + k % 4, :]).then_inc(gate_kept.sem, gate_kept.one("gate", k))


def stage_norm_project(nc, m, l, which):
    w_dram = m.inp["w_in"] if which == 0 else m.inp["peer_wq"]
    width = D_IN if which == 0 else HEADS * 2 * P
    NB = -(-width // 512)
    XS = m.o
    with stage(nc) as sem:
        w_loaded = [sem(f"w_loaded{b}") for b in range(2)]
        squares = Marks(sem("squares_summed"), "tile")
        mean_ready, rstd_ready = sem("mean_square_ready"), sem("rstd_ready")
        scaled = Marks(sem("tile_scaled"), "tile")
        turned = Marks(sem("chunk_turned"), "chunk")
        h_lat, h_ctx = Marks(sem("h_latent_ready"), "chunk"), Marks(sem("h_context_ready"), "chunk")
        made = Marks(sem("product_made"), "block")
        kept = [Marks(sem("product_kept_by_vector"), "block"), Marks(sem("product_kept_by_scalar"), "block")]
        ordered, keys_loaded = sem("norm_order"), sem("keys_loaded")

        blocks = []
        for n in range(NB):
            cols = min(512, width - n * 512)
            if which == 0:
                blocks += [(n, t, cols) for t in range(TILES)]
            else:
                blocks += [(n, 2 * j + part, (P, DEC)[part]) for j in range(4) for part in range(2)]

        last_of = [max(i for i, b in enumerate(blocks) if b[0] == n) for n in range(NB)]

        def output(i):
            n, k, cols = blocks[i]
            if which == 0:
                return m.z[:, k, n * 512:n * 512 + cols]
            j, part = 4 * n + k // 2, k % 2
            return m.qT[:, j, part * P:part * P + cols]

        with nc.Block() as block:
            @block.sync
            def _(eng):
                src = at_layer(w_dram, l).rearrange("(c p) n -> p c n", p=P)
                for n in range(NB):
                    cols = min(512, width - n * 512)
                    if n >= 2:
                        eng.wait_ge(*made("block", last_of[n - 2]))
                    eng.dma_start(m.w[n % 2][:, :, 0:cols], src[:, :, n * 512:n * 512 + cols]).then_inc(w_loaded[n % 2], 16)

            @block.scalar
            def _(eng):
                for t in range(TILES):
                    eng.activation(XS[:, t, :], m.x[:, t, :], ACT.Square, scale=float(D) ** -0.5,
                                   accum_out=m.small[:, t:t + 1]).then_inc(squares.sem, squares.one("tile", t))
                for c in range(KC):
                    eng.wait_ge(*turned("chunk", c))
                    eng.activation(m.hT[:, c, 0:P], m.ps[:, 2 * (c % 2) + 1, 0:P], ACT.Identity,
                                   scale=m.mod_col[:, 2 * which + 1, 0, c:c + 1],
                                   bias=m.mod_col[:, 2 * which, 0, c:c + 1]).then_inc(h_ctx.sem, h_ctx.one("chunk", c))
                for i in range(1, len(blocks), 2):
                    eng.wait_ge(*made("block", i))
                    eng.activation(output(i), m.ps[:, 4 + i % 4, 0:blocks[i][2]], ACT.Copy).then_inc(
                        kept[1].sem, kept[1].one("block", i // 2))

            @block.gpsimd
            def _(eng):
                eng.wait_ge(mean_ready, 1)
                eng.tensor_tensor(m.small[:, 16:16 + TILES], m.small[:, 8:8 + TILES], m.neg_half[:, 0:TILES],
                                  ALU.pow).then_inc(rstd_ready, 1)

            @block.vector
            def _(eng):
                eng.wait_ge(*squares("tile", TILES - 1))
                eng.tensor_scalar(m.small[:, 8:8 + TILES], m.small[:, 0:TILES], EPS, None, ALU.add).then_inc(mean_ready, 1)
                eng.wait_ge(rstd_ready, 1)
                for t in range(TILES):
                    eng.tensor_scalar(XS[:, t, :], m.x[:, t, :], m.small[:, 16 + t:17 + t], None,
                                      ALU.mult).then_inc(scaled.sem, scaled.one("tile", t))
                for c in range(KC):
                    eng.wait_ge(*turned("chunk", c))
                    eng.tensor_scalar(m.hT[:, c, P:TOK], m.ps[:, 2 * (c % 2), :],
                                      m.mod_col[:, 2 * which + 1, 1, c:c + 1], m.mod_col[:, 2 * which, 1, c:c + 1],
                                      ALU.mult, ALU.add).then_inc(h_lat.sem, h_lat.one("chunk", c))
                for i in range(0, len(blocks), 2):
                    eng.wait_ge(*made("block", i))
                    eng.tensor_copy(output(i), m.ps[:, 4 + i % 4, 0:blocks[i][2]]).then_inc(
                        kept[0].sem, kept[0].one("block", i // 2))

            @block.tensor
            def _(eng):
                eng.wait_ge(*scaled("tile", TILES - 1))
                for c in range(KC):
                    if c >= 2:
                        eng.wait_ge(*h_lat("chunk", c - 2))
                        eng.wait_ge(*h_ctx("chunk", c - 2))
                    eng.transpose(m.ps[:, 2 * (c % 2) + 1, 0:P], XS[:, 0, c * P:(c + 1) * P], const(m, "ident"))
                    for t in range(1, TILES):
                        mm = eng.transpose(m.ps[:, 2 * (c % 2), (t - 1) * P:t * P], XS[:, t, c * P:(c + 1) * P],
                                           const(m, "ident"))
                    mm.then_inc(turned.sem, turned.one("chunk", c))
                eng.wait_ge(*h_lat("chunk", KC - 1))
                eng.wait_ge(*h_ctx("chunk", KC - 1))
                for i, (n, k, cols) in enumerate(blocks):
                    if i == 0 or blocks[i - 1][0] != n:
                        eng.wait_ge(w_loaded[n % 2], 16 * (n // 2 + 1))
                    if i >= 4:
                        eng.wait_ge(*kept[i % 2]("block", (i - 4) // 2))
                    for c in range(KC):
                        if which == 0:
                            mm = eng.matmul(m.ps[:, 4 + i % 4, 0:cols], m.hT[:, c, k * P:(k + 1) * P],
                                            m.w[n % 2][:, c, 0:cols], start=(c == 0), stop=(c == KC - 1))
                        else:
                            j, part = k // 2, k % 2
                            mm = eng.matmul(m.ps[:, 4 + i % 4, 0:cols], m.w[n % 2][:, c, j * P:(j + 1) * P],
                                            m.hT[:, c, part * P:part * P + cols], start=(c == 0), stop=(c == KC - 1))
                    mm.then_inc(made.sem, made.one("block", i))


def stage_rwkv(nc, m, l):
    STEPS = TILES
    LANES = range(2)
    PE_POINTS = (["ranks_turned", "logits", "cumulated", "rows_turned", "products", "c0"]
                 + [f"{x}{j}" for j in range(1, 7) for x in (("cx", "xcx", "xy") if j < 6 else ("cx", "xy"))] + ["rhs", "u", "end"])
    V_POINTS = (["logits_biased", "gates", "exclusive", "factors", "keys_turned", "masked", "c0t", "xy0"]
                + ["state_scaled"] + [f"{x}{j}" for j in range(1, 7) for x in (("inv", "xy") if j < 6 else ("xy",))] + ["y_kept", "state_kept"])
    A_POINTS = (["rank_tanh", "rank_copied", "tanh", "decays_read", "decays", "queries_turned"]
                + [f"cx{j}" for j in range(1, 7)] + ["rhs", "u"])
    G_POINTS = ["norm"] + [f"level{j}" for j in range(1, 7)]

    turns = [(d, n) for n in range(STEPS) for d in LANES]
    PAIRS = list(zip([None] + turns, turns + [None]))

    def tile_of(n, d):
        return n if n == 0 or d == 0 else TILES - n

    with stage(nc) as sem:
        loaded, zeroed = sem("rwkv_weights_loaded"), sem("state_zeroed")
        state_loaded = [sem(f"state{d}_loaded") for d in LANES]
        state_stored = [sem(f"state{d}_stored") for d in LANES]
        pe = [Marks(sem(f"pe{d}"), *PE_POINTS) for d in LANES]
        vec = [Marks(sem(f"vector{d}"), *V_POINTS) for d in LANES]
        act = [Marks(sem(f"scalar{d}"), *A_POINTS) for d in LANES]
        pool = [Marks(sem(f"pool{d}"), *G_POINTS) for d in LANES]
        squares = [Marks(sem(f"squares{d}"), "sum") for d in LANES]
        ordered, act_ordered = sem("rwkv_order"), sem("rwkv_scalar_order")
        ident = const(m, "ident")

        def bank(d, k):
            return m.ps[:, 4 * d + k, :]

        def heads4(ap):
            return ap.rearrange("p (h x) -> p h x", h=4)

        with nc.Block() as block:
            @block.sync
            def _(eng):
                eng.dma_start(m.wu[:, :, :], at_layer(m.inp["rw_wu"], l).rearrange("e r n -> r e n")).then_inc(loaded, 16)
                eng.dma_start(m.au[:, :, :], at_layer(m.inp["rw_au"], l).rearrange("e r n -> r e n")).then_inc(loaded, 16)
                eng.dma_start(m.gu[:, :], at_layer(m.inp["rw_gu"], l)).then_inc(loaded, 16)
                for d in LANES:
                    eng.wait_ge(*vec[d]("state_kept", 0))
                    for par in range(2):
                        eng.dma_start(m.out["state"][bass.ds(l, 1), d, par].rearrange("l k q v -> (l k) q v"),
                                      m.state[d][par * HD:(par + 1) * HD, :, par * HD:(par + 1) * HD]).then_inc(state_stored[d], 16)
                    eng.wait_ge(state_stored[d], 32)
                    for par in range(2):
                        eng.dma_start(m.state[d][par * HD:(par + 1) * HD, :, par * HD:(par + 1) * HD],
                                      m.inp["state"][bass.ds(l, 1), d, par].rearrange("l k q v -> (l k) q v")).then_inc(state_loaded[d], 16)
                for d in LANES:
                    eng.wait_ge(state_loaded[d], 32)
                eng.wait_ge(loaded, 48)

            @block.tensor
            def _(eng):
                def prepare(part, d, n):
                    z = m.z[:, tile_of(n, d), :]
                    if part == 1:
                        if n > 0:
                            eng.wait_ge(*vec[d]("state_kept", n - 1))
                        eng.transpose(bank(d, 0)[0:64, 0:P], z[:, ZWD + 64 * d:ZWD + 64 * d + 64], ident)
                        eng.transpose(bank(d, 0)[0:32, P:2 * P], z[:, ZAD + 32 * d:ZAD + 32 * d + 32],
                                      ident).then_inc(pe[d].sem, pe[d].one("ranks_turned", n))
                    elif part == 2:
                        eng.wait_ge(*act[d]("rank_copied", n))
                        eng.matmul(bank(d, 1)[:, 0:GW], m.wdT[d][:, :], m.wu[:, d, :], start=True, stop=True)
                        eng.matmul(bank(d, 1)[:, GW:2 * GW], m.adT[d][:, :], m.au[:, d, :], start=True,
                                   stop=True).then_inc(pe[d].sem, pe[d].one("logits", n))
                    elif part == 3:
                        eng.wait_ge(*vec[d]("gates", n))
                        eng.matmul(bank(d, 0)[:, 0:GW], const(m, f"cum{d}"), m.sg[d][:, 0:GW], start=True, stop=True)
                        for q in range(2):
                            mm = eng.matmul(bank(d, 0)[:, GW + 2 * q:GW + 2 * q + 2], m.sg[d][:, q * P:(q + 1) * P],
                                            const(m, f"half{d}"), start=True, stop=True)
                        mm.then_inc(pe[d].sem, pe[d].one("cumulated", n))
                    elif part == 5:
                        eng.wait_ge(*vec[d]("factors", n))
                        for q in range(2):
                            for k, a in enumerate((m.kq[d], m.rq[d])):
                                eng.transpose(bank(d, 2)[:, (2 * q + k) * P:(2 * q + k + 1) * P], a[:, q * P:(q + 1) * P], ident)
                            for k, a in enumerate((m.bd[d], m.kd[d])):
                                mm = eng.transpose(bank(d, 3)[:, (2 * q + k) * P:(2 * q + k + 1) * P], a[:, q * P:(q + 1) * P], ident)
                        mm.then_inc(pe[d].sem, pe[d].one("rows_turned", n))
                    elif part == 6:
                        eng.wait_ge(*act[d]("queries_turned", n))
                        eng.wait_ge(*vec[d]("keys_turned", n))
                        for h in range(4):
                            q, base = h // 2, HD * (h % 2)
                            rhs = m.qT_rw[d][base:base + HD, q * 2 * P:(q + 1) * 2 * P]
                            for k in range(2):
                                mm = eng.matmul(bank(d, 2 * k + h % 2)[:, q * 2 * P:(q + 1) * 2 * P],
                                                m.kT_rw[d][base:base + HD, (2 * q + k) * P:(2 * q + k + 1) * P], rhs,
                                                start=True, stop=True)
                        mm.then_inc(pe[d].sem, pe[d].one("products", n))
                    elif part == 7:
                        eng.wait_ge(*vec[d]("c0t", n))
                        for h in range(4):
                            mm = eng.matmul(bank(d, 0)[:, h * P:(h + 1) * P], m.ct[d][0][:, h * P:(h + 1) * P], ident,
                                            start=True, stop=True)
                        mm.then_inc(pe[d].sem, pe[d].one("c0", n))

                def level_cx(j, d, n):
                    eng.wait_ge(*vec[d](f"inv{j - 1}" if j > 1 else "xy0", n))
                    eng.wait_ge(*pool[d](f"level{j}", n))
                    for h in range(4):
                        s = slice(h * P, (h + 1) * P)
                        mm = eng.matmul(bank(d, 1)[:, s], m.ct[d][j % 2][:, s], m.inv[d][:, s], start=True, stop=True)
                    mm.then_inc(pe[d].sem, pe[d].one(f"cx{j}", n))

                def level_xy(j, d, n):
                    eng.wait_ge(*act[d](f"cx{j}", n))
                    eng.wait_ge(*vec[d](f"xy{j - 1}", n))
                    if j < 6:
                        for h in range(4):
                            s = slice(h * P, (h + 1) * P)
                            mm = eng.matmul(bank(d, 2)[:, s], m.invT[d][:, s], m.cx[d][:, s], start=True, stop=True)
                        mm.then_inc(pe[d].sem, pe[d].one(f"xcx{j}", n))
                    for h in range(4):
                        s = slice(h * P, (h + 1) * P)
                        mm = eng.matmul(bank(d, 3)[:, s], m.cx[d][:, s], m.invT[d][:, s], start=True, stop=True)
                    mm.then_inc(pe[d].sem, pe[d].one(f"xy{j}", n))

                def right_side(d, n):
                    v = m.z[:, tile_of(n, d), ZV:ZV + GW]
                    eng.wait_ge(*vec[d]("state_scaled", n))
                    for h in range(4):
                        q = h // 2
                        if h % 2 == 0:
                            eng.matmul(bank(d, 0)[:, q * P:(q + 1) * P], m.qT_rw[d][:, 2 * q * P:(2 * q + 1) * P],
                                       m.state_in[d][:, q, :], start=True, stop=False, skip_group_check=True)
                        mm = eng.matmul(bank(d, 0)[:, h * HD:(h + 1) * HD], m.mg[d][:, 2 * h * P:(2 * h + 1) * P],
                                        v[:, h * HD:(h + 1) * HD], start=False, stop=True, skip_group_check=True)
                    mm.then_inc(pe[d].sem, pe[d].one("rhs", n))

                def solution(d, n):
                    eng.wait_ge(*act[d]("rhs", n))
                    eng.wait_ge(*vec[d]("xy6", n))
                    for h in range(4):
                        mm = eng.matmul(bank(d, 1)[:, h * HD:(h + 1) * HD], m.invT[d][:, h * P:(h + 1) * P],
                                        m.rhs[d][:, h * HD:(h + 1) * HD], start=True, stop=True)
                    mm.then_inc(pe[d].sem, pe[d].one("u", n))

                def outputs(d, n):
                    v = m.z[:, tile_of(n, d), ZV:ZV + GW]
                    eng.wait_ge(*act[d]("u", n))
                    for h in range(4):
                        q, hs = h // 2, slice(h * HD, (h + 1) * HD)
                        if h % 2 == 0:
                            eng.matmul(bank(d, 2)[:, q * P:(q + 1) * P], m.qT_rw[d][:, (2 * q + 1) * P:(2 * q + 2) * P],
                                       m.state_in[d][:, q, :], start=True, stop=False, skip_group_check=True)
                        eng.matmul(bank(d, 2)[:, hs], m.mg[d][:, (2 * h + 1) * P:(2 * h + 2) * P], v[:, hs],
                                   start=False, stop=False, skip_group_check=True)
                        eng.matmul(bank(d, 2)[:, hs], m.lh[d][:, (2 * h + 1) * P:(2 * h + 2) * P], m.u[d][:, hs],
                                   start=False, stop=True, skip_group_check=True)
                    for q in range(2):
                        qs = slice(q * P, (q + 1) * P)
                        eng.matmul(bank(d, 3)[:, qs], ident, m.state_in[d][:, q, :], start=True, stop=False, skip_group_check=True)
                        eng.matmul(bank(d, 3)[:, qs], m.kd[d][:, qs], v[:, qs], start=False, stop=False, skip_group_check=True)
                        mm = eng.matmul(bank(d, 3)[:, qs], m.bd[d][:, qs], m.u[d][:, qs], start=False, stop=True, skip_group_check=True)
                    mm.then_inc(pe[d].sem, pe[d].one("end", n))

                eng.wait_ge(loaded, 48)
                for solved, prepared in PAIRS:
                    for j in range(1, 7):
                        if solved:
                            level_cx(j, *solved)
                        if prepared:
                            prepare(j, *prepared)
                        if solved:
                            level_xy(j, *solved)
                    if solved:
                        right_side(*solved)
                    if prepared:
                        prepare(7, *prepared)
                    if solved:
                        solution(*solved)
                        outputs(*solved)

            @block.scalar
            def _(eng):
                o = Order(eng, act_ordered)

                def prepare(part, d, n):
                    if part == 1:
                        eng.wait_ge(*pe[d]("ranks_turned", n))
                        eng.activation(m.wdT[d][:, :], bank(d, 0)[0:64, 0:P], ACT.Tanh).then_inc(act[d].sem, act[d].one("rank_tanh", n))
                        eng.activation(m.adT[d][:, :], bank(d, 0)[0:32, P:2 * P], ACT.Copy).then_inc(act[d].sem, act[d].one("rank_copied", n))
                    elif part == 2:
                        eng.wait_ge(*vec[d]("logits_biased", n))
                        eng.activation(m.sg[d][:, :], m.sg[d][:, :], ACT.Tanh, scale=0.5).then_inc(act[d].sem, act[d].one("tanh", n))
                    elif part == 3:
                        eng.wait_ge(*pe[d]("cumulated", n))
                        if n > 0:
                            eng.wait_ge(*pe[d]("cx6", n - 1))
                        o(eng.activation(m.dec[d][:, 0, :], bank(d, 0)[:, 0:GW], ACT.Exp, scale=-DECAY))
                        o(eng.activation(m.ends[d][:, :], bank(d, 0)[:, GW:GW + 4], ACT.Exp, scale=-DECAY))
                        eng.activation(m.dec[d][:, 1, :], bank(d, 0)[:, 0:GW], ACT.Exp, scale=DECAY).then_inc(act[d].sem, act[d].one("decays_read", n))
                    elif part == 4:
                        eng.wait_ge(*vec[d]("exclusive", n))
                        eng.activation(m.dec[d][:, 2, :], m.dec[d][:, 3, :], ACT.Exp, scale=-DECAY).then_inc(act[d].sem, act[d].one("decays", n))
                    elif part == 5:
                        eng.wait_ge(*pe[d]("rows_turned", n))
                        eng.activation(m.qT_rw[d][:, :], bank(d, 2), ACT.Copy).then_inc(act[d].sem, act[d].one("queries_turned", n))

                def level_cx(j, d, n):
                    eng.wait_ge(*pe[d](f"cx{j}", n))
                    eng.activation(m.cx[d][:, :], bank(d, 1), ACT.Copy).then_inc(act[d].sem, act[d].one(f"cx{j}", n))

                def solve(d, n):
                    eng.wait_ge(*pe[d]("rhs", n))
                    eng.activation(m.rhs[d][:, :], bank(d, 0)[:, 0:GW], ACT.Copy).then_inc(act[d].sem, act[d].one("rhs", n))
                    eng.wait_ge(*pe[d]("u", n))
                    eng.activation(m.u[d][:, :], bank(d, 1)[:, 0:GW], ACT.Copy).then_inc(act[d].sem, act[d].one("u", n))

                for solved, prepared in PAIRS:
                    for j in range(1, 7):
                        if solved:
                            level_cx(j, *solved)
                        if prepared:
                            prepare(j, *prepared)
                    if solved:
                        solve(*solved)

            @block.gpsimd
            def _(eng):
                def norm(d, n):
                    eng.wait_ge(*squares[d]("sum", n))
                    eng.tensor_tensor(m.kn[d][:, 4:8], m.kn[d][:, 0:4], m.neg_half[:, 0:4], ALU.pow).then_inc(
                        pool[d].sem, pool[d].one("norm", n))

                def level(j, d, n):
                    eng.wait_ge(*vec[d]("masked", n))
                    if j == 2:
                        eng.wait_ge(*vec[d]("xy0", n))
                    if j > 2:
                        eng.wait_ge(*pe[d](f"cx{j - 2}", n))
                    eng.tensor_tensor(heads4(m.ct[d][j % 2][:, :]),
                                      m.lh[d][:, :].rearrange("p (h k x) -> p h k x", h=4, k=2)[:, :, 0, :],
                                      bc(const(m, f"level{d}", j * P, P), 1, 4), ALU.mult).then_inc(
                        pool[d].sem, pool[d].one(f"level{j}", n))

                for solved, prepared in PAIRS:
                    if solved:
                        level(2, *solved)
                    if prepared:
                        norm(*prepared)
                    if solved:
                        for j in range(3, 7):
                            level(j, *solved)
                    if prepared:
                        level(1, *prepared)

            @block.vector
            def _(eng):
                o = Order(eng, ordered)

                def prepare(part, d, n):
                    z = m.z[:, tile_of(n, d), :]
                    a, kraw = m.sg[d][:, GW:2 * GW], z[:, ZK:ZK + GW]
                    tmp, kk = m.tmp[d][:, :], m.kk[d][:, :]
                    if part == 1:
                        o(eng.tensor_tensor(kk, kraw, row(m, "rw_kk"), ALU.mult))
                        o(eng.tensor_tensor(tmp, kk, kk, ALU.mult))
                        o(eng.tensor_reduce(m.kn[d][:, 0:4], heads4(tmp), AX.X, ALU.add))
                        eng.tensor_scalar(m.kn[d][:, 0:4], m.kn[d][:, 0:4], EPS, None, ALU.add).then_inc(squares[d].sem, squares[d].one("sum", n))
                    elif part == 2:
                        eng.wait_ge(*pe[d]("logits", n))
                        eng.tensor_tensor(m.sg[d][:, :], bank(d, 1), row(m, "wa0", 512 * d, 512), ALU.add).then_inc(
                            vec[d].sem, vec[d].one("logits_biased", n))
                    elif part == 3:
                        eng.wait_ge(*act[d]("tanh", n))
                        eng.tensor_scalar(m.sg[d][:, :], m.sg[d][:, :], 0.5, 0.5, ALU.mult, ALU.add).then_inc(vec[d].sem, vec[d].one("gates", n))
                        eng.wait_ge(*vec[d]("gates", n))
                        eng.wait_ge(*pool[d]("norm", n))
                        o(eng.tensor_tensor(heads4(m.kk[d][:, :]), heads4(m.kk[d][:, :]), bc(m.kn[d][:, 4:8], 2, HD), ALU.mult))
                    elif part == 4:
                        eng.wait_ge(*act[d]("decays_read", n))
                        eng.tensor_tensor(m.dec[d][:, 3, :], bank(d, 0)[:, 0:GW], m.sg[d][:, 0:GW], ALU.subtract).then_inc(
                            vec[d].sem, vec[d].one("exclusive", n))
                        o(eng.scalar_tensor_tensor(tmp, a, 1.0, row(m, "rw_ka"), ALU.subtract, ALU.mult))
                        o(eng.scalar_tensor_tensor(tmp, tmp, 1.0, kraw, ALU.add, ALU.mult))
                        o(eng.tensor_tensor(m.kd[d][:, :], tmp, m.dec[d][:, 1, :], ALU.mult))
                        o(eng.tensor_tensor(tmp, kk, a, ALU.mult))
                        o(eng.tensor_tensor(m.rq[d][:, :], z[:, ZR:ZR + GW], m.dec[d][:, 0, :], ALU.mult))
                        o(eng.scalar_tensor_tensor(m.bd[d][:, :], tmp, -1.0, m.dec[d][:, 1, :], ALU.mult, ALU.mult))
                        eng.wait_ge(*act[d]("decays", n))
                        eng.tensor_tensor(m.kq[d][:, :], kk, m.dec[d][:, 2, :], ALU.mult).then_inc(vec[d].sem, vec[d].one("factors", n))
                    elif part == 5:
                        eng.wait_ge(*pe[d]("rows_turned", n))
                        eng.tensor_copy(m.kT_rw[d][:, :], bank(d, 3)).then_inc(vec[d].sem, vec[d].one("keys_turned", n))
                    elif part == 6:
                        eng.wait_ge(*pe[d]("products", n))
                        for k, (bank_k, to) in enumerate(((0, m.lh[d]), (1, m.lh[d]), (2, m.mg[d]), (3, m.mg[d]))):
                            par = k % 2
                            ins = eng.tensor_tensor(to.rearrange("p (q par x) -> p q par x", q=2, par=2)[:, :, par, :],
                                                    bank(d, bank_k).rearrange("p (h x) -> p h x", h=2),
                                                    bc(const(m, f"tri{d}"), 1, 2), ALU.mult)
                            if k < 3:
                                o(ins)
                        ins.then_inc(vec[d].sem, vec[d].one("masked", n))
                        eng.wait_ge(*vec[d]("masked", n))
                        if n > 0:
                            eng.wait_ge(*pe[d]("end", n - 1))
                        eng.tensor_tensor(heads4(m.ct[d][0][:, :]),
                                          m.lh[d][:, :].rearrange("p (h k x) -> p h k x", h=4, k=2)[:, :, 0, :],
                                          bc(const(m, f"level{d}", 0, P), 1, 4), ALU.mult).then_inc(vec[d].sem, vec[d].one("c0t", n))
                    else:
                        eng.wait_ge(*vec[d]("c0t", n))
                        o(eng.tensor_tensor(heads4(m.invT[d][:, :]), heads4(m.ct[d][0][:, :]), bc(ident, 1, 4), ALU.add))
                        eng.wait_ge(*pe[d]("c0", n))
                        eng.tensor_tensor(heads4(m.inv[d][:, :]), heads4(bank(d, 0)), bc(ident, 1, 4), ALU.add).then_inc(
                            vec[d].sem, vec[d].one("xy0", n))
                        if n == 1:
                            eng.wait_ge(state_loaded[d], 32)
                        for q in range(2):
                            ins = eng.tensor_scalar(m.state_in[d][:, q, :], m.state[d][:, q, :], m.ends[d][:, 2 * q:2 * q + 1],
                                                    None, ALU.mult)
                        ins.then_inc(vec[d].sem, vec[d].one("state_scaled", n))

                def level_xy(j, d, n):
                    if j < 6:
                        eng.wait_ge(*pe[d](f"xcx{j}", n))
                        eng.tensor_tensor(m.inv[d][:, :], bank(d, 2), m.inv[d][:, :], ALU.add).then_inc(
                            vec[d].sem, vec[d].one(f"inv{j}", n))
                    eng.wait_ge(*pe[d](f"xy{j}", n))
                    eng.tensor_tensor(m.invT[d][:, :], bank(d, 3), m.invT[d][:, :], ALU.add).then_inc(
                        vec[d].sem, vec[d].one(f"xy{j}", n))

                def keep(d, n):
                    eng.wait_ge(*pe[d]("end", n))
                    eng.tensor_copy(m.o[:, tile_of(n, d), d * GW:(d + 1) * GW], bank(d, 2)[:, 0:GW]).then_inc(vec[d].sem, vec[d].one("y_kept", n))
                    for q in range(2):
                        ins = eng.scalar_tensor_tensor(m.state[d][:, q, :], bank(d, 3)[:, q * P:(q + 1) * P],
                                                       m.ends[d][:, 2 * q + 1:2 * q + 2], const(m, "blocks"), ALU.mult, ALU.mult)
                        if q == 0:
                            o(ins)
                    ins.then_inc(vec[d].sem, vec[d].one("state_kept", n))
                    eng.wait_ge(*vec[d]("state_kept", n))

                for d in LANES:
                    o(eng.memset(m.state[d][:, :, :], 0.0))
                for solved, prepared in PAIRS:
                    for j in range(1, 7):
                        if prepared:
                            prepare(j, *prepared)
                        if solved:
                            level_xy(j, *solved)
                    if prepared:
                        prepare(7, *prepared)
                    if solved:
                        keep(*solved)


def stage_rwkv_output(nc, m):
    with stage(nc) as sem:
        pe = Marks(sem("gate_pe"), "turned", "gated")
        act = Marks(sem("gate_scalar"), "tanh")
        vec = Marks(sem("gate_vector"), "squares", "sigmoid", "done")
        pool = Marks(sem("gate_pool"), "norm")
        ordered = sem("gate_order")

        def heads4(ap):
            return ap.rearrange("p (h x) -> p h x", h=4)

        with nc.Block() as block:
            @block.tensor
            def _(eng):
                for t in range(TILES):
                    if t > 0:
                        eng.wait_ge(*vec("done", t - 1))
                    eng.transpose(m.ps[:, 0, 0:P], m.z[:, t, ZGD:ZGD + P], const(m, "ident")).then_inc(pe.sem, pe.one("turned", t))
                    eng.wait_ge(*vec("sigmoid", t))
                    eng.matmul(m.ps[:, 1, 0:GW], m.gdT[:, :], m.gu[:, :], start=True, stop=True).then_inc(pe.sem, pe.one("gated", t))

            @block.scalar
            def _(eng):
                for t in range(TILES):
                    eng.wait_ge(*pe("turned", t))
                    if t > 0:
                        eng.wait_ge(*pe("gated", t - 1))
                    eng.activation(m.gdT[:, :], m.ps[:, 0, 0:P], ACT.Tanh, scale=0.5).then_inc(act.sem, act.one("tanh", t))

            @block.gpsimd
            def _(eng):
                for t in range(TILES):
                    eng.wait_ge(*vec("squares", t))
                    eng.tensor_tensor(m.kn[0][:, 4:8], m.kn[0][:, 0:4], m.neg_half[:, 0:4], ALU.pow).then_inc(pool.sem, pool.one("norm", t))

            @block.vector
            def _(eng):
                o = Order(eng, ordered)
                for t in range(TILES):
                    z = m.z[:, t, :]
                    y, tmp, bonus = m.kk[0][:, :], m.tmp[0][:, :], m.kk[1][:, :]
                    o(eng.tensor_tensor(y, m.o[:, t, 0:GW], m.o[:, t, GW:2 * GW], ALU.add))
                    o(eng.tensor_tensor(tmp, y, y, ALU.mult))
                    o(eng.tensor_reduce(m.kn[0][:, 0:4], heads4(tmp), AX.X, ALU.add))
                    eng.tensor_scalar(m.kn[0][:, 0:4], m.kn[0][:, 0:4], 1.0 / HD, EPS, ALU.mult, ALU.add).then_inc(vec.sem, vec.one("squares", t))
                    o(eng.tensor_tensor(tmp, z[:, ZR:ZR + GW], z[:, ZK:ZK + GW], ALU.mult))
                    o(eng.tensor_tensor(tmp, tmp, row(m, "rw_rk"), ALU.mult))
                    o(eng.tensor_reduce(m.kn[1][:, 0:4], heads4(tmp), AX.X, ALU.add))
                    o(eng.tensor_tensor(heads4(bonus), heads4(z[:, ZV:ZV + GW]), bc(m.kn[1][:, 0:4], 2, HD), ALU.mult))
                    eng.wait_ge(*act("tanh", t))
                    eng.tensor_scalar(m.gdT[:, :], m.gdT[:, :], 0.5, 0.5, ALU.mult, ALU.add).then_inc(vec.sem, vec.one("sigmoid", t))
                    eng.wait_ge(*pool("norm", t))
                    o(eng.tensor_tensor(heads4(y), heads4(y), bc(m.kn[0][:, 4:8], 2, HD), ALU.mult))
                    o(eng.tensor_tensor(y, y, row(m, "rw_gn"), ALU.mult))
                    o(eng.tensor_tensor(y, y, bonus, ALU.add))
                    eng.wait_ge(*pe("gated", t))
                    eng.tensor_tensor(m.o[:, t, 0:GW], y, m.ps[:, 1, 0:GW], ALU.mult).then_inc(vec.sem, vec.one("done", t))
                    eng.wait_ge(*vec("done", t))


def rope(o, eng, x, half, cos, sin, tmp):
    heads = x.shape[1]
    x1, x2 = x[:, :, 0:half], x[:, :, half:2 * half]
    c, s = bc(cos, 1, heads), bc(sin, 1, heads)
    t1, t2 = (t.rearrange("p (h x) -> p h x", h=heads) for t in tmp)
    o(eng.tensor_tensor(t1, x2, s, ALU.mult))
    o(eng.tensor_tensor(t2, x1, s, ALU.mult))
    o(eng.tensor_tensor(x1, x1, c, ALU.mult))
    o(eng.tensor_tensor(x2, x2, c, ALU.mult))
    o(eng.tensor_tensor(x1, x1, t1, ALU.subtract))
    o(eng.tensor_tensor(x2, x2, t2, ALU.add))


def stage_attention_inputs(nc, m, l):
    STEPS = TILES + 1
    with stage(nc) as sem:
        loaded, stored = sem("attn_loaded"), sem("caches_stored")
        squares = Marks(sem("first_squares"), "sum")
        act = Marks(sem("attn_scalar"), "latents_turned", "values", "squares", "queries_kept")
        vec = Marks(sem("first_mean"), "mean", "rows")
        vec2 = Marks(sem("attn_vector"), "gqa_q", "gqa_k", "expanded", "mean", "rows", "keys_kept")
        pool, pool2 = Marks(sem("first_norm"), "norm"), Marks(sem("second_norm"), "norm")
        pe = Marks(sem("attn_pe"), "turned", "expanded", "heads_turned")
        ordered, act_ordered = sem("attn_order"), sem("attn_scalar_order")
        ident = const(m, "ident")

        def slot(i):
            return {0: 0, TILES: 1}.get(i, i + 1)

        with nc.Block() as block:
            @block.sync
            def _(eng):
                wuq = at_layer(m.inp["mla_wuq"], l)
                eng.dma_start(m.wuq0, wuq[0:P, :]).then_inc(loaded, 16)
                eng.dma_start(m.wuq1, wuq[P:Q_RANK, :]).then_inc(loaded, 16)
                eng.dma_start(m.wukv, at_layer(m.inp["mla_wukv"], l)).then_inc(loaded, 16)
                eng.dma_start(m.cache_ckv, at_layer(m.inp["cache_mla_ckv"][0], l)).then_inc(loaded, 16)
                eng.dma_start(m.cache_krope, at_layer(m.inp["cache_mla_krope"][0], l)).then_inc(loaded, 16)
                eng.dma_start(m.cache_k, at_layer(m.inp["cache_gqa_k"][0], l).rearrange("t h x -> t (h x)")).then_inc(loaded, 16)
                eng.dma_start(m.cache_v, at_layer(m.inp["cache_gqa_v"][0], l).rearrange("t h x -> t (h x)")).then_inc(loaded, 16)
                eng.dma_start(at_layer(m.out["krope"][0], l), m.z[:, 0, ZKR:ZKR + ROPE]).then_inc(stored, 16)
                eng.dma_start(at_layer(m.out["gqa_v"][0], l).rearrange("t h x -> t (h x)"), m.z[:, 0, ZVG:ZVG + 2 * HD]).then_inc(stored, 16)
                eng.wait_ge(*vec("rows", 0))
                eng.dma_start(at_layer(m.out["ckv"][0], l), m.cn).then_inc(stored, 16)
                eng.dma_start(at_layer(m.out["gqa_k"][0], l).rearrange("t h x -> t (h x)"), m.gqk[:, 4 * HD:6 * HD]).then_inc(stored, 16)
                eng.wait_ge(stored, 64)
                eng.wait_ge(loaded, 112)

            @block.scalar
            def _(eng):
                o = Order(eng, act_ordered)

                def first(t):
                    if t > 0:
                        eng.wait_ge(*vec("rows", t - 1))
                        eng.wait_ge(*vec2("mean", t - 1))
                    z = m.z[:, t, :]
                    o(eng.activation(m.sq[:, 0:Q_RANK], z[:, ZQC:ZQC + Q_RANK], ACT.Square, scale=Q_RANK ** -0.5, accum_out=m.small[:, 0:1]))
                    o(eng.activation(m.sq[:, 0:KV_RANK], z[:, ZCKV:ZCKV + KV_RANK], ACT.Square, scale=KV_RANK ** -0.5, accum_out=m.small[:, 1:2]))
                    eng.activation(m.sq[:, 0:6 * HD], z[:, ZQG:ZQG + 6 * HD], ACT.Square, scale=HD ** -0.5).then_inc(squares.sem, squares.one("sum", t))

                for i in range(STEPS):
                    if i < TILES:
                        first(i)
                    eng.wait_ge(*pe("turned", i))
                    lo = 0 if i < TILES else 256
                    eng.activation(m.latT[:, lo:384], m.ps[:, 0, lo:384], ACT.Copy).then_inc(act.sem, act.one("latents_turned", i))
                    eng.wait_ge(*vec2("expanded", i))
                    eng.activation(m.vm[:, slot(i), :].rearrange("p (h x) -> p h x", h=4),
                                   m.ps[:, 4, :].rearrange("p (h x) -> p h x", h=4)[:, :, NOPE:P], ACT.Copy).then_inc(act.sem, act.one("values", i))
                    lo = 0 if i < TILES else 4
                    if i < TILES:
                        eng.wait_ge(*vec("mean", i))
                    eng.activation(m.sq[:, lo * QK:8 * QK], m.qk[:, lo * QK:8 * QK], ACT.Square, scale=QK ** -0.5).then_inc(act.sem, act.one("squares", i))
                    eng.wait_ge(*pe("heads_turned", i))
                    if i < TILES:
                        eng.activation(m.qTm[:, :, i * P:(i + 1) * P], m.ps[0:QK, 5, :].rearrange("p (h x) -> p h x", h=4),
                                       ACT.Copy).then_inc(act.sem, act.one("queries_kept", i))

            @block.gpsimd
            def _(eng):
                for i in range(STEPS):
                    if i < TILES:
                        eng.wait_ge(*vec("mean", i))
                        eng.tensor_tensor(m.small[:, 8:16], m.small[:, 0:8], m.neg_half[:, 0:8], ALU.pow).then_inc(pool.sem, pool.one("norm", i))
                    eng.wait_ge(*vec2("mean", i))
                    lo = 0 if i < TILES else 4
                    eng.tensor_tensor(m.small[:, 24 + lo:32], m.small[:, 16 + lo:24], m.neg_half[:, lo:8], ALU.pow).then_inc(pool2.sem, pool2.one("norm", i))

            @block.tensor
            def _(eng):
                eng.wait_ge(loaded, 112)
                for i in range(STEPS):
                    token = i < TILES
                    if token:
                        eng.wait_ge(*vec("rows", i))
                        eng.transpose(m.ps[:, 0, 0:P], m.qn[:, 0:P], ident)
                        eng.transpose(m.ps[0:64, 0, P:2 * P], m.qn[:, P:Q_RANK], ident)
                        for h in range(4):
                            eng.transpose(m.ps[0:HD, 1, h * P:(h + 1) * P], m.gqk[:, h * HD:(h + 1) * HD], ident)
                    for h in range(2):
                        src = m.gqk[:, (4 + h) * HD:(5 + h) * HD] if token else m.cache_k[:, h * HD:(h + 1) * HD]
                        if i > 0 and h == 0:
                            eng.wait_ge(*vec2("gqa_k", i - 1))
                        eng.transpose(m.ps[0:HD, 2, h * P:(h + 1) * P], src, ident)
                    eng.transpose(m.ps[:, 0, 2 * P:3 * P], m.cn if token else m.cache_ckv, ident).then_inc(pe.sem, pe.one("turned", i))
                    eng.wait_ge(*act("latents_turned", i))
                    if token:
                        eng.matmul(m.ps[:, 3, 0:4 * QK], m.latT[:, 0:P], m.wuq0, start=True, stop=False)
                        eng.matmul(m.ps[:, 3, 0:4 * QK], m.latT[0:64, P:2 * P], m.wuq1, start=False, stop=True)
                    if i > 0:
                        eng.wait_ge(*act("values", i - 1))
                    eng.matmul(m.ps[:, 4, :], m.latT[:, 2 * P:3 * P], m.wukv, start=True, stop=True).then_inc(pe.sem, pe.one("expanded", i))
                    eng.wait_ge(*vec2("rows", i))
                    if token:
                        for h in range(4):
                            eng.transpose(m.ps[0:QK, 5, h * P:(h + 1) * P], m.qk[:, h * QK:(h + 1) * QK], ident)
                    for h in range(4):
                        mm = eng.transpose(m.ps[0:QK, 6, h * P:(h + 1) * P], m.qk[:, (4 + h) * QK:(5 + h) * QK], ident)
                    mm.then_inc(pe.sem, pe.one("heads_turned", i))

            @block.vector
            def _(eng):
                o = Order(eng, ordered)
                for i in range(STEPS):
                    token = i < TILES
                    if token:
                        z, tab = m.z[:, i, :], 96 * (i - 1)
                        eng.wait_ge(*squares("sum", i))
                        o(eng.tensor_reduce(m.small[:, 2:8], m.sq[:, 0:6 * HD].rearrange("p (h x) -> p h x", h=6), AX.X, ALU.add))
                        eng.tensor_scalar(m.small[:, 0:8], m.small[:, 0:8], EPS, None, ALU.add).then_inc(vec.sem, vec.one("mean", i))
                        eng.wait_ge(*pool("norm", i))
                        if i == 1:
                            eng.wait_ge(stored, 64)
                        g6 = m.gqk.rearrange("p (h x) -> p h x", h=6)
                        o(eng.tensor_tensor(g6, z[:, ZQG:ZQG + 6 * HD].rearrange("p (h x) -> p h x", h=6),
                                            bc(m.small[:, 10:16], 2, HD), ALU.mult))
                        o(eng.tensor_tensor(m.gqk, m.gqk, row(m, "gqa_g"), ALU.mult))
                        if i > 0:
                            rope(o, eng, g6, 32, const(m, "rope", tab, 32), const(m, "rope", tab + 32, 32), (m.rt1, m.rt2))
                        o(eng.scalar_tensor_tensor(m.qn[:, :], z[:, ZQC:ZQC + Q_RANK], m.small[:, 8:9], row(m, "qa_g"), ALU.mult, ALU.mult))
                        eng.scalar_tensor_tensor(m.cn, z[:, ZCKV:ZCKV + KV_RANK], m.small[:, 9:10], row(m, "kva_g"),
                                                 ALU.mult, ALU.mult).then_inc(vec.sem, vec.one("rows", i))
                    eng.wait_ge(*pe("turned", i))
                    if token:
                        eng.tensor_copy(m.qTg[:, :, i * P:(i + 1) * P], m.ps[0:HD, 1, :].rearrange("p (h x) -> p h x", h=4)).then_inc(
                            vec2.sem, vec2.one("gqa_q", i))
                    else:
                        eng.tensor_copy(m.small[:, 0:1], m.neg_half[:, 0:1]).then_inc(vec2.sem, vec2.one("gqa_q", i))
                    eng.tensor_copy(m.kTg[:, :, slot(i) * P:(slot(i) + 1) * P],
                                    m.ps[0:HD, 2, 0:2 * P].rearrange("p (h x) -> p h x", h=2)).then_inc(vec2.sem, vec2.one("gqa_k", i))
                    eng.wait_ge(*pe("expanded", i))
                    if token:
                        o(eng.tensor_copy(m.qk[:, 0:4 * QK], m.ps[:, 3, 0:4 * QK]))
                    k4 = m.qk[:, 4 * QK:8 * QK].rearrange("p (h x) -> p h x", h=4)
                    o(eng.tensor_copy(k4[:, :, 0:NOPE], m.ps[:, 4, :].rearrange("p (h x) -> p h x", h=4)[:, :, 0:NOPE]))
                    kr = m.z[:, i, ZKR:ZKR + ROPE] if token else m.cache_krope
                    eng.tensor_copy(k4[:, :, NOPE:QK], bc(kr, 1, 4)).then_inc(vec2.sem, vec2.one("expanded", i))
                    eng.wait_ge(*act("squares", i))
                    lo = 0 if token else 4
                    n = 8 - lo
                    o(eng.tensor_reduce(m.small[:, 16 + lo:24], m.sq[:, lo * QK:8 * QK].rearrange("p (h x) -> p h x", h=n), AX.X, ALU.add))
                    eng.tensor_scalar(m.small[:, 16 + lo:24], m.small[:, 16 + lo:24], EPS, None, ALU.add).then_inc(vec2.sem, vec2.one("mean", i))
                    eng.wait_ge(*pool2("norm", i))
                    x = m.qk[:, lo * QK:8 * QK].rearrange("p (h x) -> p h x", h=n)
                    o(eng.tensor_tensor(x, x, bc(m.small[:, 24 + lo:32], 2, QK), ALU.mult))
                    ins = eng.tensor_tensor(m.qk[:, lo * QK:8 * QK], m.qk[:, lo * QK:8 * QK], row(m, "qk_g", lo * QK, n * QK), ALU.mult)
                    if token and i > 0:
                        o(ins)
                        rope(o, eng, x[:, :, NOPE:QK], 16, const(m, "rope", tab + 64, 16), const(m, "rope", tab + 80, 16),
                             (m.rt1[:, 0:128], m.rt2[:, 0:128]))
                        ins = eng.tensor_copy(m.small[:, 0:1], m.neg_half[:, 0:1])
                    ins.then_inc(vec2.sem, vec2.one("rows", i))
                    eng.wait_ge(*pe("heads_turned", i))
                    eng.tensor_copy(m.kTm[:, :, slot(i) * P:(slot(i) + 1) * P],
                                    m.ps[0:QK, 6, :].rearrange("p (h x) -> p h x", h=4)).then_inc(vec2.sem, vec2.one("keys_kept", i))
                    eng.wait_ge(*vec2("keys_kept", i))


def stage_attention(nc, m):
    UNITS = [(t, kind, h) for t in range(TILES) for kind in range(2) for h in range(4)]
    N = len(UNITS)

    def keys(t):
        return (0, 1) if t == 0 else (1, TILES)

    def key_v(kind, h, s):
        if kind == 0:
            return m.vm[:, s, h * HD:(h + 1) * HD]
        if s == 1:
            return m.cache_v[:, h // 2 * HD:(h // 2 + 1) * HD]
        return m.z[:, s if s == 0 else s - 1, ZVG + h // 2 * HD:ZVG + (h // 2 + 1) * HD]

    SCALE = (QK ** -0.5, HD ** -0.5)
    with stage(nc) as sem:
        pe = [Marks(sem(f"{n}_pe"), "unit") for n in ("scores", "turned", "attended")]
        most = Marks(sem("max_ready"), "raw", "unit")
        expd = Marks(sem("exp_ready"), "unit")
        kept_a, kept_v = Marks(sem("turned_kept_scalar"), "unit"), Marks(sem("turned_kept_vector"), "unit")
        inverse, done = Marks(sem("sum_inverse"), "unit"), Marks(sem("attention_done"), "unit")
        with nc.Block() as block:
            @block.tensor
            def _(eng):
                def scores(u):
                    t, kind, h = UNITS[u]
                    s0, n = keys(t)
                    q = (m.qTm if kind == 0 else m.qTg)[:, h, t * P:(t + 1) * P]
                    k = m.kTm[:, h, :] if kind == 0 else m.kTg[:, h // 2, :]
                    if u >= 2:
                        eng.wait_ge(*expd("unit", u - 2))
                    mm = eng.matmul(m.ps[:, 2 * (u % 2), 0:min(n, 4) * P], q, k[:, s0 * P:(s0 + min(n, 4)) * P], start=True, stop=True)
                    if n > 4:
                        mm = eng.matmul(m.ps[:, 2 * (u % 2) + 1, 0:P], q, k[:, (s0 + 4) * P:(s0 + 5) * P], start=True, stop=True)
                    mm.then_inc(pe[0].sem, pe[0].one("unit", u))

                def attended(u):
                    t, kind, h = UNITS[u]
                    s0, n = keys(t)
                    if u >= 2:
                        eng.wait_ge(*done("unit", u - 2))
                    for j in range(n):
                        mm = eng.matmul(m.ps[:, 6 + u % 2, 0:HD], m.probT[u % 2][:, j * P:(j + 1) * P], key_v(kind, h, s0 + j),
                                        start=(j == 0), stop=(j == n - 1))
                    mm.then_inc(pe[2].sem, pe[2].one("unit", u))

                scores(0)
                for u in range(N):
                    t, kind, h = UNITS[u]
                    s0, n = keys(t)
                    if u + 1 < N:
                        scores(u + 1)
                    eng.wait_ge(*expd("unit", u))
                    if u >= 1:
                        eng.wait_ge(*kept_v("unit", u - 1))
                        eng.wait_ge(*kept_a("unit", u - 1))
                    for j in range(n):
                        mm = eng.transpose(m.ps[:, 4 + j // 4, j % 4 * P:(j % 4 + 1) * P], m.prob[u % 2][:, j * P:(j + 1) * P], const(m, "ident"))
                    mm.then_inc(pe[1].sem, pe[1].one("unit", u))
                    if u > 0:
                        attended(u - 1)
                eng.wait_ge(*kept_v("unit", N - 1))
                eng.wait_ge(*kept_a("unit", N - 1))
                attended(N - 1)

            @block.scalar
            def _(eng):
                for u in range(N):
                    t, kind, h = UNITS[u]
                    n = keys(t)[1]
                    eng.wait_ge(*most("unit", u))
                    if u >= 2:
                        eng.wait_ge(*pe[1]("unit", u - 2))
                        eng.wait_ge(*inverse("unit", u - 2))
                    scores = m.ps[:, 2 * (u % 2):2 * (u % 2) + 2, :].rearrange("p b n -> p (b n)")[:, 0:n * P]
                    eng.activation(m.prob[u % 2][:, 0:n * P], scores, ACT.Exp, scale=SCALE[kind],
                                   bias=m.small[:, 2 + u % 2:3 + u % 2], accum_out=m.small[:, 4 + u % 2:5 + u % 2]).then_inc(expd.sem, expd.one("unit", u))
                    eng.wait_ge(*pe[1]("unit", u))
                    if u >= 2:
                        eng.wait_ge(*pe[2]("unit", u - 2))
                    if n > 4:
                        eng.activation(m.probT[u % 2][:, 4 * P:5 * P], m.ps[:, 5, 0:P], ACT.Copy).then_inc(kept_a.sem, kept_a.one("unit", u))
                    else:
                        eng.activation(m.small[:, 12:13], m.neg_half[:, 0:1], ACT.Copy).then_inc(kept_a.sem, kept_a.one("unit", u))
                        eng.wait_ge(*kept_a("unit", u))

            @block.vector
            def _(eng):
                def maximum(u):
                    t, kind, h = UNITS[u]
                    n = keys(t)[1]
                    eng.wait_ge(*pe[0]("unit", u))
                    if u >= 2:
                        eng.wait_ge(*expd("unit", u - 2))
                    scores = m.ps[:, 2 * (u % 2):2 * (u % 2) + 2, :].rearrange("p b n -> p (b n)")[:, 0:n * P]
                    eng.tensor_reduce(m.small[:, u % 2:u % 2 + 1], scores, AX.X, ALU.max).then_inc(most.sem, most.one("raw", u))
                    eng.wait_ge(*most("raw", u))
                    eng.tensor_scalar(m.small[:, 2 + u % 2:3 + u % 2], m.small[:, u % 2:u % 2 + 1], -SCALE[kind], None,
                                      ALU.mult).then_inc(most.sem, most.one("unit", u))

                def finish(u):
                    t, kind, h = UNITS[u]
                    eng.wait_ge(*inverse("unit", u))
                    eng.wait_ge(*pe[2]("unit", u))
                    at = (1 + kind) * GW + h * HD
                    eng.tensor_scalar(m.o[:, t, at:at + HD], m.ps[:, 6 + u % 2, 0:HD], m.small[:, 6 + u % 2:7 + u % 2], None,
                                      ALU.mult).then_inc(done.sem, done.one("unit", u))

                maximum(0)
                for u in range(N):
                    t, kind, h = UNITS[u]
                    n = keys(t)[1]
                    if u + 1 < N:
                        maximum(u + 1)
                    eng.wait_ge(*pe[1]("unit", u))
                    if u >= 2:
                        eng.wait_ge(*pe[2]("unit", u - 2))
                    eng.tensor_copy(m.probT[u % 2][:, 0:min(n, 4) * P], m.ps[:, 4, 0:min(n, 4) * P]).then_inc(kept_v.sem, kept_v.one("unit", u))
                    if u >= 2:
                        eng.wait_ge(*done("unit", u - 2))
                    eng.reciprocal(m.small[:, 6 + u % 2:7 + u % 2], m.small[:, 4 + u % 2:5 + u % 2]).then_inc(
                        inverse.sem, inverse.one("unit", u))
                    if u > 0:
                        finish(u - 1)
                finish(N - 1)


def stage_conv(nc, m):
    with stage(nc) as sem:
        u_ready, shifted, done, ordered = Marks(sem("conv_u"), "tile"), Marks(sem("conv_shifted"), "tile"), Marks(sem("conv_done"), "tile"), sem("conv_order")
        with nc.Block() as block:
            @block.gpsimd
            def _(eng):
                for t in range(TILES):
                    eng.tensor_tensor(m.z[:, t, 0:GW], m.z[:, t, ZC:ZC + GW], m.z[:, t, ZX:ZX + GW], ALU.mult).then_inc(u_ready.sem, u_ready.one("tile", t))

            @block.tensor
            def _(eng):
                eng.wait_ge(*u_ready("tile", TILES - 1))
                for t in range(TILES):
                    if t >= 2:
                        eng.wait_ge(*done("tile", t - 2))
                    first, last = t <= 1, t in (0, TILES - 1)
                    b = 2 * (t % 2)
                    mm = eng.matmul(m.ps[:, b, 0:GW], const(m, "from_prev"), m.z[:, t, 0:GW], start=True, stop=first)
                    if not first:
                        mm = eng.matmul(m.ps[:, b, 0:GW], const(m, "from_prev_tile"), m.z[:, t - 1, 0:GW], start=False, stop=True)
                    mm = eng.matmul(m.ps[:, b + 1, 0:GW], const(m, "from_next"), m.z[:, t, 0:GW], start=True, stop=last)
                    if not last:
                        mm = eng.matmul(m.ps[:, b + 1, 0:GW], const(m, "from_next_tile"), m.z[:, t + 1, 0:GW], start=False, stop=True)
                    mm.then_inc(shifted.sem, shifted.one("tile", t))

            @block.vector
            def _(eng):
                o = Order(eng, ordered)
                for t in range(TILES):
                    b = 2 * (t % 2)
                    y, tmp = m.o[:, t, 3 * GW:4 * GW], m.z[:, t, GW:2 * GW]
                    eng.wait_ge(*shifted("tile", t))
                    o(eng.tensor_tensor(y, m.ps[:, b, 0:GW], row(m, "conv_w", 0, GW), ALU.mult))
                    o(eng.tensor_tensor(tmp, m.z[:, t, 0:GW], row(m, "conv_w", GW, GW), ALU.mult))
                    o(eng.tensor_tensor(y, y, tmp, ALU.add))
                    o(eng.tensor_tensor(tmp, m.ps[:, b + 1, 0:GW], row(m, "conv_w", 2 * GW, GW), ALU.mult))
                    o(eng.tensor_tensor(y, y, tmp, ALU.add))
                    o(eng.tensor_tensor(y, y, row(m, "conv_b"), ALU.add))
                    eng.tensor_tensor(y, y, m.z[:, t, ZB:ZB + GW], ALU.mult).then_inc(done.sem, done.one("tile", t))


def stage_output(nc, m, l):
    with stage(nc) as sem:
        w_loaded = [sem(f"w_out_loaded{b}") for b in range(2)]
        turned = Marks(sem("o_turned"), "chunk")
        kept_v, kept_a = Marks(sem("o_kept_vector"), "chunk"), Marks(sem("o_kept_scalar"), "chunk")
        made, gated, added = Marks(sem("out_made"), "block"), Marks(sem("out_gated"), "block"), Marks(sem("out_added"), "block")
        blocks = [(n, t) for n in range(2) for t in range(TILES)]
        with nc.Block() as block:
            @block.sync
            def _(eng):
                src = at_layer(m.inp["w_out"], l).rearrange("(c p) n -> p c n", p=P)
                for n in range(2):
                    eng.dma_start(m.w[n], src[:, :, n * 512:(n + 1) * 512]).then_inc(w_loaded[n], 16)

            @block.tensor
            def _(eng):
                for c in range(KC):
                    if c >= 2:
                        eng.wait_ge(*kept_v("chunk", c - 2))
                        eng.wait_ge(*kept_a("chunk", c - 2))
                    eng.transpose(m.ps[:, 2 * (c % 2) + 1, 0:P], m.o[:, 0, c * P:(c + 1) * P], const(m, "ident"))
                    for t in range(1, TILES):
                        mm = eng.transpose(m.ps[:, 2 * (c % 2), (t - 1) * P:t * P], m.o[:, t, c * P:(c + 1) * P], const(m, "ident"))
                    mm.then_inc(turned.sem, turned.one("chunk", c))
                eng.wait_ge(*kept_v("chunk", KC - 1))
                eng.wait_ge(*kept_a("chunk", KC - 1))
                for i, (n, t) in enumerate(blocks):
                    if t == 0:
                        eng.wait_ge(w_loaded[n], 16)
                    if i >= 4:
                        eng.wait_ge(*gated("block", i - 4))
                    for c in range(KC):
                        mm = eng.matmul(m.ps[:, 4 + i % 4, :], m.hT[:, c, t * P:(t + 1) * P], m.w[n][:, c, :],
                                        start=(c == 0), stop=(c == KC - 1))
                    mm.then_inc(made.sem, made.one("block", i))

            @block.scalar
            def _(eng):
                for c in range(KC):
                    eng.wait_ge(*turned("chunk", c))
                    eng.activation(m.hT[:, c, 0:P], m.ps[:, 2 * (c % 2) + 1, 0:P], ACT.Copy).then_inc(kept_a.sem, kept_a.one("chunk", c))

            @block.gpsimd
            def _(eng):
                for i, (n, t) in enumerate(blocks):
                    x = m.x[:, t, n * 512:(n + 1) * 512]
                    eng.wait_ge(*gated("block", i))
                    eng.tensor_tensor(x, x, m.z[:, i % 4, 0:512], ALU.add).then_inc(added.sem, added.one("block", i))

            @block.vector
            def _(eng):
                for c in range(KC):
                    eng.wait_ge(*turned("chunk", c))
                    eng.tensor_copy(m.hT[:, c, P:TOK], m.ps[:, 2 * (c % 2), :]).then_inc(kept_v.sem, kept_v.one("chunk", c))
                for i, (n, t) in enumerate(blocks):
                    eng.wait_ge(*made("block", i))
                    if i >= 4:
                        eng.wait_ge(*added("block", i - 4))
                    eng.tensor_tensor(m.z[:, i % 4, 0:512], m.ps[:, 4 + i % 4, :], m.gate[:, 0, min(t, 1), n * 512:(n + 1) * 512],
                                      ALU.mult).then_inc(gated.sem, gated.one("block", i))


def top16_step(eng, k, values, index, src, scratch):
    if k == 0:
        return eng.max(values[:, 0:8], src)
    if k == 1:
        return eng.max_index(index[:, 0:8], values[:, 0:8], src)
    if k == 2:
        return eng.match_replace(scratch, values[:, 0:8], src, -3e38)
    if k == 3:
        return eng.max(values[:, 8:16], scratch)
    return eng.max_index(index[:, 8:16], values[:, 8:16], scratch)


def rank_keys_step(eng, m, o, g, k):
    for c in range(2):
        o.mark(top16_step(eng, k, m.key_v[:, 2 * g + c, :], m.key_i[:, 2 * g + c, :], m.score_tile[:, 2 * g + c, :],
                          m.scratch[c][:, 0:P]))


HEAD_STEPS = 14


def rank_pairs_step(eng, m, o, h, k):
    for c in range(2):
        g = h + c
        cand, digit_i, digit_f, number = m.cand[c], m.digit_i[:, c, :, :], m.digit_f[:, c, :, :], m.number[:, c, :, :]
        experts = slice(g * TOPK, (g + 1) * TOPK)
        if k == 0:
            ins = eng.tensor_tensor(cand.rearrange("p (a b) -> p a b", a=TOPK), bc(m.key_v[:, 2 * g, :], 2, TOPK),
                                    bc(m.key_v[:, 2 * g + 1, :], 1, TOPK), ALU.add)
        elif k < 6:
            ins = top16_step(eng, k - 1, m.best[:, g, :], m.pos[:, g, :], cand, m.scratch[c])
        elif k == 6:
            ins = eng.tensor_scalar(digit_i[:, 0, :], m.pos[:, g, :], 4, None, ALU.logical_shift_right)
        elif k == 7:
            ins = eng.tensor_scalar(digit_i[:, 1, :], m.pos[:, g, :], 15, None, ALU.bitwise_and)
        elif k == 8:
            ins = eng.tensor_copy(digit_f, digit_i)
        elif k == 9:
            ins = eng.tensor_tensor(m.onehot[c], bc(digit_f, 3, TOPK), bc(bc(const(m, "sixteen"), 1, TOPK), 1, 2), ALU.is_equal)
        elif k == 10:
            ins = eng.tensor_tensor(m.onehot[c], m.onehot[c], bc(m.key_f[:, 2 * g:2 * g + 2, :], 2, TOPK), ALU.mult)
        elif k == 11:
            ins = eng.tensor_reduce(number, m.onehot[c], AX.X, ALU.add)
        elif k == 12:
            ins = eng.scalar_tensor_tensor(number[:, 0, :], number[:, 0, :], float(NKEY), number[:, 1, :], ALU.mult, ALU.add)
        else:
            ins = eng.tensor_scalar(m.expert_next[:, experts], number[:, 0, :], row(m, "expert_base"), None, ALU.add)
        o.mark(ins)


def stage_scores(nc, m, l):
    J = 2 * HEADS
    with stage(nc) as sem:
        loaded = sem("keys_loaded")
        scored = Marks(sem("scores_made"), "tile")
        kept = [Marks(sem("scores_kept_by_scalar"), "tile"), Marks(sem("scores_kept_by_vector"), "tile")]
        stored = [sem(f"scores_stored{b}") for b in range(2)]

        def target(t):
            return m.score_tile if t == 0 else m.score_out[(t - 1) % 2]

        def keep(eng, t):
            eng.wait_ge(*scored("tile", t))
            if t >= 3:
                eng.wait_ge(stored[(t - 1) % 2], 16)
            return target(t).rearrange("p j n -> p (j n)"), m.ps[:, 4 * (t % 2):4 * (t % 2) + 4, :].rearrange("p b n -> p (b n)")

        with nc.Block() as block:
            @block.sync
            def _(eng):
                eng.dma_start(m.keys, at_layer(m.inp["keys"], l)).then_inc(loaded, 16)
                for t in range(1, TILES):
                    eng.wait_ge(*kept[t % 2]("tile", t // 2))
                    eng.dma_start(m.scores[t - 1], target(t)).then_inc(stored[(t - 1) % 2], 16)
                for b in range(2):
                    eng.wait_ge(stored[b], 32)

            @block.tensor
            def _(eng):
                eng.wait_ge(loaded, 16)
                for t in range(TILES):
                    if t >= 2:
                        eng.wait_ge(*kept[t % 2]("tile", t // 2 - 1))
                    for j in range(J):
                        mm = eng.matmul(m.ps[:, 4 * (t % 2) + j // 4, j % 4 * P:(j % 4 + 1) * P], m.qT[:, j, t * P:(t + 1) * P],
                                        m.keys[:, j, :], start=True, stop=True)
                    mm.then_inc(scored.sem, scored.one("tile", t))

            @block.scalar
            def _(eng):
                for t in range(0, TILES, 2):
                    out, src = keep(eng, t)
                    eng.activation(out, src, ACT.Copy).then_inc(kept[0].sem, kept[0].one("tile", t // 2))

            @block.vector
            def _(eng):
                for t in range(1, TILES, 2):
                    out, src = keep(eng, t)
                    eng.tensor_copy(out, src).then_inc(kept[1].sem, kept[1].one("tile", t // 2))


def stage_experts(nc, m, l):
    HALF, HV = TOPK // 2, TOPK // 4
    BODIES = 2 * HEADS
    base = l * (TILES * BODIES)
    PER_TILE = HEADS * (HALF + HV)
    ROUTE = HEADS * 2 * 5 + 1 + HEADS * HEAD_STEPS + 4
    with stage(nc) as sem:
        staged, requested = sem("indices_staged"), sem("half_bodies_requested")
        used = [sem("ring_half0_used_by_vector"), sem("ring_half1_used_by_vector")]
        summed = [sem("ring_half0_used_by_tensor"), sem("ring_half1_used_by_tensor")]
        turned, h_kept = sem("h_turned"), sem("h_tile_kept")
        acts_used = sem("gelu_order")
        cube_ready, tanh_ready = sem("cube_ready"), sem("tanh_ready")
        weights_ready, diags_ready = sem("weights_ready"), sem("weight_diagonals_ready")
        sum_kept, sums_used, gate_turned = sem("tensor_sum_kept"), sem("residual_order"), sem("latent_gate_placed")
        scores_loaded, keys_ranked = sem("next_scores_loaded"), sem("keys_ranked")
        route_steps, route_ready, begun = sem("route_steps"), sem("experts_ready"), sem("pair_steps_begun")
        shifted_ready, exp_ready = sem("best_shifted"), sem("best_exp_ready")
        with nc.Block() as block:
            @block.sync
            def _(eng):
                for t in range(1, TILES):
                    eng.wait_ge(keys_ranked, t)
                    eng.dma_start(m.score_tile, m.scores[t - 1]).then_inc(scores_loaded, 16)

            @block.gpsimd
            def _(eng):
                with eng.Fori(0, TILES) as t:
                    eng.wait_ge(route_ready, t + 1)
                    eng.sem_inc(requested, 1)
                    eng.tensor_copy(m.expert_now, m.expert_next).then_inc(staged, 1)
                    for phase, table in enumerate((m.inp["peer_u"], m.inp["peer_v"])):
                        with eng.Fori(0, HEADS) as g:
                            body = t * BODIES + g + phase * HEADS
                            eng.wait_ge(staged, t * (2 * BODIES + 1) + 1)
                            for half in range(2):
                                if phase == 0:
                                    eng.wait_ge(used[half], t * PER_TILE + g * HALF + 1)
                                    eng.wait_ge(summed[half], t * (HEADS * HV) + 1)
                                else:
                                    eng.wait_ge(used[half], t * PER_TILE + HEADS * HALF + g * HV + 1)
                                    eng.wait_ge(summed[half], t * (HEADS * HV) + g * HV + 1)
                                eng.tensor_copy(m.stage_i[:, half * HALF:(half + 1) * HALF],
                                                m.expert_now[:, bass.ds(g * TOPK + half * HALF, HALF)]).then_inc(staged, 1)
                                eng.wait_ge(staged, body * 2 + t + half + 2)
                                eng.sem_inc(requested, 1)
                                for s in range(half * HALF, (half + 1) * HALF):
                                    eng.indirect_dma_start(m.ring[s], None, at_layer_rows(table),
                                                           bass.IndirectOffsetOnAxis(ap=m.stage_i[:, s:s + 1], axis=0)).then_inc(m.row_loaded[s], 16)

            @block.scalar
            def _(eng):
                def exp_next(t):
                    eng.wait_ge(shifted_ready, t + 1)
                    eng.activation(m.shifted, m.shifted, ACT.Exp).then_inc(exp_ready, 1)

                def tile(t, last):
                    eng.wait_ge(turned, t + 1)
                    eng.activation(m.h_tile, m.hT[:, :, bass.ds(t * P, P)], ACT.Copy).then_inc(h_kept, 1)
                    eng.wait_ge(cube_ready, t + 2)
                    eng.activation(m.cube, m.cube, ACT.Tanh, scale=0.7978845608028654).then_inc(tanh_ready, 1)
                    for g in range(HEADS):
                        if g == 0:
                            eng.wait_ge(weights_ready, t + 1)
                        for s in range(0, TOPK, 2):
                            if g == 0:
                                if s % HALF == 0:
                                    eng.wait_ge(summed[s // HALF], t * (HEADS * HV) + 1)
                            else:
                                eng.wait_ge(summed[s // HALF], t * (HEADS * HV) + (g - 1) * HV + s % HALF // 2 + 2)
                            k = g * TOPK + s
                            eng.activation(m.diag[:, s // 2, :], const(m, "ident"), ACT.Copy, scale=m.weight[:, k:k + 1]).then_inc(
                                diags_ready, 1)
                        if g == HEADS // 2 and not last:
                            exp_next(t + 1)
                    for half in range(2):
                        eng.wait_ge(summed[half], (t + 1) * (HEADS * HV) + 1)
                    eng.wait_ge(sums_used, t * 3 + 1)
                    eng.activation(m.sum, m.ps[:, 4:6, :].rearrange("p b n -> p (b n)"), ACT.Copy).then_inc(sum_kept, 1)
                    eng.wait_ge(sums_used, t * 3 + 3)
                    eng.activation(m.gate[:, 1, 0, :], m.gate[:, 1, 1, :], ACT.Copy).then_inc(gate_turned, 1)

                for counter in (sum_kept, gate_turned):
                    eng.sem_inc(counter, 1)
                exp_next(0)
                with eng.Fori(0, TILES - 1) as t:
                    tile(t, False)
                tile(TILES - 1, True)

            @block.tensor
            def _(eng):
                def tile(t):
                    eng.wait_ge(h_kept, t + 1)
                    eng.wait_ge(cube_ready, t + 1)
                    for c in range(KC):
                        mm = eng.transpose(m.ps[:, c // 4, c % 4 * P:(c % 4 + 1) * P], m.h_tile[:, c, :], const(m, "ident"))
                    mm.then_inc(turned, 1)
                    eng.wait_ge(sum_kept, t + 1)
                    for g in range(HEADS):
                        for s in range(0, TOPK, 2):
                            eng.wait_ge(diags_ready, t * (HEADS * HALF) + g * HALF + s // 2 + 1)
                            eng.wait_ge(m.row_loaded[s], (base + t * BODIES + HEADS + g) * 16 + 16)
                            for n in range(2):
                                mm = eng.matmul(m.ps[:, 4 + n, :], m.diag[:, s // 2, :], m.ring[s][:, n * 512:(n + 1) * 512],
                                                start=(g == 0 and s == 0), stop=(g == HEADS - 1 and s == TOPK - 2))
                            mm.then_inc(summed[s // HALF], 1)

                for counter in (turned, *summed):
                    eng.sem_inc(counter, 1)
                with eng.Fori(0, TILES - 1) as t:
                    tile(t)
                tile(TILES - 1)

            @block.vector
            def _(eng):
                h_rows = m.ps[:, 0:2, :].rearrange("p b n -> p (b n)")
                acc = m.ps[:, 2:4, :].rearrange("p b n -> p (b n)")
                GELU = 5

                def shift_best(o):
                    o.after(0)
                    eng.tensor_tensor(m.shifted, m.best, m.best[:, :, 0:1].broadcast_to((P, HEADS, TOPK)), ALU.subtract).then_inc(
                        shifted_ready, 1)

                def finish_softmax(o, t):
                    eng.wait_ge(exp_ready, t + 1)
                    o.mark(eng.tensor_reduce(m.share_sum[:, 0:HEADS], m.shifted, AX.X, ALU.add))
                    o.after(0)
                    o.mark(eng.reciprocal(m.share_sum[:, HEADS:2 * HEADS], m.share_sum[:, 0:HEADS]))
                    o.after(0)
                    o.mark(eng.tensor_tensor(m.share.rearrange("p (h k) -> p h k", h=HEADS), m.shifted,
                                             bc(m.share_sum[:, HEADS:2 * HEADS], 2, TOPK), ALU.mult))

                def number_keys(o):
                    o.after(0)
                    o.mark(eng.tensor_copy(m.key_f, m.key_i))
                    o.after(0)
                    eng.sem_inc(keys_ranked, 1)

                def route_done(o):
                    o.after(0)
                    eng.sem_inc(route_ready, 1)
                    eng.sem_inc(route_steps, 1)
                    o.n += 1

                def tile(t, last):
                    o = Order(eng, route_steps, (t + 1) * ROUTE)
                    eng.wait_ge(turned, t + 2)
                    if not last:
                        eng.wait_ge(scores_loaded, t * 16 + 16)
                    for g in range(HEADS):
                        for s in range(TOPK):
                            if not last and s < 5:
                                o.after(0)
                            eng.wait_ge(m.row_loaded[s], (base + t * BODIES + g) * 16 + 16)
                            k = g * TOPK + s
                            eng.tensor_tensor_reduce(m.ring[s], m.ring[s], h_rows, 1.0, 0.0, ALU.mult, ALU.add,
                                                     m.acts[:, k:k + 1]).then_inc(used[s // HALF], 1)
                            if not last and s < 5:
                                rank_keys_step(eng, m, o, g, s)
                    if not last:
                        number_keys(o)
                    for half in range(2):
                        eng.wait_ge(used[half], t * PER_TILE + HEADS * HALF + 1)
                    k = t * GELU
                    eng.tensor_tensor(m.cube, m.acts, m.acts, ALU.mult).then_inc(acts_used, 1)
                    eng.wait_ge(acts_used, k + 1)
                    eng.tensor_scalar(m.cube, m.cube, 0.044715, 1.0, ALU.mult, ALU.add).then_inc(acts_used, 1)
                    eng.wait_ge(acts_used, k + 2)
                    eng.tensor_tensor(m.cube, m.cube, m.acts, ALU.mult).then_inc(cube_ready, 1)
                    eng.scalar_tensor_tensor(m.acts, m.acts, 0.5, m.share, ALU.mult, ALU.mult).then_inc(acts_used, 1)
                    eng.memset(acc, 0.0).then_inc(acts_used, 1)
                    eng.wait_ge(acts_used, k + 4)
                    eng.wait_ge(tanh_ready, t + 1)
                    eng.scalar_tensor_tensor(m.weight, m.cube, 1.0, m.acts, ALU.add, ALU.mult).then_inc(weights_ready, 1)
                    eng.sem_inc(acts_used, 1)
                    eng.wait_ge(weights_ready, t + 1)
                    for g in range(HEADS):
                        for s in range(TOPK):
                            if s % 2 == 1:
                                done = t * PER_TILE + HEADS * HALF + g * HV
                                if s == 1:
                                    eng.wait_ge(used[1], done + 1)
                                else:
                                    eng.wait_ge(used[(s - 2) // HALF], done + (s - 2) % HALF // 2 + 2)
                                eng.wait_ge(m.row_loaded[s], (base + t * BODIES + HEADS + g) * 16 + 16)
                                k = g * TOPK + s
                                eng.scalar_tensor_tensor(acc, m.ring[s], m.weight[:, k:k + 1], acc, ALU.mult,
                                                         ALU.add).then_inc(used[s // HALF], 1)
                            if not last and g < HEADS // 2 and s < HEAD_STEPS:
                                o.after(0)
                                eng.sem_inc(begun, 1)
                                rank_pairs_step(eng, m, o, 2 * g, s)
                        if not last and g == HEADS // 2 - 1:
                            shift_best(o)
                            route_done(o)
                        if not last and g == HEADS // 2:
                            finish_softmax(o, t + 1)
                            o.after(0)
                            assert o.n == ROUTE
                    eng.wait_ge(used[1], (t + 1) * PER_TILE + 1)
                    eng.wait_ge(sum_kept, t + 2)
                    eng.tensor_tensor(m.sum, m.sum, acc, ALU.add).then_inc(sums_used, 1)
                    eng.wait_ge(sums_used, t * 3 + 2)
                    eng.wait_ge(gate_turned, t + 1)
                    eng.tensor_tensor(m.sum, m.sum, m.gate[:, 1, 0, :], ALU.mult).then_inc(sums_used, 1)
                    eng.wait_ge(sums_used, t * 3 + 3)
                    x = m.x_flat[:, bass.ds(t * D, D)]
                    eng.tensor_tensor(x, x, m.sum, ALU.add).then_inc(sums_used, 1)

                for counter in (cube_ready, sums_used, *used):
                    eng.sem_inc(counter, 1)
                o = Order(eng, route_steps, 0)
                for g in range(HEADS):
                    for k in range(5):
                        o.after(0)
                        rank_keys_step(eng, m, o, g, k)
                number_keys(o)
                for h in range(0, HEADS, 2):
                    for k in range(HEAD_STEPS):
                        o.after(0)
                        rank_pairs_step(eng, m, o, h, k)
                shift_best(o)
                route_done(o)
                finish_softmax(o, 0)
                o.after(0)
                assert o.n == ROUTE
                with eng.Fori(0, TILES - 1) as t:
                    tile(t, False)
                tile(TILES - 1, True)


def at_layer_rows(table):
    return table.rearrange("l e d -> (l e) d")


def stage_finish(nc, m):
    with stage(nc) as sem:
        stored = sem("tokens_stored")
        with nc.Block() as block:
            @block.sync
            def _(eng):
                eng.dma_start(m.out["y_prompt"][0], m.x[:, 0, :]).then_inc(stored, 16)
                eng.dma_start(m.out["y_sample"][0].rearrange("(t p) d -> p t d", p=P), m.x[:, 1:TILES, :]).then_inc(stored, 16)
                eng.wait_ge(stored, 32)


def place(nc, ctx, m):
    def sb(name, shape, dt=F32):
        return ctx.enter_context(nc.sbuf_tensor(name, shape, dt))

    m.x = sb("x", [P, TILES, D])
    m.o = sb("o", [P, TILES, D])
    m.hT = sb("hT", [P, KC, TOK])
    m.z = sb("z", [P, TILES, D_IN])
    m.rows = sb("rows", [P, NROW])
    m.const = sb("const", [P, NCONST])
    m.gate = sb("gate", [P, 2, 2, D])
    m.mod_col = sb("mod_col", [P, 4, 2, KC])
    m.norm_g = sb("norm_g", [P, 2, KC])
    m.cond = sb("cond", [P, KC, 2])
    m.small = sb("small", [P, 32])
    m.neg_half = sb("neg_half", [P, 16])
    wall = sb("w", [P, 2 * KC * 512])
    m.ps = ctx.enter_context(nc.psum_tensor("ps", [P, 8, 512], F32))
    m.w = [wall[:, b * KC * 512:(b + 1) * KC * 512].rearrange("p (c n) -> p c n", c=KC) for b in range(2)]
    m.cond_tanh = wall[:, 0:2 * KC].rearrange("p (c s) -> p c s", c=KC)
    zall = m.z[:, :, :].rearrange("p t n -> p (t n)")
    m.modrow, m.modbias = zall[0:2, 0:6 * D], zall[0:2, 6 * D:12 * D]

    m.state = [sb(f"state{d}", [P, 2, P]) for d in range(2)]
    m.state_in = [sb(f"state_in{d}", [P, 2, P]) for d in range(2)]
    m.gu = sb("gu", [P, GW])
    hall = m.hT[:, :, :].rearrange("p c n -> p (c n)")
    lane = []
    for d, (region, at) in enumerate(((wall, 0), (hall, 0))):
        lane.append(region[:, at:at + 5120])
    over = [wall[:, 5120:5120 + 1536], wall[:, 6656:6656 + 1536]]
    names = ("dec", "ct", "inv", "sg", "rows4", "kT", "qT", "lh", "mg", "invT")
    m.dec, m.ct, m.sg, m.inv, m.kq, m.rq, m.rhs, m.u = [], [], [], [], [], [], [], []
    m.kd, m.bd, m.kT_rw, m.cx, m.qT_rw, m.lh, m.mg, m.invT = [], [], [], [], [], [], [], []
    m.kk, m.tmp, m.kn, m.ends, m.wdT, m.adT = [], [], [], [], [], []
    for d in range(2):
        a, b = lane[d], over[d]
        m.dec.append(a[:, 0:1024].rearrange("p (k n) -> p k n", k=4))
        m.ct.append([a[:, 0:512], a[:, 512:1024]])
        m.sg.append(a[:, 1024:1536])
        m.inv.append(a[:, 1024:1536])
        m.kq.append(a[:, 1536:1792])
        m.rq.append(a[:, 1792:2048])
        m.rhs.append(a[:, 1536:1792])
        m.u.append(a[:, 1792:2048])
        m.kT_rw.append(a[:, 2048:2560])
        m.cx.append(a[:, 2048:2560])
        m.qT_rw.append(a[:, 2560:3072])
        m.lh.append(a[:, 3072:4096])
        m.mg.append(a[:, 4096:5120])
        m.invT.append(b[:, 0:512])
        m.kd.append(b[:, 512:768])
        m.bd.append(b[:, 768:1024])
        m.kk.append(b[:, 1024:1280])
        m.tmp.append(b[:, 1280:1536])
        m.kn.append(sb(f"kn{d}", [P, 8]))
        m.ends.append(sb(f"ends{d}", [P, 4]))
        m.wdT.append(m.o[0:64, d, 512:640])
        m.adT.append(m.o[0:32, d, 640:768])
    m.wu = m.o[0:64, 2, 512:1024].rearrange("r (e n) -> r e n", e=2)
    m.au = m.o[0:32, 3, 512:1024].rearrange("r (e n) -> r e n", e=2)
    m.gdT = m.o[:, 4, 512:640]

    m.qTm = wall[0:QK, 0:2560].rearrange("p (h n) -> p h n", h=4)
    m.kTm = wall[0:QK, 2560:5632].rearrange("p (h n) -> p h n", h=4)
    m.vm = wall[:, 5632:7168].rearrange("p (s n) -> p s n", s=6)
    m.qk = wall[:, 7168:7936]
    m.latT = sb("latT", [P, 384])
    m.qTg = hall[0:HD, 0:2560].rearrange("p (h n) -> p h n", h=4)
    m.kTg = hall[0:HD, 2560:4096].rearrange("p (h n) -> p h n", h=2)
    m.sq = hall[:, 4096:4864]
    m.cache_v = hall[:, 4864:4992]
    m.cn = hall[:, 4992:5120]
    m.wuq0, m.wuq1 = m.o[:, 0, 256:640], m.o[0:64, 0, 640:1024]
    m.wukv, m.qn = m.o[:, 1, 256:768], m.o[:, 1, 768:960]
    m.gqk, m.rt1, m.rt2 = m.o[:, 2, 256:640], m.o[:, 3, 256:448], m.o[:, 3, 448:640]
    m.cache_ckv, m.cache_krope, m.cache_k = m.o[:, 4, 256:384], m.o[:, 4, 384:416], m.o[:, 4, 416:544]
    m.prob = [m.z[:, k, 0:640] for k in range(2)]
    m.probT = [m.z[:, 2 + k, 0:640] for k in range(2)]

    m.qT = zall[:, 0:2 * HEADS * TOK].rearrange("p (j n) -> p j n", j=2 * HEADS)
    m.keys = wall[:, 0:2048].rearrange("p (j n) -> p j n", j=2 * HEADS)
    oall = m.o[:, :, :].rearrange("p t n -> p (t n)")
    m.score_tile = wall[:, 5120:7168].rearrange("p (j n) -> p j n", j=2 * HEADS)
    m.score_out = [oall[:, b * 2048:(b + 1) * 2048].rearrange("p (j n) -> p j n", j=2 * HEADS) for b in range(2)]
    m.key_v = oall[:, 0:256].rearrange("p (j n) -> p j n", j=2 * HEADS)
    m.key_f = oall[:, 256:512].rearrange("p (j n) -> p j n", j=2 * HEADS)
    m.scratch = [oall[:, 512 + 256 * c:768 + 256 * c] for c in range(2)]
    m.cand = [oall[:, 1024 + 256 * c:1280 + 256 * c] for c in range(2)]
    m.onehot = [oall[:, 1536 + 512 * c:2048 + 512 * c].rearrange("p (d k j) -> p d k j", d=2, k=TOPK) for c in range(2)]
    m.best = oall[:, 2560:2688].rearrange("p (h n) -> p h n", h=HEADS)
    m.shifted = oall[:, 2688:2816].rearrange("p (h n) -> p h n", h=HEADS)
    m.digit_f = oall[:, 2816:2880].rearrange("p (c d k) -> p c d k", c=2, d=2)
    m.number = oall[:, 2880:2944].rearrange("p (c d k) -> p c d k", c=2, d=2)
    m.share_sum = oall[:, 2944:2960]
    ints = sb("ints", [P, 512], U32)
    m.key_i = ints[:, 0:256].rearrange("p (j n) -> p j n", j=2 * HEADS)
    m.pos = ints[:, 256:384].rearrange("p (h n) -> p h n", h=HEADS)
    m.digit_i = ints[:, 384:448].rearrange("p (c d k) -> p c d k", c=2, d=2)
    m.stage_i = ints[:, 448:464]
    experts = sb("experts", [P, 2, SLOTS], U32)
    m.expert_next, m.expert_now = experts[:, 0, :], experts[:, 1, :]
    m.diag = oall[:, 3072:4096].rearrange("p (s n) -> p s n", s=TOPK // 2)
    m.sum = oall[:, 4096:5120]
    m.ring = [zall[:, s * D:(s + 1) * D] for s in range(13)] + [wall[:, s * D:(s + 1) * D] for s in range(3)]
    m.h_tile = wall[:, 3072:4096].rearrange("p (c n) -> p c n", c=KC)
    m.acts, m.cube, m.weight, m.share = (wall[:, 4096 + SLOTS * k:4096 + SLOTS * (k + 1)] for k in range(4))
    m.x_flat = m.x[:, :, :].rearrange("p t n -> p (t n)")
    m.row_loaded = [ctx.enter_context(nc.semaphore(f"row_loaded{s}")) for s in range(TOPK)]


def build(nc, m):
    with ExitStack() as ctx:
        place(nc, ctx, m)
        stage_start(nc, m)
        with nc.Fori(0, DEPTH) as l:
            stage_modulation(nc, m, l)
            stage_norm_project(nc, m, l, 0)
            stage_rwkv(nc, m, l)
            stage_rwkv_output(nc, m)
            stage_attention_inputs(nc, m, l)
            stage_attention(nc, m)
            stage_conv(nc, m)
            stage_output(nc, m, l)
            stage_norm_project(nc, m, l, 1)
            stage_scores(nc, m, l)
            stage_experts(nc, m, l)
        stage_finish(nc, m)


IN = ["x_prompt", "x_sample", "cache_mla_ckv", "cache_mla_krope", "cache_gqa_k", "cache_gqa_v",
      "b_mod", "w_mod", "w_in", "w_out", "rw_wu", "rw_au", "rw_gu", "mla_wuq", "mla_wukv", "peer_wq",
      "peer_u", "peer_v"]


def layout(inputs):
    a = {k: np.ascontiguousarray(np.asarray(inputs[k])) for k in IN}
    g = {k: np.asarray(v) for k, v in inputs.items()}
    cond = np.stack([g["c_ctx"], g["c"][0]], 1)
    a["cond"] = np.ascontiguousarray(cond.reshape(KC, P, 2).transpose(1, 0, 2))
    a["const"] = constants()
    a["norm_g"] = np.ascontiguousarray(np.stack([g["norm1_g"], g["norm2_g"]], 1).reshape(DEPTH, 2, KC, P).transpose(0, 3, 1, 2))
    wa0 = np.concatenate([g["rw_w0"], g["rw_a0"]], 2).reshape(DEPTH, 1024)
    parts = {"rw_kk": g["rw_kk"], "rw_ka": g["rw_ka"], "wa0": wa0, "rw_rk": g["rw_rk"].reshape(DEPTH, GW),
             "rw_gn": g["rw_gn"], "qa_g": g["mla_qa_g"], "kva_g": g["mla_kva_g"],
             "qk_g": np.concatenate([g["mla_qn_g"]] * 4 + [g["mla_kn_g"]] * 4, 1),
             "gqa_g": np.concatenate([g["gqa_qn_g"]] * 4 + [g["gqa_kn_g"]] * 2, 1),
             "conv_w": g["conv_w"].reshape(DEPTH, 768), "conv_b": g["conv_b"],
             "expert_base": NEXP * np.arange(DEPTH, dtype=np.float32)[:, None]}
    a["rows"] = np.concatenate([parts[k] for k, _ in ROW_PARTS], 1)
    s = g["state_rwkv"][0].reshape(DEPTH, 2, 2, 2, HD, HD)
    a["state"] = np.ascontiguousarray(s.transpose(0, 1, 3, 5, 2, 4))
    keys = np.stack([g["peer_k1"], g["peer_k2"]], 2).reshape(DEPTH, 2 * HEADS, NKEY, P)
    a["keys"] = np.ascontiguousarray(keys.transpose(0, 3, 1, 2))
    return a


OUT = [("y_prompt", (1, SEQ, D)), ("y_sample", (1, DEC, D)), ("state", (DEPTH, 2, 2, HD, 2, HD)),
       ("ckv", (1, DEPTH, SEQ, KV_RANK)), ("krope", (1, DEPTH, SEQ, ROPE)),
       ("gqa_k", (1, DEPTH, SEQ, 2, HD)), ("gqa_v", (1, DEPTH, SEQ, 2, HD))]


def declare(nc, arrays):
    m = Memory()
    for name, a in arrays.items():
        m.inp[name] = nc.dram_tensor("in_" + name, a.shape, F32, kind="ExternalInput").ap()
    m.scores = nc.dram_tensor("scores", (TILES - 1, P, 2 * HEADS, NKEY), F32, kind="Internal").ap()
    for name, shape in OUT:
        m.out[name] = nc.dram_tensor("out_" + name, shape, F32, kind="ExternalOutput").ap()
    return m


def kernel(**inputs):
    import concourse.bacc as bacc
    from concourse.bass_utils import run_bass_kernel_spmd

    arrays = layout(inputs)
    nc = bacc.Bacc("TRN2", target_bir_lowering=False, num_devices=1)
    m = declare(nc, arrays)
    build(nc, m)
    r = run_bass_kernel_spmd(nc, [{"in_" + k: v for k, v in arrays.items()}], core_ids=[0]).results[0]
    state = r["out_state"].transpose(0, 1, 4, 2, 5, 3).reshape(1, DEPTH, 2, 4, HD, HD)
    return tuple(state if n == "state" else r["out_" + n] for n, _ in OUT)
```
